# Optimizing a Trainium2 kernel written in Bass

```python
import jax, jax.numpy as jnp
from jax import lax
import numpy as np

D_MODEL = 1024
BATCH = 1
SEQ = 512
DEPTH = 2
DEC_BATCH = 8
DEC_SEQ = 16
PAST_LEN = 256

CHUNK = 64
D_PLE = 256
D_FF = 2816
N_EVEN = (DEPTH + 1) // 2
N_ODD = DEPTH // 2
H_A = 4
DK_A = 128
DV_A = 128
CONV_A = 4
QKV_A = H_A * (2 * DK_A + DV_A)
H_B = 4
DK_B = 128
DV_B = 128
CONV_C = 3
MIX_EVEN = H_A * DV_A + H_B * DV_B
EPS = 1e-6

kernel_name = "hybrid_gdn_mlstm_shortconv_stream_step"

def _even_split_sizes():
    return [QKV_A, H_A * DV_A, H_A, H_A,
            H_B * DK_B, H_B * DK_B, H_B * DV_B, H_B * DV_B, H_B, H_B]

def rmsnorm(x, g):
    xf = x.astype(jnp.float32)
    y = xf * lax.rsqrt(jnp.mean(xf * xf, axis=-1, keepdims=True) + EPS)
    return (y * g.astype(jnp.float32)).astype(x.dtype)

def l2norm(x):
    return x * lax.rsqrt(jnp.sum(x * x, axis=-1, keepdims=True) + EPS)

def swiglu(x, w_gu, w_d):
    a, b = jnp.split(x @ w_gu, 2, axis=-1)
    return (jax.nn.silu(a) * b) @ w_d

def causal_dwconv(hist, w):
    K = w.shape[0]
    T = hist.shape[1] - K + 1
    out = hist[:, 0:T] * w[0]
    for j in range(1, K):
        out = out + hist[:, j:j + T] * w[j]
    return out

def _to_chunks(a, cs):
    B, T, H = a.shape[:3]
    a = a.reshape((B, T // cs, cs, H) + a.shape[3:])
    perm = (1, 0, 3, 2) + tuple(range(4, a.ndim))
    return a.transpose(perm)

def _from_chunks(a):
    N, B, H, cs, d = a.shape
    return a.transpose(1, 0, 3, 2, 4).reshape(B, N * cs, H, d)

def gated_delta_chunked(q, k, v, beta, g, S0):
    T = q.shape[1]
    cs = min(CHUNK, T)
    dv = v.shape[-1]
    q, k, v = _to_chunks(q, cs), _to_chunks(k, cs), _to_chunks(v, cs)
    beta, g = _to_chunks(beta, cs), _to_chunks(g, cs)
    G = jnp.cumsum(g, axis=-1)
    idx = jnp.arange(cs)
    incl = idx[:, None] >= idx[None, :]
    strict = idx[:, None] > idx[None, :]
    diff = G[..., :, None] - G[..., None, :]
    gam = jnp.where(incl, jnp.exp(jnp.where(incl, diff, 0.0)), 0.0)
    kk = jnp.einsum('nbhtd,nbhsd->nbhts', k, k)
    A = jnp.eye(cs, dtype=jnp.float32) + jnp.where(strict, beta[..., :, None] * kk * gam, 0.0)
    eG = jnp.exp(G)
    rhs = jnp.concatenate([beta[..., None] * v, (beta * eG)[..., None] * k], axis=-1)
    sol = lax.linalg.triangular_solve(A, rhs, left_side=True, lower=True, unit_diagonal=True)
    u_v, w = sol[..., :dv], sol[..., dv:]
    p_qk = jnp.einsum('nbhtd,nbhsd->nbhts', q, k) * gam
    k_end = k * jnp.exp(G[..., -1:] - G)[..., None]
    gL = G[..., -1]

    def step(S, xs):
        q_c, u_v_c, w_c, p_c, eG_c, k_end_c, gL_c = xs
        u = u_v_c - jnp.einsum('bhtk,bhkv->bhtv', w_c, S)
        o = eG_c[..., None] * jnp.einsum('bhtk,bhkv->bhtv', q_c, S) + jnp.einsum('bhts,bhsv->bhtv', p_c, u)
        S = jnp.exp(gL_c)[..., None, None] * S + jnp.einsum('bhsk,bhsv->bhkv', k_end_c, u)
        return S, o

    S, o = lax.scan(step, S0, (q, u_v, w, p_qk, eG, k_end, gL))
    return _from_chunks(o), S

def mlstm_chunked(q, k, v, logi, logf, C0, n0, m0):
    T = q.shape[1]
    cs = min(CHUNK, T)
    q, k, v = _to_chunks(q, cs), _to_chunks(k, cs), _to_chunks(v, cs)
    logi, logf = _to_chunks(logi, cs), _to_chunks(logf, cs)
    b = jnp.cumsum(logf, axis=-1)
    idx = jnp.arange(cs)
    incl = idx[:, None] >= idx[None, :]
    dmat = jnp.where(incl, b[..., :, None] - b[..., None, :] + logi[..., None, :], -jnp.inf)
    dmax = jnp.max(dmat, axis=-1)
    s_qk = jnp.einsum('nbhtd,nbhsd->nbhts', q, k)

    def step(carry, xs):
        C, n, m = carry
        q_c, k_c, v_c, b_c, d_c, dmax_c, s_c = xs
        m_t = jnp.maximum(b_c + m[..., None], dmax_c)
        w_inter = jnp.exp(b_c + m[..., None] - m_t)
        w_intra = jnp.exp(d_c - m_t[..., None])
        a = s_c * w_intra
        num = w_inter[..., None] * jnp.einsum('bhtk,bhkv->bhtv', q_c, C) + jnp.einsum('bhts,bhsv->bhtv', a, v_c)
        den = w_inter * jnp.einsum('bhtk,bhk->bht', q_c, n) + jnp.sum(a, axis=-1)
        h = num / jnp.maximum(jnp.abs(den), jnp.exp(-m_t))[..., None]
        decay = w_inter[..., -1]
        kw = k_c * w_intra[..., -1, :][..., None]
        C = decay[..., None, None] * C + jnp.einsum('bhsk,bhsv->bhkv', kw, v_c)
        n = decay[..., None] * n + jnp.sum(kw, axis=-2)
        return (C, n, m_t[..., -1]), h

    (C, n, m), h = lax.scan(step, (C0, n0, m0), (q, k, v, b, dmat, dmax, s_qk))
    return _from_chunks(h), C, n, m

def even_mixer(xn, conv_st, S0, C0, n0, m0, w_in, gdn_conv_w, gdn_a_log, gdn_dt_bias, gdn_norm_w,
               mlstm_b_i, mlstm_b_f, mlstm_norm_w, w_out):
    B, T, _ = xn.shape
    f32 = jnp.float32
    splits = np.cumsum(_even_split_sizes())[:-1].tolist()
    qkv_a, z_a, beta_a, a_a, q_b, k_b, v_b, o_b, i_b, f_b = jnp.split(xn @ w_in, splits, axis=-1)
    hist = jnp.concatenate([conv_st.astype(qkv_a.dtype), qkv_a], axis=1)
    new_conv = hist[:, -(CONV_A - 1):]
    qkv_a = jax.nn.silu(causal_dwconv(hist, gdn_conv_w)).astype(f32)
    q_a, k_a, v_a = jnp.split(qkv_a, [H_A * DK_A, 2 * H_A * DK_A], axis=-1)
    q_a = l2norm(q_a.reshape(B, T, H_A, DK_A)) * (DK_A ** -0.5)
    k_a = l2norm(k_a.reshape(B, T, H_A, DK_A))
    v_a = v_a.reshape(B, T, H_A, DV_A)
    beta = jax.nn.sigmoid(beta_a.astype(f32))
    g = -jnp.exp(gdn_a_log.astype(f32)) * jax.nn.softplus(a_a.astype(f32) + gdn_dt_bias.astype(f32))
    o_a, S = gated_delta_chunked(q_a, k_a, v_a, beta, g, S0.astype(f32))
    o_a = o_a * lax.rsqrt(jnp.mean(o_a * o_a, axis=-1, keepdims=True) + EPS) * gdn_norm_w.astype(f32)
    o_a = (o_a * jax.nn.silu(z_a.astype(f32).reshape(B, T, H_A, DV_A))).reshape(B, T, H_A * DV_A)
    q_b = q_b.astype(f32).reshape(B, T, H_B, DK_B) * (DK_B ** -0.5)
    k_b = k_b.astype(f32).reshape(B, T, H_B, DK_B)
    v_b = v_b.astype(f32).reshape(B, T, H_B, DV_B)
    logi = i_b.astype(f32) + mlstm_b_i.astype(f32)
    logf = jax.nn.log_sigmoid(f_b.astype(f32) + mlstm_b_f.astype(f32))
    h_b, C, n, m = mlstm_chunked(q_b, k_b, v_b, logi, logf, C0.astype(f32), n0.astype(f32), m0.astype(f32))
    h_b = h_b * lax.rsqrt(jnp.mean(h_b * h_b, axis=-1, keepdims=True) + EPS)
    h_b = h_b.reshape(B, T, H_B * DV_B) * mlstm_norm_w.astype(f32) * jax.nn.sigmoid(o_b.astype(f32))
    out = jnp.concatenate([o_a, h_b], axis=-1).astype(xn.dtype) @ w_out
    dt = xn.dtype
    return out, (new_conv.astype(dt), S.astype(dt), C.astype(dt), n.astype(dt), m.astype(dt))

def odd_mixer(xn, conv_st, w_in, conv_w, w_out):
    h, bg, cg = jnp.split(xn @ w_in, 3, axis=-1)
    u = cg * h
    hist = jnp.concatenate([conv_st.astype(u.dtype), u], axis=1)
    new_st = hist[:, -(CONV_C - 1):]
    y = bg * causal_dwconv(hist, conv_w)
    return y @ w_out, new_st

def run_trunk(x, p, init_even, init_odd, norm_g, final_norm, ffn_w_gu, ffn_w_d, w_ple, w_ple_gate,
              w_in_even, gdn_conv_w, gdn_a_log, gdn_dt_bias, gdn_norm_w, mlstm_b_i, mlstm_b_f,
              mlstm_norm_w, w_out_even, w_in_odd, conv_c_w, w_out_odd):
    new_even, new_odd = [], []
    for i in range(DEPTH):
        j = i // 2
        x = x + 0.5 * swiglu(rmsnorm(x, norm_g[i, 0]), ffn_w_gu[i, 0], ffn_w_d[i, 0])
        xn = rmsnorm(x, norm_g[i, 1])
        if i % 2 == 0:
            y, st = even_mixer(xn, *init_even[j], w_in_even[j], gdn_conv_w[j], gdn_a_log[j], gdn_dt_bias[j],
                               gdn_norm_w[j], mlstm_b_i[j], mlstm_b_f[j], mlstm_norm_w[j], w_out_even[j])
            new_even.append(st)
        else:
            y, st = odd_mixer(xn, init_odd[j], w_in_odd[j], conv_c_w[j], w_out_odd[j])
            new_odd.append(st)
        x = x + y
        x = x + 0.5 * swiglu(rmsnorm(x, norm_g[i, 2]), ffn_w_gu[i, 1], ffn_w_d[i, 1])
        xg = rmsnorm(x, norm_g[i, 3])
        x = x + (p[i].astype(x.dtype) @ w_ple[i]) * jax.nn.sigmoid(xg @ w_ple_gate[i])
    y = rmsnorm(x, final_norm)
    st_even = [jnp.stack([s[c] for s in new_even]) for c in range(5)]
    st_odd = jnp.stack(new_odd)
    return y, st_even[0], st_even[1], st_even[2], st_even[3], st_even[4], st_odd

def setup_inputs(seed: int = 0) -> dict:
    key = jax.random.key(seed)
    ks = jax.random.split(key, 32)
    nrm = lambda k, s, sc: jax.random.normal(k, s, jnp.float32) * sc
    dt = jnp.exp(jax.random.uniform(ks[20], (N_EVEN, H_A), jnp.float32, np.log(1e-3), np.log(1e-1)))
    return {
        "x_prompt": nrm(ks[0], (BATCH, SEQ, D_MODEL), 1.0),
        "x_sample": nrm(ks[1], (DEC_BATCH, DEC_SEQ, D_MODEL), 1.0),
        "state_gdn_conv": nrm(ks[2], (N_EVEN, DEC_BATCH, CONV_A - 1, QKV_A), 1.0),
        "state_gdn_S": nrm(ks[3], (N_EVEN, DEC_BATCH, H_A, DK_A, DV_A), 0.1),
        "state_mlstm_C": nrm(ks[4], (N_EVEN, DEC_BATCH, H_B, DK_B, DV_B), 0.1),
        "state_mlstm_n": nrm(ks[5], (N_EVEN, DEC_BATCH, H_B, DK_B), 0.1),
        "state_mlstm_m": nrm(ks[6], (N_EVEN, DEC_BATCH, H_B), 1.0),
        "state_conv": nrm(ks[7], (N_ODD, DEC_BATCH, CONV_C - 1, D_MODEL), 1.0),
        "p_prompt": nrm(ks[8], (DEPTH, BATCH, SEQ, D_PLE), 1.0),
        "p_sample": nrm(ks[9], (DEPTH, DEC_BATCH, DEC_SEQ, D_PLE), 1.0),
        "norm_g": 1.0 + nrm(ks[10], (DEPTH, 4, D_MODEL), 0.02),
        "final_norm": 1.0 + nrm(ks[11], (D_MODEL,), 0.02),
        "ffn_w_gu": nrm(ks[12], (DEPTH, 2, D_MODEL, 2 * D_FF), D_MODEL ** -0.5),
        "ffn_w_d": nrm(ks[13], (DEPTH, 2, D_FF, D_MODEL), D_FF ** -0.5),
        "w_ple": nrm(ks[14], (DEPTH, D_PLE, D_MODEL), D_PLE ** -0.5),
        "w_ple_gate": nrm(ks[15], (DEPTH, D_MODEL, D_MODEL), D_MODEL ** -0.5),
        "w_in_even": nrm(ks[16], (N_EVEN, D_MODEL, sum(_even_split_sizes())), D_MODEL ** -0.5),
        "gdn_conv_w": nrm(ks[17], (N_EVEN, CONV_A, QKV_A), CONV_A ** -0.5),
        "gdn_a_log": jnp.log(jax.random.uniform(ks[18], (N_EVEN, H_A), jnp.float32, 1.0, 16.0)),
        "gdn_dt_bias": dt + jnp.log(-jnp.expm1(-dt)),
        "gdn_norm_w": 1.0 + nrm(ks[19], (N_EVEN, DV_A), 0.02),
        "mlstm_b_i": nrm(ks[21], (N_EVEN, H_B), 0.1),
        "mlstm_b_f": jnp.linspace(3.0, 6.0, H_B, dtype=jnp.float32)[None, :] + nrm(ks[22], (N_EVEN, H_B), 0.1),
        "mlstm_norm_w": 1.0 + nrm(ks[23], (N_EVEN, H_B * DV_B), 0.02),
        "w_out_even": nrm(ks[24], (N_EVEN, MIX_EVEN, D_MODEL), MIX_EVEN ** -0.5),
        "w_in_odd": nrm(ks[25], (N_ODD, D_MODEL, 3 * D_MODEL), D_MODEL ** -0.5),
        "conv_c_w": nrm(ks[26], (N_ODD, CONV_C, D_MODEL), CONV_C ** -0.5),
        "w_out_odd": nrm(ks[27], (N_ODD, D_MODEL, D_MODEL), D_MODEL ** -0.5),
    }

def reference(x_prompt, x_sample, state_gdn_conv, state_gdn_S, state_mlstm_C, state_mlstm_n, state_mlstm_m,
              state_conv, p_prompt, p_sample, norm_g, final_norm, ffn_w_gu, ffn_w_d, w_ple, w_ple_gate,
              w_in_even, gdn_conv_w, gdn_a_log, gdn_dt_bias, gdn_norm_w, mlstm_b_i, mlstm_b_f, mlstm_norm_w,
              w_out_even, w_in_odd, conv_c_w, w_out_odd):
    dt = x_prompt.dtype
    Bp = x_prompt.shape[0]
    zero_even = (jnp.zeros((Bp, CONV_A - 1, QKV_A), dt), jnp.zeros((Bp, H_A, DK_A, DV_A), dt),
                 jnp.zeros((Bp, H_B, DK_B, DV_B), dt), jnp.zeros((Bp, H_B, DK_B), dt), jnp.zeros((Bp, H_B), dt))
    init_even_p = [zero_even for _ in range(N_EVEN)]
    init_odd_p = [jnp.zeros((Bp, CONV_C - 1, D_MODEL), dt) for _ in range(N_ODD)]
    init_even_s = [(state_gdn_conv[j], state_gdn_S[j], state_mlstm_C[j], state_mlstm_n[j], state_mlstm_m[j])
                   for j in range(N_EVEN)]
    init_odd_s = [state_conv[j] for j in range(N_ODD)]
    weights = (norm_g, final_norm, ffn_w_gu, ffn_w_d, w_ple, w_ple_gate, w_in_even, gdn_conv_w, gdn_a_log,
               gdn_dt_bias, gdn_norm_w, mlstm_b_i, mlstm_b_f, mlstm_norm_w, w_out_even, w_in_odd, conv_c_w,
               w_out_odd)
    y_p, gconv_p, gS_p, mC_p, mn_p, mm_p, conv_p = run_trunk(x_prompt, p_prompt, init_even_p, init_odd_p, *weights)
    y_s, gconv_s, gS_s, mC_s, mn_s, mm_s, conv_s = run_trunk(x_sample, p_sample, init_even_s, init_odd_s, *weights)
    return (y_p, y_s, gconv_p, gS_p, mC_p, mn_p, mm_p, conv_p, gconv_s, gS_s, mC_s, mn_s, mm_s, conv_s)


_drawn_inputs = setup_inputs


def setup_inputs(seed=0):
    import zlib

    import numpy as np

    out = dict(_drawn_inputs(seed))
    spreads = {}
    factors = {'final_norm': 2.824, 'gdn_norm_w': 6.08, 'mlstm_b_i': 4.322, 'mlstm_norm_w': 6.622}
    for name, (base, spread) in spreads.items():
        noise = np.random.default_rng([zlib.crc32(name.encode()), seed]).standard_normal(out[name].shape)
        drawn = base * np.exp(spread * noise) if base else spread * noise
        out[name] = __import__('jax').numpy.asarray(drawn.astype(out[name].dtype))
    for name, factor in factors.items():
        out[name] = (out[name] * factor).astype(out[name].dtype)
    return out
```

```python
import concourse.bass as bass
from concourse import mybir
from contextlib import ExitStack


def stream_step(nc, ins, outs):
    fp32 = mybir.dt.float32
    fp32r = mybir.dt.float32r
    ALU = mybir.AluOpType
    ACT = mybir.ActivationFunctionType

    P = 128
    BATCH, SEQ, D = ins["x_prompt"].shape
    DECB, DECT, _ = ins["x_sample"].shape
    DEPTH = ins["norm_g"].shape[0]
    DFF = ins["ffn_w_d"].shape[2]
    DPLE = ins["w_ple"].shape[1]
    HA, DK = ins["state_gdn_S"].shape[2:4]
    HB = ins["state_mlstm_C"].shape[2]
    assert BATCH == 1 and DECB * DECT == P and SEQ % P == 0 and HA == HB == 4 and DK == P
    T = SEQ + P
    HT = T // 2
    NTILE = T // P
    KD = D // P
    NF = DFF // P
    PARTS = [8, 8, NF - 16]
    KP = DPLE // P
    KA, KC = ins["gdn_conv_w"].shape[1], ins["conv_c_w"].shape[1]
    EPS = 1e-6
    NA = 3 * HA
    LVL = 7
    LVLS = 4
    MW = P + 1

    ctx = ExitStack()
    with ctx:
        base = nc.sbuf_base
        arena = ctx.enter_context(nc.sbuf_tensor("arena", [P, (229344 - base - 64) // 4], fp32))
        place = [-(-base // 32) * 32]

        def at(name, shape, offset, dt=fp32):
            return nc.alloc_sbuf_tensor_at(name, shape, dt, offset=offset)

        def sb(name, shape, dt=fp32):
            size = 4
            for s in shape[1:]:
                size *= s
            place[0] = -(-place[0] // 32) * 32
            t = at(name, shape, place[0], dt)
            place[0] += size
            assert place[0] <= 229344, (name, place[0])
            return t

        def sem(name):
            return ctx.enter_context(nc.semaphore(name))

        x = sb("x", [P, KD, T])
        xh = sb("xh", [P, KD, T], fp32r)
        xl = sb("xl", [P, KD, T], fp32r)
        raw = sb("raw", [P, 4, KD, P])
        whi = sb("whi", [P, 2, KD, P], fp32r)
        wlo = sb("wlo", [P, 2, KD, P], fp32r)
        PIECE = 4 * T
        B0 = -(-place[0] // 32) * 32
        qkv = sb("qkv", [P, 2 * NA, T])
        hh = at("hh", [P, 8, T], B0, fp32r)
        hl = at("hl", [P, 8, T], B0 + 8 * PIECE, fp32r)
        sig = at("sig", [P, 8, T], B0 + 16 * PIECE)
        xstage = at("xstage", [P, NTILE, D], B0)
        vstage = at("vstage", [P, 2, P], B0 + 8 * PIECE)
        castage = at("castage", [P, NA * P], B0 + 9 * PIECE)
        ccstage = at("ccstage", [P, D], B0 + 12 * PIECE)
        ystage = at("ystage", [P, NTILE, D], B0 + 2 * PIECE)
        pstage = at("pstage", [P, NTILE, DPLE], B0 + 2 * PIECE)
        st = sb("st", [P, HB, DECB, MW])
        sg = at("sg", [P, HA, DECB, P], place[0] - 4 * HB * DECB * MW)
        S0 = place[0] - 4 * HB * DECB * MW
        castout = at("castout", [P, NA * P], S0)
        ccout = at("ccout", [P, D], S0)
        pS = sb("pS", [P, HA, P])
        pC = sb("pC", [P, HB, MW])
        r = sb("r", [P, T])
        sumsq = sb("sumsq", [P, T])
        T0 = -(-place[0] // 32) * 32
        W9 = sb("W9", [P, 9, HA * MW])
        gt = at("gt", [P, T], T0)
        stt = at("stt", [P, T], T0 + PIECE)
        ut = at("ut", [P, T], T0 + 2 * PIECE)
        hf = at("hf", [P, T], T0 + 3 * PIECE)
        sq = at("sq", [P, T], T0 + 4 * PIECE)
        HISTA = SEQ + KA - 1 + DECB * (DECT + KA - 1)
        HISTC = SEQ + KC - 1 + DECB * (DECT + KC - 1)
        HISTB = -(-4 * HISTA // 32) * 32
        hist = at("hist", [P, HISTA], T0 + 5 * PIECE)
        ct = at("ct", [P, HISTA], T0 + 5 * PIECE + HISTB)
        assert 5 * PIECE + 2 * HISTB <= 9 * HA * MW * 4
        R1 = sb("R1", [P, T])
        nout = at("nout", [P, (HB + 1) * P], place[0] - PIECE)
        R0 = place[0]
        R2 = sb("R2", [P, T])
        CA, CC = KA - 1, KC - 1
        castate = at("castate", [P, NA, DECB * CA], R0)
        cacoll = at("cacoll", [P, NA, CA + DECB * CA], R0 + 4 * NA * DECB * CA)
        ccstate = sb("ccstate", [P, KD, DECB * CC])
        cccoll = at("cccoll", [P, KD, CC + DECB * CC], R0)
        ident = sb("ident", [P, P])
        level = sb("level", [P, LVL, P])
        incl = sb("incl", [P, 2, P])
        bmask = sb("bmask", [P, DECB])
        NV1 = DEPTH * 4 * KD + KD
        NV2 = KA * NA + KC * KD + HB + 1
        vec1 = sb("vec1", [P, NV1])
        vec2 = sb("vec2", [P, NV2])
        one = sb("one", [P, 1])
        eps = sb("eps", [P, 1])
        wg = sb("wg", [P, KD, 16])
        gcol = sb("gcol", [P, 8])
        small = sb("small", [4, 8])
        m0 = sb("m0", [4, DECB])
        mfin = sb("mfin", [4, 1 + DECB])
        NSEG = SEQ // P + DECB
        minr = sb("minr", [4, NSEG])
        cend = sb("cend", [4, NSEG])

        ps = [ctx.enter_context(nc.psum_tensor(f"ps{i}", [P, 2, 512], fp32)) for i in range(4)]

        def halves(tok):
            return tok.rearrange("p (a b) -> p a b", a=2)

        def bank(i):
            return ps[i // 2][:, i % 2, :]

        def heads(i):
            return bank(i).rearrange("p (h t) -> p h t", h=HA)

        def uexp(width):
            a = 6 if width == P else 7
            return W9[:, a:a + 2, :].rearrange("p a b -> p (a b)")[:, 0:DECB * width].rearrange("p (b c) -> p b c", b=DECB)

        def W(i):
            return W9[:, i, 0:HA * P].rearrange("p (h t) -> p h t", h=HA)

        raw_loaded = [sem(f"raw_loaded{i}") for i in range(4)]
        hi_ready = sem("hi_ready")
        lo_ready = sem("lo_ready")
        job_done = sem("job_done")
        slot_free = [sem(f"slot_free{i}") for i in range(4)]
        xg_hi = sem("xg_hi")
        xg_ready = sem("xg_ready")
        x_new = sem("x_new")
        sq_ready = sem("sq_ready")
        root_ready = sem("root_ready")
        gate_in = sem("gate_in")
        act_out = sem("act_out")
        h_ready = sem("h_ready")
        dve_own = sem("dve_own")
        act_own = sem("act_own")
        pool_own = sem("pool_own")
        consts_ready = sem("consts_ready")
        pool_consts = sem("pool_consts")
        in_loaded = [sem(f"in_loaded{i}") for i in range(6)]
        out_stored = sem("out_stored")
        p_loaded = sem("p_loaded")
        p_hi = sem("p_hi")
        stage_free = sem("stage_free")
        hn_sq = sem("hn_sq")
        hn_root = sem("hn_root")
        conv_in = sem("conv_in")
        conv_out = sem("conv_out")
        row_in = sem("row_in")
        row_act = sem("row_act")
        rows_ready = sem("rows_ready")
        coll_ready = sem("coll_ready")
        coll_out = sem("coll_out")
        states_loaded = sem("states_loaded")
        states_stored = sem("states_stored")
        states_done = sem("states_done")
        hn_used = sem("hn_used")
        m_final = sem("m_final")
        y_in = sem("y_in")
        y_out = sem("y_out")
        core = {k: sem("core_" + k) for k in
                "bcast prod expin gam eg np kend c0 tr ktok x0 ctl m1 m1c d xr ks rT rt rtok u utok o up state uexp sup vt vtok den".split()}

        blocks = []
        jobs = []
        block_job = []

        def job(kind, n=None):
            jobs.append((kind, n))
            return len(jobs) - 1

        def blk(src, kt, kind):
            blocks.append((src, kt))
            block_job.append(job(kind, len(blocks) - 1))
            return len(blocks) - 1

        stages = []
        prod = 0

        def load_stage():
            nonlocal prod
            s = dict(kind="load", vec=job("vec"), cs=job("cs"), x=[job("xT") for _ in range(KD)], prod=0)
            stages.append(s)
            prod = 1

        def ffn_stage(i, f, first_pair):
            nonlocal prod
            gu, dn = ins["ffn_w_gu"][i, f], ins["ffn_w_d"][i, f]
            j0 = 0
            for part, cnt in enumerate(PARTS):
                s = dict(kind="gu", pair0=first_pair + j0, count=cnt, norm=None, prod=prod - 1, first=part == 0,
                         n0=len(blocks), src=gu, col0=j0)
                for q in range(cnt):
                    blk((gu, (j0 + q) * P), KD, "gate")
                    if part == 0 and q == 0:
                        s["norm"] = job("norm")
                    blk((gu, DFF + (j0 + q) * P), KD, "up")
                stages.append(s)
                last = part == len(PARTS) - 1
                s = dict(kind="down", n0=len(blocks), kt=cnt, last=last, scale=0.5, hbase=first_pair + j0,
                         prod=prod if last else None, g=(i * 4 + (1 if f == 0 else 3)) * KD)
                for o in range(KD):
                    blk((dn, o * P, j0 * P), cnt, "down")
                stages.append(s)
                j0 += cnt
            prod += 1

        pairs = 0
        load_stage()
        ffn_stage(0, 0, pairs)
        pairs += NF
        w_in = ins["w_in_even"][0]
        wcol = [0, HA * P, 2 * HA * P, 3 * HA * P]
        gcol0 = 4 * HA * P
        bcol = [gcol0 + 2 * HA + q * HB * P for q in range(4)]
        icol = bcol[3] + HB * P
        s = dict(kind="even_in", n0=len(blocks), prod=prod - 1, pos=[])
        for q in range(3):
            for h in range(HA):
                blk((w_in, wcol[q] + h * P), KD, "conv")
                if q == 0 and h == 0:
                    s["norm"] = job("norm")
                s["pos"].append([0, 4, 16][q] + h)
        s["coll"] = [job("coll"), job("coll")]
        s["gates"] = blk((None, 0), KD, "gates")
        for q in range(3):
            for h in range(HB):
                blk((w_in, bcol[q] + h * P), KD, "plain")
                s["pos"].append([8, 12, 20][q] + h)
        s["l2"] = [job("hn") for _ in range(2 * HA)]
        stages.append(s)
        stages.append(dict(kind="core"))
        s = dict(kind="even_z", onorm=[job("hn") for _ in range(HA + HB)], n0=len(blocks), pair0=pairs)
        for h in range(HA):
            blk((w_in, wcol[3] + h * P), KD, "z")
        for h in range(HB):
            blk((w_in, bcol[3] + h * P), KD, "z")
        stages.append(s)
        stages.append(dict(kind="down", n0=len(blocks), kt=KD, last=True, scale=1.0, hbase=pairs, prod=prod, g=2 * KD))
        for o in range(KD):
            blk((ins["w_out_even"][0], o * P, 0), KD, "down")
        prod += 1
        pairs += HA + HB
        ffn_stage(0, 1, pairs)
        pairs += NF

        def ple_stage(i):
            nonlocal prod, pairs
            s = dict(kind="ple", i=i, n0=len(blocks), prod=prod - 1, hbase=pairs)
            for o in range(KD):
                blk((ins["w_ple_gate"][i], o * P), KD, "pgate")
                if o == 0:
                    s["norm"] = job("norm")
                    s["pT"] = [job("pT") for _ in range(KP)]
            for o in range(KD):
                blk((ins["w_ple"][i], o * P), KP, "pemb")
            s["next"] = prod
            s["g"] = (i + 1) * 4 * KD
            stages.append(s)
            prod += 1
            pairs += KP

        ple_stage(0)
        ffn_stage(1, 0, pairs)
        pairs += NF
        w_odd = ins["w_in_odd"][0]
        s = dict(kind="odd_in", n0=len(blocks), prod=prod - 1, hbase=pairs)
        for q in range(KD):
            blk((w_odd, q * P), KD, "gate")
            if q == 0:
                s["norm"] = job("norm")
            blk((w_odd, 2 * D + q * P), KD, "up")
        s["coll"] = [job("coll")]
        for q in range(KD):
            blk((w_odd, D + q * P), KD, "bg")
        stages.append(s)
        stages.append(dict(kind="down", n0=len(blocks), kt=KD, last=True, scale=1.0, hbase=pairs, prod=prod, g=6 * KD))
        for o in range(KD):
            blk((ins["w_out_odd"][0], o * P, 0), KD, "down")
        prod += 1
        pairs += KD
        ffn_stage(1, 1, pairs)
        pairs += NF
        ple_stage(1)
        s = dict(kind="final", prod=prod - 1)
        s["norm"] = job("norm")
        s["y"] = [job("yT") for _ in range(KD)]
        stages.append(s)
        NB = len(blocks)

        hn0 = 0
        for s in stages:
            if s["kind"] == "even_in":
                s["hn0"] = hn0
                hn0 += 2 * HA
            if s["kind"] == "even_z":
                s["hn0"] = hn0
        act0 = 0
        for s in stages:
            s["act0"] = act0
            if s["kind"] == "gu":
                act0 += s["count"]
            elif s["kind"] == "even_z":
                act0 += HA + HB
            elif s["kind"] == "ple":
                act0 += KD

        core_jobs = next(s["onorm"][0] for s in stages if s["kind"] == "even_z")

        class Tally:

            def __init__(self, engine):
                self.engine, self.counts, self.turn, self.per = engine, {}, None, {}

            def __call__(self, _, s):
                self.counts[s.name] = self.counts.get(s.name, 0) + 1
                v = self.counts[s.name]
                self.engine.wait_ge(s, v if self.turn is None else self.turn * self.per[s.name] + v)

            def enter(self, turn, per):
                self.turn, self.per = turn, {k.name: v for k, v in per.items()}
                self.before = dict(self.counts)

            def leave(self, trips):
                for k, v in self.counts.items():
                    body = v - self.before.get(k, 0)
                    assert body == self.per.get(k, 0), (k, body)
                    self.counts[k] = self.before.get(k, 0) + body * trips
                self.turn = None

        def turns(value, turn, per):
            return value if turn is None else turn * per + value

        block = ctx.enter_context(nc.Block())

        @block.sync
        def _(sp):
            xs = xstage[:, :, :]
            sp.dma_start(xs[:, 0:NTILE - 1, :], ins["x_prompt"][0].rearrange("(t p) d -> p t d", p=P)).then_inc(in_loaded[0], 16)
            sp.dma_start(xs[:, NTILE - 1, :], ins["x_sample"].rearrange("b t d -> (b t) d")).then_inc(in_loaded[0], 16)
            sp.dma_start(vstage[0:DEPTH * 4 * KD, 0, :], ins["norm_g"].rearrange("i f (k p) -> (i f k) p", p=P)).then_inc(in_loaded[1], 16)
            sp.dma_start(vstage[DEPTH * 4 * KD:NV1, 0, :], ins["final_norm"].rearrange("(k p) -> k p", p=P)).then_inc(in_loaded[1], 16)
            a, b = KA * NA, KA * NA + KC * KD
            sp.dma_start(vstage[0:a, 1, :], ins["gdn_conv_w"][0].rearrange("j (k p) -> (j k) p", p=P)).then_inc(in_loaded[1], 16)
            sp.dma_start(vstage[a:b, 1, :], ins["conv_c_w"][0].rearrange("j (k p) -> (j k) p", p=P)).then_inc(in_loaded[1], 16)
            sp.dma_start(vstage[b:b + HB, 1, :], ins["mlstm_norm_w"][0].rearrange("(k p) -> k p", p=P)).then_inc(in_loaded[1], 16)
            sp.dma_start(vstage[b + HB:b + HB + 1, 1, :], ins["gdn_norm_w"]).then_inc(in_loaded[1], 16)
            sp.dma_start(castage[0:DECB * CA, :], ins["state_gdn_conv"][0].rearrange("b t c -> (b t) c")).then_inc(in_loaded[2], 16)
            sp.dma_start(ccstage[0:DECB * CC, :], ins["state_conv"][0].rearrange("b t c -> (b t) c")).then_inc(in_loaded[2], 16)
            with nc.allow_non_contiguous_dma(reason="a few words of gate parameters"):
                for q, name in enumerate(["gdn_a_log", "gdn_dt_bias", "mlstm_b_i", "mlstm_b_f"]):
                    sp.dma_start(small[0:4, q:q + 1], ins[name].rearrange("a h -> h a")).then_inc(in_loaded[3], 16)
                sp.dma_start(m0[0:4, :], ins["state_mlstm_m"][0].rearrange("b h -> h b")).then_inc(in_loaded[3], 16)
                wv = w_in.rearrange("(k p) c -> p k c", p=P)
                sp.dma_start(wg[:, :, 0:8], wv[:, :, gcol0:gcol0 + 8]).then_inc(in_loaded[4], 16)
                sp.dma_start(wg[:, :, 8:16], wv[:, :, icol:icol + 8]).then_inc(in_loaded[4], 16)

            def load(n, source, off=0):
                slot = n % 4
                if n >= 4:
                    sp.wait_ge(lo_ready, n - 3 + off)
                sp.dma_start(raw[:, slot, 0:source.shape[1], :], source).then_inc(raw_loaded[slot], 16)

            def source(n):
                src, kt = blocks[n]
                if len(src) == 2:
                    return src[0].rearrange("(k p) c -> p k c", p=P)[:, :, src[1]:src[1] + P]
                return src[0][src[2]:src[2] + kt * P, src[1]:src[1] + P].rearrange("(k p) c -> p k c", p=P)

            n = 0
            for s in stages:
                if s["kind"] == "gu":
                    gv = s["src"].rearrange("(k p) c -> p k c", p=P)
                    lead = 4
                    for n in range(s["n0"], s["n0"] + lead):
                        load(n, source(n))
                    trips = (2 * s["count"] - lead) // 4
                    with sp.Fori(0, trips) as i:
                        for u in range(4):
                            n = s["n0"] + lead + u
                            c = (s["col0"] + (lead + u) // 2) * P + (u % 2) * DFF
                            load(n, gv[:, :, bass.ds(i * (2 * P) + c, P)], i * 4)
                elif s["kind"] in ("down", "ple", "even_z", "odd_in", "even_in"):
                    count = {"down": KD, "ple": 2 * KD, "even_z": HA + HB, "odd_in": 3 * KD, "even_in": 2 * NA + 1}[s["kind"]]
                    if s["kind"] == "ple":
                        sp.wait_ge(job_done, block_job[s["n0"] - 1] + 1)
                        i = s["i"]
                        sp.dma_start(pstage[:, 0:NTILE - 1, :], ins["p_prompt"][i, 0].rearrange("(t p) d -> p t d", p=P)).then_inc(p_loaded, 16)
                        sp.dma_start(pstage[:, NTILE - 1, :], ins["p_sample"][i].rearrange("b t d -> (b t) d")).then_inc(p_loaded, 16)
                    for n in range(s["n0"] + (4 if s["kind"] == "even_z" else 0), s["n0"] + count):
                        if blocks[n][0][0] is None:
                            sp.wait_ge(lo_ready, n - 3)
                            sp.sem_inc(raw_loaded[n % 4], 16)
                        else:
                            load(n, source(n))
                    if s["kind"] == "even_in":
                        sp.wait_ge(coll_out, 1)
                        sp.dma_start(outs["gdn_conv_p"][0, 0], castout[0:CA, :]).then_inc(out_stored, 16)
                        sp.dma_start(outs["gdn_conv_s"][0].rearrange("b t c -> (b t) c"), castout[CA:CA + DECB * CA, :]).then_inc(out_stored, 16)
                    if s["kind"] == "odd_in":
                        sp.wait_ge(coll_out, 2)
                        sp.dma_start(outs["conv_p"][0, 0], ccout[0:CC, :]).then_inc(out_stored, 16)
                        sp.dma_start(outs["conv_s"][0].rearrange("b t c -> (b t) c"), ccout[CC:CC + DECB * CC, :]).then_inc(out_stored, 16)
                elif s["kind"] == "core":
                    z0 = next(z["n0"] for z in stages if z["kind"] == "even_z")
                    for n in range(z0, z0 + 4):
                        load(n, source(n))
                    sp.wait_ge(m_final, 1)
                    with nc.allow_non_contiguous_dma(reason="a few words"):
                        sp.dma_start(outs["mlstm_m_p"][0].rearrange("b h -> h b"), mfin[:, 0:1]).then_inc(out_stored, 16)
                        sp.dma_start(outs["mlstm_m_s"][0].rearrange("b h -> h b"), mfin[:, 1:]).then_inc(out_stored, 16)
                    sp.wait_ge(out_stored, 4 * 16)
                    for h in range(HA):
                        sp.dma_start(sg[:, h], ins["state_gdn_S"][0, :, h].rearrange("b k v -> k b v")).then_inc(states_loaded, 16)
                    sp.wait_ge(core["up"], NTILE)
                    sp.dma_start(outs["gdn_S_p"][0, 0].rearrange("h k v -> k h v"), pS[:]).then_inc(states_stored, 16)
                    for h in range(HA):
                        sp.dma_start(outs["gdn_S_s"][0, :, h].rearrange("b k v -> k b v"), sg[:, h]).then_inc(states_stored, 16)
                    sp.wait_ge(states_stored, 16 * (1 + HA))
                    for h in range(HB):
                        sp.dma_start(st[:, h, :, 0:P], ins["state_mlstm_C"][0, :, h].rearrange("b k v -> k b v")).then_inc(states_loaded, 16)
                        with nc.allow_non_contiguous_dma(reason="normalisers as a column"):
                            sp.dma_start(st[:, h, :, P:MW], ins["state_mlstm_n"][0, :, h].rearrange("b (k o) -> k b o", o=1)).then_inc(states_loaded, 16)
                    sp.wait_ge(core["up"], 2 * NTILE)
                    sp.dma_start(outs["mlstm_C_p"][0, 0].rearrange("h k v -> k h v"), pC[:, :, 0:P]).then_inc(out_stored, 16)
                    for h in range(HB):
                        sp.dma_start(outs["mlstm_C_s"][0, :, h].rearrange("b k v -> k b v"), st[:, h, :, 0:P]).then_inc(out_stored, 16)
                    sp.wait_ge(states_done, 1)
                    sp.dma_start(outs["mlstm_n_p"][0, 0], nout[0:HB, 0:P]).then_inc(out_stored, 16)
                    sp.dma_start(outs["mlstm_n_s"][0].rearrange("b h k -> b (h k)"), nout[0:DECB, P:]).then_inc(out_stored, 16)
            sp.wait_ge(y_out, KD)
            sp.dma_start(outs["y_p"][0].rearrange("(t p) d -> p t d", p=P), ystage[:, 0:NTILE - 1, :]).then_inc(out_stored, 16)
            sp.dma_start(outs["y_s"].rearrange("b t d -> (b t) d"), ystage[:, NTILE - 1, :]).then_inc(out_stored, 16)
            sp.wait_ge(out_stored, (2 + 2 + 2 + 1 + HB + 2 + 2) * 16)

        @block.gpsimd
        def _(pool):
            own = [0]

            def step(ins_):
                own[0] += 1
                ins_.then_inc(pool_own, 1)
                pool.wait_ge(pool_own, own[0])

            def select(out, pattern, base_, mult, op):
                step(pool.affine_select(out=out, in_=out, compare_op=op, fill=0.0, base=base_, pattern=pattern,
                                        channel_multiplier=mult))

            step(pool.memset(ident[:], 0.0))
            step(pool.affine_select(out=ident[:], in_=ident[:], compare_op=ALU.not_equal, fill=1.0, base=0,
                                    pattern=[[-1, P]], channel_multiplier=1))
            step(pool.memset(one[:], 1.0))
            step(pool.memset(R1[:], 0.0))
            step(pool.memset(incl[:], 1.0))
            for g in range(2):
                select(incl[:, g, :], [[1, P]], 0, -1, ALU.is_ge)
            select(incl[:, 1, :], [[-DECT, DECB], [0, DECT]], 0, 1, ALU.is_ge)
            step(pool.memset(bmask[:], 1.0))
            select(bmask[:], [[-DECT, DECB]], 0, 1, ALU.is_ge)
            select(bmask[:], [[DECT, DECB]], DECT - 1, -1, ALU.is_ge)
            step(pool.memset(level[:], 1.0))
            for l in range(LVL):
                w = 1 << l
                v = level[:, l, :]
                if P // (2 * w) > 1:
                    select(v, [[-2 * w, P // (2 * w)], [0, 2 * w]], 0, 1, ALU.is_ge)
                select(v, [[2 * w, P // (2 * w)], [0, 2 * w]], w - 1, -1, ALU.is_ge)
                step(pool.memset(v.rearrange("p (b w) -> p b w", w=2 * w)[:, :, 0:w], 0.0))
            pool.sem_inc(pool_consts, 1)

            def low(n, kt, off=0, src=None, dst_hi=None, dst=None):
                slot, ws = n % 4, n % 2
                pool.wait_ge(hi_ready, n + 1 + off)
                pool.tensor_tensor(wlo[:, ws, 0:kt, :], raw[:, slot, 0:kt, :], whi[:, ws, 0:kt, :].bitcast(fp32),
                                   ALU.subtract).then_inc(lo_ready, 1)

            n = 0
            while n < NB:
                kt = blocks[n][1]
                if blocks[n][0][0] is None:
                    pool.wait_ge(hi_ready, n + 1)
                    quad = wlo[:, n % 2].rearrange("p k (q c) -> p k q c", q=4)[:, :, :, 0:4]
                    quadh = whi[:, n % 2].rearrange("p k (q c) -> p k q c", q=4)[:, :, :, 0:4].bitcast(fp32)
                    pool.tensor_tensor(quad, wg[:].rearrange("p k (q c) -> p k q c", q=4), quadh,
                                       ALU.subtract).then_inc(lo_ready, 1)
                    n += 1
                    continue
                run = 0
                while n + run < NB and blocks[n + run][1] == kt and blocks[n + run][0][0] is not None:
                    run += 1
                if run >= 8:
                    with pool.Fori(0, run // 4) as i:
                        for u in range(4):
                            low(n + u, kt, i * 4)
                    n += run // 4 * 4
                    run %= 4
                for u in range(run):
                    low(n, kt)
                    n += 1

        @block.tensor
        def _(pe):
            def wait_slot(j, turn=None):
                if j >= 4:
                    pe.wait_ge(slot_free[j % 4], turns(j // 4, turn, 1))

            def mm(n, hi, lo, turn=None, first=None):
                j, kt, ws = block_job[n], blocks[n][1], n % 2
                wait_slot(j, turn)
                pe.wait_ge(lo_ready, turns(n + 1, turn, 4))
                for k in range(kt):
                    if first is not None:
                        pe.wait_ge(first[0], first[1] + k + 1)
                    for c in range(2):
                        cs = slice(c * HT, (c + 1) * HT)
                        pe.matmul(ps[j % 4][:, c, 0:HT], whi[:, ws, k], hi[:, k, cs], start=(k == 0), stop=False)
                        pe.matmul(ps[j % 4][:, c, 0:HT], whi[:, ws, k], lo[:, k, cs], start=False, stop=False)
                    for c in range(2):
                        cs = slice(c * HT, (c + 1) * HT)
                        last = pe.matmul(ps[j % 4][:, c, 0:HT], wlo[:, ws, k], hi[:, k, cs], start=False, stop=(k == kt - 1))
                last.then_inc(job_done, 1)

            def sum_job(j, src):
                wait_slot(j)
                for c in range(2):
                    last = pe.matmul(ps[j % 4][:, c, 0:HT], one[:].to_broadcast([P, P]), src[:, c * HT:(c + 1) * HT],
                                     start=True, stop=True)
                last.then_inc(job_done, 1)

            def norm_job(s):
                pe.wait_ge(xg_ready, 8 * s["prod"] + 8)
                sum_job(s["norm"], sumsq)

            def tposes(j, pieces):
                wait_slot(j)
                for c, col, src in pieces:
                    rows, cols = src.shape
                    last = pe.transpose(ps[j % 4][0:cols, c, col:col + rows], src, ident[0:rows, 0:rows])
                last.then_inc(job_done, 1)

            def tile(t):
                return slice(t * P, (t + 1) * P)

            def spread(b, rows, first_row, t):
                for h in range(HA):
                    c = first_row + h
                    pe.matmul(bank(b)[:, h * P:(h + 1) * P], ident[:, c:c + 1].to_broadcast([P, P]), rows[:, tile(t)],
                              start=True, stop=True)

            def per_head(b, lhsT, rhs, N=P):
                for h in range(HA):
                    last = pe.matmul(bank(b)[:, h * P:(h + 1) * P], lhsT(h), rhs(h), start=True, stop=True)
                return last

            def delta_tile(t):
                sample = t == NTILE - 1
                L = LVLS if sample else LVL
                q, k = qkv[:, 0:HA, tile(t)], qkv[:, HA:2 * HA, tile(t)]
                li = (LVL - 1) * t
                if t:
                    pe.wait_ge(core["up"], t)
                spread(0, R1, 0, t)
                spread(1, R1, 32, t)
                spread(2, R1, 64, t)
                pe.transpose(bank(3)[:, 0:P], R1[:, tile(t)], ident[:]).then_inc(core["bcast"], 1)
                pe.wait_ge(core["prod"], t + 1)
                per_head(4, lambda h: k[:, h], lambda h: W(0)[:, h])
                per_head(5, lambda h: k[:, h], lambda h: q[:, h]).then_inc(core["np"], 1)
                pe.wait_ge(core["kend"], t + 1)
                for h in range(HA):
                    pe.transpose(bank(7)[:, h * P:(h + 1) * P], W(3)[:, h], ident[:])
                pe.wait_ge(core["c0"], t + 1)
                for h in range(HA):
                    last = pe.transpose(bank(6)[:, h * P:(h + 1) * P], W(1)[:, h], ident[:])
                last.then_inc(core["tr"], 1)
                for l in range(1, L):
                    pe.wait_ge(core["ctl"], li + l)
                    if l == 1:
                        pe.wait_ge(core["x0"], t + 1)
                    else:
                        pe.wait_ge(core["xr"], li + l - 1)
                    per_head(0, lambda h: W(1)[:, h], lambda h: W(6)[:, h]).then_inc(core["m1"], 1)
                    pe.wait_ge(core["m1c"], li + l)
                    last = per_head(1, lambda h: W(8)[:, h], lambda h: W(7)[:, h])
                    if l < L - 1:
                        last = per_head(2, lambda h: W(7)[:, h], lambda h: W(8)[:, h])
                    last.then_inc(core["d"], 1)
                pe.wait_ge(core["xr"], li + L - 1)
                if sample:
                    pe.wait_ge(states_loaded, 16 * HA)
                NBK = DECB if sample else 1
                w = P // NBK

                def state(h, b):
                    return sg[:, h, b, :] if sample else pS[:, h, :]

                for h in range(HA):
                    for b in range(NBK):
                        last = pe.matmul(bank(3)[:, h * P + b * w:h * P + (b + 1) * w], state(h, b), W(0)[:, h, b * w:(b + 1) * w],
                                         start=True, stop=True)
                last.then_inc(core["ks"], 1)
                pe.wait_ge(core["rT"], t + 1)
                for h in range(HA):
                    last = pe.transpose(bank(4)[:, h * P:(h + 1) * P], W(6)[:, h], ident[:])
                last.then_inc(core["rt"], 1)
                pe.wait_ge(core["rtok"], t + 1)
                per_head(5, lambda h: W(7)[:, h], lambda h: W(8)[:, h]).then_inc(core["u"], 1)
                pe.wait_ge(core["utok"], t + 1)
                for h in range(HA):
                    pe.matmul(bank(6)[:, h * P:(h + 1) * P], W(1)[:, h], W(5)[:, h], start=True, stop=False)
                    for b in range(NBK):
                        last = pe.matmul(bank(6)[:, h * P + b * w:h * P + (b + 1) * w], state(h, b), q[:, h, b * w:(b + 1) * w],
                                         start=False, stop=(b == NBK - 1))
                if sample:
                    last.then_inc(core["o"], 1)
                    for h in range(HA):
                        pe.wait_ge(core["uexp"], h + 1)
                        for c in range(2):
                            last = pe.matmul(ps[h % 2][:, c, :], W(3)[:, h], uexp(P)[:, c * 4:(c + 1) * 4, :], start=True, stop=True)
                        last.then_inc(core["sup"], 1)
                else:
                    per_head(7, lambda h: W(3)[:, h], lambda h: W(1)[:, h]).then_inc(core["o"], 1)

            def mlstm_tile(t):
                sample = t == NTILE - 1
                g = NTILE + t
                q, k, v = (qkv[:, a:a + HB, tile(t)] for a in (8, 12, 20))
                pe.wait_ge(core["up"], g)
                spread(0, R2, 0, t)
                spread(1, R2, 32, t)
                spread(2, R2, 64, t)
                spread(3, R2, 96, t)
                pe.transpose(bank(4)[:, 0:P], R1[:, tile(t)], ident[:])
                per_head(5, lambda h: k[:, h], lambda h: q[:, h])
                for h in range(HB):
                    last = pe.transpose(bank(6)[:, h * P:(h + 1) * P], v[:, h], ident[:])
                last.then_inc(core["bcast"], 1)
                pe.wait_ge(core["kend"], g + 1)
                for h in range(HB):
                    last = pe.transpose(bank(0)[:, h * P:(h + 1) * P], W(4)[:, h], ident[:])
                last.then_inc(core["tr"], 1)
                if sample:
                    pe.wait_ge(states_loaded, 16 * (HA + 2 * HB))
                NBK = DECB if sample else 1
                w = P // NBK

                def state(h, b):
                    return st[:, h, b, :] if sample else pC[:, h, :]

                pe.wait_ge(core["vt"], t + 1)
                for h in range(HB):
                    hs = h * P
                    pe.matmul(bank(1)[:, hs:hs + P], W9[:, 5, h * MW:h * MW + P], W(3)[:, h], start=True, stop=False)
                    for b in range(NBK):
                        pe.matmul(bank(1)[:, hs + b * w:hs + (b + 1) * w], state(h, b)[:, 0:P], q[:, h, b * w:(b + 1) * w],
                                  start=False, stop=(b == NBK - 1))
                    pe.matmul(bank(2)[:, hs:hs + P], one[:].to_broadcast([P, P]), W(3)[:, h], start=True, stop=False)
                    for b in range(NBK):
                        last = pe.matmul(bank(2)[:, hs + b * w:hs + (b + 1) * w], state(h, b)[:, P:MW].to_broadcast([P, P]),
                                         q[:, h, b * w:(b + 1) * w], start=False, stop=(b == NBK - 1))
                last.then_inc(core["np"], 1)
                pe.wait_ge(core["ktok"], t + 1)
                if sample:
                    for h in range(HB):
                        pe.wait_ge(core["uexp"], HA + h + 1)
                        for c, (a, b) in enumerate([(0, 3), (3, 6), (6, 8)]):
                            last = pe.matmul(bank(3 + c)[:, 0:(b - a) * MW], W(6)[:, h], uexp(MW)[:, a:b, :], start=True, stop=True)
                        last.then_inc(core["sup"], 1)
                else:
                    for h in range(HB):
                        last = pe.matmul(bank(3 + h // 2)[:, h % 2 * MW:(h % 2 + 1) * MW], W(6)[:, h],
                                         W9[:, 5, h * MW:(h + 1) * MW], start=True, stop=True)
                    last.then_inc(core["o"], 1)

            pe.wait_ge(pool_consts, 1)
            for s in stages:
                kind = s["kind"]
                if kind == "load":
                    pe.wait_ge(in_loaded[1], 6 * 16)
                    tposes(s["vec"], [(0, 0, vstage[0:NV1, 0, :]), (1, 0, vstage[0:NV2, 1, :])])
                    pe.wait_ge(in_loaded[2], 2 * 16)
                    tposes(s["cs"], [(0, b * DECB * CA, castage[0:DECB * CA, b * P:(b + 1) * P]) for b in range(NA)] +
                           [(1, b * DECB * CC, ccstage[0:DECB * CC, b * P:(b + 1) * P]) for b in range(KD)])
                    pe.wait_ge(in_loaded[0], 2 * 16)
                    for q, j in enumerate(s["x"]):
                        tposes(j, [(t // 4, t % 4 * P, xstage[:, t, q * P:(q + 1) * P]) for t in range(NTILE)])
                elif kind == "gu":
                    n0, count, lead = s["n0"], 2 * s["count"], 4
                    for u in range(lead):
                        mm(n0 + u, xh, xl, first=(xg_ready, 8 * s["prod"]) if u == 0 and s["first"] else None)
                        if u == 0 and s["norm"] is not None:
                            norm_job(s)
                    with pe.Fori(0, (count - lead) // 4) as i:
                        for u in range(4):
                            mm(n0 + lead + u, xh, xl, turn=i)
                elif kind == "down":
                    for o in range(KD):
                        mm(s["n0"] + o, hh, hl, first=(h_ready, s["hbase"]) if o == 0 else None)
                elif kind == "even_in":
                    n = s["n0"]
                    for b in range(NA):
                        mm(n + b, xh, xl, first=(xg_ready, 8 * s["prod"]) if b == 0 else None)
                        if b == 0:
                            norm_job(s)
                    pe.wait_ge(coll_ready, 1)
                    for j, first, last in ((s["coll"][0], 0, 8), (s["coll"][1], 8, NA)):
                        tposes(j, [((b - first) // 4, b % 4 * P, cacoll[:, b, :]) for b in range(first, last)])
                    for b in range(NA + 1):
                        mm(n + NA + b, xh, xl)
                    for q, j in enumerate(s["l2"]):
                        pe.wait_ge(hn_sq, s["hn0"] + q + 1)
                        sum_job(j, [sq, ut][q % 2])
                elif kind == "core":
                    for c in range(4):
                        pe.wait_ge(slot_free[c], (core_jobs + 3 - c) // 4)
                    pe.wait_ge(rows_ready, 1)
                    for t in range(NTILE):
                        delta_tile(t)
                    for t in range(NTILE):
                        mlstm_tile(t)
                    pe.wait_ge(core["up"], 2 * NTILE)
                    pe.transpose(bank(0)[0:HB, 0:P], pC[:, :, P], ident[:])
                    for h in range(HB):
                        last = pe.transpose(bank(1)[0:DECB, h * P:(h + 1) * P], st[:, h, :, P], ident[:])
                    last.then_inc(core["tr"], 1)
                elif kind == "even_z":
                    pe.wait_ge(states_done, 1)
                    for q, j in enumerate(s["onorm"]):
                        pe.wait_ge(hn_sq, s["hn0"] + q + 1)
                        sum_job(j, [sq, ut][q % 2])
                    for q in range(HA + HB):
                        mm(s["n0"] + q, xh, xl)
                elif kind == "ple":
                    mm(s["n0"], xh, xl, first=(xg_ready, 8 * s["prod"]))
                    norm_job(s)
                    pe.wait_ge(p_loaded, 32 * (s["i"] + 1))
                    for q, j in enumerate(s["pT"]):
                        tposes(j, [(t // 4, t % 4 * P, pstage[:, t, q * P:(q + 1) * P]) for t in range(NTILE)])
                    for o in range(1, KD):
                        mm(s["n0"] + o, xh, xl)
                    pe.wait_ge(h_ready, s["hbase"] + KP)
                    for o in range(KD):
                        mm(s["n0"] + KD + o, hh, hl[:, 6:8, :])
                elif kind == "odd_in":
                    n = s["n0"]
                    for b in range(2 * KD):
                        mm(n + b, xh, xl, first=(xg_ready, 8 * s["prod"]) if b == 0 else None)
                        if b == 0:
                            norm_job(s)
                    pe.wait_ge(coll_ready, 2)
                    tposes(s["coll"][0], [(b // 4, b % 4 * P, cccoll[:, b, :]) for b in range(KD)])
                    for b in range(KD):
                        mm(n + 2 * KD + b, xh, xl)
                elif kind == "final":
                    norm_job(s)
                    for q, j in enumerate(s["y"]):
                        pe.wait_ge(y_in, q + 1)
                        tposes(j, [(t // 4, t % 4 * P, [gt, ut][q % 2][:, t * P:(t + 1) * P]) for t in range(NTILE)])

        @block.scalar
        def _(act):
            own = Tally(act)

            def prep(n, turn=None):
                if n >= NB:
                    return
                kt = blocks[n][1]
                act.wait_ge(raw_loaded[n % 4], turns(16 * (n // 4 + 1), turn, 16))
                if n >= 2:
                    act.wait_ge(job_done, turns(block_job[n - 2] + 1, turn, 4))
                if blocks[n][0][0] is None:
                    act.wait_ge(in_loaded[4], 2 * 16)
                    act.copy(whi[:, n % 2].rearrange("p k (q c) -> p k q c", q=4)[:, :, :, 0:4],
                             wg[:].rearrange("p k (q c) -> p k q c", q=4)).then_inc(hi_ready, 1)
                else:
                    act.copy(whi[:, n % 2, 0:kt, :], raw[:, n % 4, 0:kt, :]).then_inc(hi_ready, 1)

            def produce(p, j, g):
                act.wait_ge(x_new, 8 * p + j + 1)
                act.activation([sq, stt][j % 2][:], x[:, j, :], ACT.Square).then_inc(sq_ready, 1)
                if g is not None:
                    act.activation(xh[:, j, :], x[:, j, :], ACT.Copy, scale=vec1[:, g + j:g + j + 1]).then_inc(xg_hi, 1)

            def norm_root(s):
                j = s["norm"]
                act.wait_ge(job_done, j + 1)
                own(act.activation(halves(r[:]), ps[j % 4][:, :, 0:HT], ACT.Sqrt, scale=1.0 / D, bias=eps[:]).then_inc(root_ready, 1), root_ready)
                act.sem_inc(slot_free[j % 4], 1)

            def head_root(s, q, j, scale):
                act.wait_ge(job_done, j + 1)
                if q >= 1:
                    act.wait_ge(hn_used, s["hn0"] + q)
                own(act.activation(halves(hf[:]), ps[j % 4][:, :, 0:HT], ACT.Sqrt, scale=scale, bias=eps[:]).then_inc(hn_root, 1), hn_root)
                act.sem_inc(slot_free[j % 4], 1)

            prep(0)
            prep(1)
            act.wait_ge(pool_consts, 1)
            for s in stages:
                kind = s["kind"]
                if kind == "load":
                    for q in range(KD):
                        produce(0, q, 0)
                elif kind == "gu":
                    n0, count, lead = s["n0"], 2 * s["count"], 4

                    def step(u, turn=None):
                        prep(n0 + u + 2, turn)
                        if u == 0 and s["norm"] is not None:
                            norm_root(s)
                        if u % 2 == 0:
                            act.wait_ge(gate_in, turns(s["act0"] + u // 2 + 1, turn, 2))
                            act.activation(stt[:], gt[:], ACT.Silu).then_inc(act_out, 1)

                    for u in range(lead):
                        step(u)
                    trips = (count - lead - 2) // 4
                    with act.Fori(0, trips) as i:
                        for u in range(4):
                            step(lead + u, i)
                    for u in range(lead + 4 * trips, count):
                        step(u)
                elif kind == "down":
                    for o in range(KD):
                        prep(s["n0"] + o + 2)
                        if s["last"]:
                            produce(s["prod"], o, s["g"])
                elif kind == "even_in":
                    n = s["n0"]
                    for b in range(NA):
                        prep(n + b + 2)
                        if b == 0:
                            norm_root(s)
                        act.wait_ge(conv_in, b + 1)
                        pos = s["pos"][b]
                        act.activation(qkv[:, pos, 0:SEQ], ct[:, 0:SEQ], ACT.Silu)
                        act.activation(qkv[:, pos, SEQ:T].rearrange("p (b t) -> p b t", t=DECT),
                                       ct[:, SEQ + CA:HISTA].rearrange("p (b t) -> p b t", t=DECT + CA)[:, :, 0:DECT],
                                       ACT.Silu).then_inc(conv_out, 1)
                    prep(n + NA + 2)
                    act.wait_ge(row_in, 1)
                    own(act.activation(R1[0:4, :], R1[0:4, :], ACT.Sigmoid).then_inc(act_own, 1), act_own)
                    own(act.activation(small[0:4, 4:5], small[0:4, 0:1], ACT.Exp).then_inc(act_own, 1), act_own)
                    for src, t1, t2, bias, sgn in ((gt, hf, sq, small[0:4, 1:2], 1.0), (ut, hist, ct, small[0:4, 5:6], -1.0)):
                        a, b_, c = src[0:4, 0:T], t1[0:4, 0:T], t2[0:4, 0:T]
                        own(act.activation(b_, a, ACT.Abs, bias=bias, scale=sgn).then_inc(act_own, 1), act_own)
                        own(act.activation(b_, b_, ACT.Exp, scale=-1.0).then_inc(act_own, 1), act_own)
                        own(act.activation(b_, b_, ACT.Ln, bias=1.0).then_inc(act_own, 1), act_own)
                        own(act.activation(c, a, ACT.Relu, bias=bias, scale=sgn).then_inc(row_act, 1), row_act)
                    for b in range(NA):
                        prep(n + NA + 1 + b + 2)
                    for q, j in enumerate(s["l2"]):
                        head_root(s, q, j, 1.0)
                elif kind == "core":
                    for t in range(NTILE):
                        L = LVLS if t == NTILE - 1 else LVL
                        li = (LVL - 1) * t
                        act.wait_ge(core["expin"], t + 1)
                        act.activation(W(1), W(1), ACT.Exp).then_inc(core["gam"], 1)
                        act.activation(W(2), heads(1), ACT.Exp)
                        act.activation(W(3), heads(2), ACT.Exp).then_inc(core["eg"], 1)
                        for l in range(1, L):
                            act.wait_ge(core["m1"], li + l)
                            act.copy(W(8), heads(0)).then_inc(core["m1c"], 1)
                        act.wait_ge(core["rt"], t + 1)
                        act.copy(W(8), heads(4)).then_inc(core["rtok"], 1)
                        act.wait_ge(core["u"], t + 1)
                        act.copy(W(1), heads(5)).then_inc(core["utok"], 1)
                    for t in range(NTILE):
                        g = NTILE + t
                        act.wait_ge(core["bcast"], g + 1)
                        act.copy(W9[:, 5, :].rearrange("p (h c) -> p h c", h=HB)[:, :, 0:P], heads(6)).then_inc(core["vt"], 1)
                        act.wait_ge(core["expin"], g + 1)
                        act.activation(W(0), W(0), ACT.Exp).then_inc(core["gam"], 1)
                        act.activation(W(1), heads(1), ACT.Exp)
                        act.activation(W(2), heads(2), ACT.Exp)
                        act.activation(W(4), heads(3), ACT.Exp).then_inc(core["eg"], 1)
                        act.wait_ge(core["tr"], g + 1)
                        act.copy(W(6), heads(0)).then_inc(core["ktok"], 1)
                elif kind == "even_z":
                    for q, j in enumerate(s["onorm"]):
                        head_root(s, q, j, 1.0 / P)
                    for q in range(HA + HB):
                        prep(s["n0"] + q + 2)
                        act.wait_ge(gate_in, s["act0"] + q + 1)
                        act.activation(stt[:], gt[:], ACT.Silu if q < HA else ACT.Sigmoid).then_inc(act_out, 1)
                elif kind == "ple":
                    for o in range(KD):
                        prep(s["n0"] + o + 2)
                        if o == 0:
                            norm_root(s)
                        act.wait_ge(gate_in, s["act0"] + o + 1)
                        act.activation(sig[:, o, :], gt[:], ACT.Sigmoid).then_inc(act_out, 1)
                        if o == 0:
                            pass
                    for o in range(KD):
                        prep(s["n0"] + KD + o + 2)
                        produce(s["next"], o, s["g"] if s["i"] + 1 < DEPTH else None)
                elif kind == "odd_in":
                    for b in range(3 * KD):
                        prep(s["n0"] + b + 2)
                        if b == 0:
                            norm_root(s)
                elif kind == "final":
                    norm_root(s)

        @block.vector
        def _(dve):
            own = Tally(dve)

            def o1(i):
                own(i.then_inc(dve_own, 1), dve_own)

            def mul(out, a, b):
                o1(dve.tensor_tensor(out, a, b, ALU.mult))

            def free(j):
                dve.sem_inc(slot_free[j % 4], 1)

            def P2(j):
                return ps[j % 4][:, :, 0:HT]

            def done(j, turn=None):
                dve.wait_ge(job_done, turns(j + 1, turn, 4))

            def produce(p, j, g):
                dve.wait_ge(sq_ready, 8 * p + j + 1)
                src = [sq, stt][j % 2][:]
                if j == 0:
                    o1(dve.tensor_copy(sumsq[:], src))
                elif g is None:
                    own(dve.tensor_tensor(sumsq[:], sumsq[:], src, ALU.add).then_inc(xg_ready, 1), xg_ready)
                else:
                    o1(dve.tensor_tensor(sumsq[:], sumsq[:], src, ALU.add))
                if g is None:
                    if j == 0:
                        dve.sem_inc(xg_ready, 1)
                        own.counts[xg_ready.name] += 1
                    return
                dve.wait_ge(xg_hi, 8 * p + j + 1)
                own(dve.scalar_tensor_tensor(xl[:, j, :], x[:, j, :], vec1[:, g + j:g + j + 1], xh[:, j, :].bitcast(fp32),
                                             ALU.mult, ALU.subtract).then_inc(xg_ready, 1), xg_ready)

            def norm_recip(s):
                dve.wait_ge(root_ready, own_norms[0] + 1)
                own_norms[0] += 1
                o1(dve.reciprocal(r[:], r[:]))

            own_norms = [0]

            def split_hidden(slot, turn=None, step=None):
                mul(hf[:], stt[:], ut[:])
                at_ = slice(slot, slot + 1) if turn is None else bass.ds(turn * step + slot, 1)
                o1(dve.tensor_tensor(hh[:, at_, :], stt[:].unsqueeze(1), ut[:].unsqueeze(1), ALU.mult))
                own(dve.tensor_tensor(hl[:, at_, :], hf[:].unsqueeze(1), hh[:, at_, :].bitcast(fp32), ALU.subtract).then_inc(h_ready, 1), h_ready)

            def head_norms(s, pieces):
                def squares(q):
                    own(dve.tensor_tensor([sq, ut][q % 2][:], pieces[q][0], pieces[q][0], ALU.mult).then_inc(hn_sq, 1), hn_sq)

                squares(0)
                for q, (src, scalar) in enumerate(pieces):
                    if q + 1 < len(pieces):
                        squares(q + 1)
                    dve.wait_ge(hn_root, s["hn0"] + q + 1)
                    o1(dve.reciprocal(gt[:], hf[:]))
                    own(dve.scalar_tensor_tensor(src, src, scalar, gt[:], ALU.mult, ALU.mult).then_inc(hn_used, 1), hn_used)

            def y_evac(q, j):
                done(j)
                o1(dve.tensor_copy(ystage[:, 0:4, q * P:(q + 1) * P], ps[j % 4][:, 0, :].rearrange("p (t c) -> p t c", c=P)))
                own(dve.tensor_copy(ystage[:, 4, q * P:(q + 1) * P], ps[j % 4][:, 1, 0:P]).then_inc(y_out, 1), y_out)
                free(j)

            def delta_tile(t):
                sample = t == NTILE - 1
                L = LVLS if sample else LVL
                li = (LVL - 1) * t
                z = slice(t * P, (t + 1) * P)
                q, k, v = (qkv[:, a:a + HA, z] for a in (0, 4, 16))
                over_heads = lambda m: m.unsqueeze(1).to_broadcast([P, HA, P])
                dve.wait_ge(core["bcast"], t + 1)
                o1(dve.tensor_copy(gcol[:, 0:4], bank(3)[:, 32:36]))
                own(dve.tensor_tensor(W(0), k, heads(0), ALU.mult).then_inc(core["prod"], 1), core["prod"])
                for h in range(HA):
                    sm = core["expin"] if h == HA - 1 else dve_own
                    own(dve.tensor_scalar(W(1)[:, h], heads(1)[:, h], gcol[:, h:h + 1], 0.0, ALU.subtract, ALU.min).then_inc(sm, 1), sm)
                mul(v, v, heads(0))
                dve.wait_ge(core["gam"], t + 1)
                mul(W(1), W(1), over_heads(incl[:, 1 if sample else 0, :]))
                dve.wait_ge(core["np"], t + 1)
                mul(W(4), heads(4), W(1))
                mul(W(5), heads(5), W(1))
                dve.wait_ge(core["eg"], t + 1)
                own(dve.tensor_tensor(W(3), W(3), k, ALU.mult).then_inc(core["kend"], 1), core["kend"])
                own(dve.tensor_tensor(W(1), W(4), over_heads(level[:, 0, :]), ALU.mult).then_inc(core["c0"], 1), core["c0"])
                o1(dve.tensor_tensor(W(7), over_heads(ident[:]), W(1), ALU.subtract))
                mul(W(0), W(0), W(2))
                mul(q, q, W(2))
                dve.wait_ge(core["tr"], t + 1)
                own(dve.tensor_tensor(W(6), over_heads(ident[:]), heads(6), ALU.subtract).then_inc(core["x0"], 1), core["x0"])

                def masked(l):
                    own(dve.tensor_tensor(W(1), W(4), over_heads(level[:, l, :]), ALU.mult).then_inc(core["ctl"], 1), core["ctl"])

                masked(1)
                o1(dve.tensor_copy(W(3), heads(7)))
                for l in range(1, L):
                    if l < L - 1:
                        dve.wait_ge(core["m1c"], li + l)
                        masked(l + 1)
                    dve.wait_ge(core["d"], li + l)
                    if l < L - 1:
                        o1(dve.tensor_tensor(W(7), W(7), heads(1), ALU.subtract))
                        own(dve.tensor_tensor(W(6), W(6), heads(2), ALU.subtract).then_inc(core["xr"], 1), core["xr"])
                    else:
                        own(dve.tensor_tensor(W(7), W(7), heads(1), ALU.subtract).then_inc(core["xr"], 1), core["xr"])
                dve.wait_ge(core["ks"], t + 1)
                own(dve.tensor_tensor(W(6), v, heads(3), ALU.subtract).then_inc(core["rT"], 1), core["rT"])
                dve.wait_ge(core["o"], t + 1)
                o1(dve.tensor_copy(v, heads(6)))
                for h in range(HA):
                    sm = core["up"] if h == HA - 1 else dve_own
                    if not sample:
                        own(dve.scalar_tensor_tensor(pS[:, h], pS[:, h], W(2)[:, h, P - 1:P], heads(7)[:, h], ALU.mult, ALU.add).then_inc(sm, 1), sm)
                        continue
                    own(dve.tensor_tensor(uexp(P), W(1)[:, h].unsqueeze(1).to_broadcast([P, DECB, P]),
                                          bmask[:].unsqueeze(2).to_broadcast([P, DECB, P]), ALU.mult).then_inc(core["uexp"], 1), core["uexp"])
                    ends = W(2)[:, h].rearrange("p (b t) -> p b t", t=DECT)[:, :, DECT - 1:DECT].to_broadcast([P, DECB, P])
                    mul(sg[:, h], sg[:, h], ends)
                    dve.wait_ge(core["sup"], h + 1)
                    for c in range(2):
                        sc = sm if c else dve_own
                        own(dve.tensor_tensor(sg[:, h, 4 * c:4 * c + 4], sg[:, h, 4 * c:4 * c + 4],
                                              ps[h % 2][:, c, :].rearrange("p (b v) -> p b v", v=P), ALU.add).then_inc(sc, 1), sc)

            def mlstm_tile(t):
                sample = t == NTILE - 1
                g = NTILE + t
                z = slice(t * P, (t + 1) * P)
                q, k, v = (qkv[:, a:a + HB, z] for a in (8, 12, 20))
                scale = float(DK) ** -0.5
                dve.wait_ge(core["bcast"], g + 1)
                o1(dve.tensor_copy(gcol[:, 4:8], bank(4)[:, 96:100]))
                for h in range(HB):
                    sm = core["expin"] if h == HB - 1 else dve_own
                    own(dve.tensor_scalar(W(0)[:, h], heads(0)[:, h], gcol[:, 4 + h:5 + h], 0.0, ALU.add, ALU.min).then_inc(sm, 1), sm)
                dve.wait_ge(core["gam"], g + 1)
                mul(W(0), W(0), incl[:, 1 if sample else 0, :].unsqueeze(1).to_broadcast([P, HB, P]))
                o1(dve.scalar_tensor_tensor(W(3), heads(5), scale, W(0), ALU.mult, ALU.mult))
                dve.wait_ge(core["eg"], g + 1)
                o1(dve.scalar_tensor_tensor(q, q, scale, W(1), ALU.mult, ALU.mult))
                o1(dve.memset(W9[:, 5, :].rearrange("p (h c) -> p h c", h=HB)[:, :, P:MW], 1.0))
                own(dve.tensor_tensor(W(4), W(4), k, ALU.mult).then_inc(core["kend"], 1), core["kend"])
                dve.wait_ge(core["np"], g + 1)
                o1(dve.tensor_scalar(W(7), heads(2), -1.0, None, ALU.mult))
                o1(dve.tensor_tensor(W(7), W(7), heads(2), ALU.max))
                o1(dve.tensor_tensor(W(7), W(7), W(2), ALU.max))
                o1(dve.reciprocal(W(7), W(7)))
                mul(v, heads(1), W(7))
                if not sample:
                    dve.wait_ge(core["o"], g + 1)
                for h in range(HB):
                    sm = core["up"] if h == HB - 1 else dve_own
                    if not sample:
                        own(dve.scalar_tensor_tensor(pC[:, h], pC[:, h], W(1)[:, h, P - 1:P],
                                                     bank(3 + h // 2)[:, h % 2 * MW:(h % 2 + 1) * MW], ALU.mult, ALU.add).then_inc(sm, 1), sm)
                        continue
                    own(dve.tensor_tensor(uexp(MW), W9[:, 5, h * MW:(h + 1) * MW].unsqueeze(1).to_broadcast([P, DECB, MW]),
                                          bmask[:].unsqueeze(2).to_broadcast([P, DECB, MW]), ALU.mult).then_inc(core["uexp"], 1), core["uexp"])
                    ends = W(1)[:, h].rearrange("p (b t) -> p b t", t=DECT)[:, :, DECT - 1:DECT].to_broadcast([P, DECB, MW])
                    mul(st[:, h], st[:, h], ends)
                    dve.wait_ge(core["sup"], HA + h + 1)
                    for c, (a, b) in enumerate([(0, 3), (3, 6), (6, 8)]):
                        sc = sm if c == 2 else dve_own
                        own(dve.tensor_tensor(st[:, h, a:b], st[:, h, a:b],
                                              bank(3 + c)[:, 0:(b - a) * MW].rearrange("p (b v) -> p b v", v=MW), ALU.add).then_inc(sc, 1), sc)


            o1(dve.memset(eps[:], EPS))
            o1(dve.memset(pS[:], 0.0))
            o1(dve.memset(pC[:], 0.0))
            for s in stages:
                kind = s["kind"]
                if kind == "load":
                    j = s["vec"]
                    done(j)
                    o1(dve.tensor_copy(vec1[:], ps[j % 4][:, 0, 0:NV1]))
                    o1(dve.tensor_copy(vec2[:], ps[j % 4][:, 1, 0:NV2]))
                    free(j)
                    j = s["cs"]
                    done(j)
                    o1(dve.tensor_copy(castate[:].rearrange("p a b -> p (a b)"), ps[j % 4][:, 0, 0:NA * DECB * CA]))
                    o1(dve.tensor_copy(ccstate[:].rearrange("p a b -> p (a b)"), ps[j % 4][:, 1, 0:KD * DECB * CC]))
                    free(j)
                    for q, j in enumerate(s["x"]):
                        done(j)
                        o1(dve.tensor_copy(x[:, q, 0:SEQ], ps[j % 4][:, 0, :]))
                        own(dve.tensor_copy(x[:, q, SEQ:T], ps[j % 4][:, 1, 0:P]).then_inc(x_new, 1), x_new)
                        free(j)
                        produce(0, q, 0)
                elif kind == "gu":
                    n0, lead = s["n0"], 4

                    def pair(q, turn=None):
                        ja, jb = block_job[n0 + 2 * q], block_job[n0 + 2 * q + 1]
                        if q == 0 and s["norm"] is not None:
                            norm_recip(s)
                        done(ja, turn)
                        own(dve.tensor_tensor(halves(gt[:]), P2(ja), halves(r[:]), ALU.mult).then_inc(gate_in, 1), gate_in)
                        free(ja)
                        done(jb, turn)
                        mul(halves(ut[:]), P2(jb), halves(r[:]))
                        free(jb)
                        dve.wait_ge(act_out, turns(s["act0"] + q + 1, turn, 2))
                        split_hidden(q, turn, 2)

                    pair(0)
                    pair(1)
                    trips = (s["count"] - 2) // 2
                    with dve.Fori(0, trips) as i:
                        own.enter(i, {gate_in: 2, dve_own: 6, h_ready: 2})
                        pair(2, i)
                        pair(3, i)
                    own.leave(trips)
                elif kind == "down":
                    for o in range(KD):
                        j = block_job[s["n0"] + o]
                        done(j)
                        sm = x_new if s["last"] else dve_own
                        own(dve.scalar_tensor_tensor(halves(x[:, o, :]), P2(j), s["scale"], halves(x[:, o, :]),
                                                     ALU.mult, ALU.add).then_inc(sm, 1), sm)
                        free(j)
                        if s["last"]:
                            produce(s["prod"], o, s["g"])
                elif kind == "even_in":
                    n = s["n0"]
                    NR = CA + DECB * CA
                    hs = hist[:, SEQ + CA:HISTA].rearrange("p (b t) -> p b t", t=DECT + CA)
                    o1(dve.memset(hist[:, 0:CA], 0.0))
                    for b in range(NA):
                        j = block_job[n + b]
                        if b == 0:
                            norm_recip(s)
                        done(j)
                        p_ = ps[j % 4]
                        mul(hist[:, CA:CA + HT], p_[:, 0, 0:HT], r[:, 0:HT])
                        mul(hist[:, CA + HT:CA + SEQ], p_[:, 1, 0:SEQ - HT], r[:, HT:SEQ])
                        mul(hs[:, :, CA:], p_[:, 1, SEQ - HT:HT].rearrange("p (b t) -> p b t", t=DECT),
                            r[:, SEQ:T].rearrange("p (b t) -> p b t", t=DECT))
                        free(j)
                        o1(dve.tensor_copy(hs[:, :, 0:CA], castate[:, b, :].rearrange("p (b t) -> p b t", t=CA)))
                        o1(dve.tensor_copy(cacoll[:, b, 0:CA], hist[:, SEQ:SEQ + CA]))
                        sm = coll_ready if b == NA - 1 else dve_own
                        own(dve.tensor_copy(cacoll[:, b, CA:].rearrange("p (b t) -> p b t", t=CA), hs[:, :, DECT:]).then_inc(sm, 1), sm)
                        C = HISTA - CA
                        if b:
                            dve.wait_ge(conv_out, b)
                        o1(dve.tensor_scalar(ct[:, 0:C], hist[:, 0:C], vec2[:, b:b + 1], None, ALU.mult))
                        for w in range(1, KA):
                            sm = conv_in if w == KA - 1 else dve_own
                            own(dve.scalar_tensor_tensor(ct[:, 0:C], hist[:, w:w + C], vec2[:, w * NA + b:w * NA + b + 1],
                                                         ct[:, 0:C], ALU.mult, ALU.add).then_inc(sm, 1), sm)
                    for j, a, b in ((s["coll"][0], 0, 8), (s["coll"][1], 8, NA)):
                        done(j)
                        for c in range((b - a) // 4):
                            sm = dve_own
                            last = dve.tensor_copy(castout[0:NR, (a + 4 * c) * P:(a + 4 * c + 4) * P], ps[j % 4][0:NR, c, :])
                            if b == NA:
                                own(last.then_inc(coll_out, 1), coll_out)
                            else:
                                o1(last)
                        free(j)
                    dve.wait_ge(conv_out, NA)
                    j = block_job[n + NA]
                    done(j)
                    for q, dst in enumerate((R1, gt, stt, ut)):
                        mul(halves(dst[0:4, :]), ps[j % 4][32 * q:32 * q + 4, :, 0:HT], halves(r[32 * q:32 * q + 4, :]))
                    free(j)
                    dve.wait_ge(in_loaded[3], 5 * 16)
                    o1(dve.tensor_scalar(small[0:4, 5:6], small[0:4, 3:4], -1.0, None, ALU.mult))
                    o1(dve.memset(R2[:], 0.0))
                    reset = sumsq[0:4, :]
                    o1(dve.memset(reset, 1.0))
                    o1(dve.memset(reset[:, 0:SEQ].rearrange("p (c t) -> p c t", t=P)[:, :, 0:1], 0.0))
                    own(dve.memset(reset[:, SEQ:T].rearrange("p (c t) -> p c t", t=DECT)[:, :, 0:1], 0.0).then_inc(row_in, 1), row_in)
                    dve.wait_ge(row_act, 1)
                    R = lambda t_: t_[0:4, 0:T]
                    o1(dve.tensor_scalar(small[0:4, 6:7], small[0:4, 4:5], -1.0, None, ALU.mult))
                    o1(dve.tensor_tensor(R(hf), R(hf), R(sq), ALU.add))
                    o1(dve.tensor_scalar(R(gt), R(hf), small[0:4, 6:7], None, ALU.mult))
                    o1(dve.tensor_tensor_scan(R(hf), reset, R(gt), 0.0, ALU.mult, ALU.add))
                    o1(dve.tensor_copy(R1[32:36, :], R(hf)))

                    def seg(row, last=False):
                        a = row[:, 0:SEQ].rearrange("p (c t) -> p c t", t=P)
                        b = row[:, SEQ:T].rearrange("p (c t) -> p c t", t=DECT)
                        return (a[:, :, P - 1:P], b[:, :, DECT - 1:DECT]) if last else (a, b)

                    for dst, row, end in zip(seg(R1[64:68, :]), seg(R(hf)), seg(R(hf), True)):
                        o1(dve.tensor_tensor(dst, end.to_broadcast(row.shape), row, ALU.subtract))
                    dve.wait_ge(row_act, 2)
                    o1(dve.scalar_tensor_tensor(R(ut), R(hist), -1.0, R(ct), ALU.mult, ALU.subtract))
                    o1(dve.tensor_scalar(R(stt), R(stt), small[0:4, 2:3], None, ALU.add))
                    o1(dve.tensor_tensor_scan(R(sq), reset, R(ut), 0.0, ALU.mult, ALU.add))
                    o1(dve.tensor_tensor_scan(ct[0:4, 0:SEQ], ut[0:4, 0:SEQ], stt[0:4, 0:SEQ], 0.0, ALU.add, ALU.max))
                    for b in range(DECB):
                        z = slice(SEQ + b * DECT, SEQ + (b + 1) * DECT)
                        o1(dve.tensor_tensor_scan(ct[0:4, z], ut[0:4, z], stt[0:4, z], m0[0:4, b:b + 1], ALU.add, ALU.max))
                    NP = SEQ // P
                    o1(dve.memset(minr[:, 0:1], 0.0))
                    o1(dve.tensor_copy(minr[:, 1:NP].unsqueeze(2), seg(R(ct), True)[0][:, 0:NP - 1]))
                    o1(dve.tensor_copy(minr[:, NP:NSEG], m0[:, :]))
                    o1(dve.tensor_copy(mfin[:, 0:1], ct[0:4, SEQ - 1:SEQ]))
                    own(dve.tensor_copy(mfin[:, 1:].unsqueeze(2), seg(R(ct), True)[1]).then_inc(m_final, 1), m_final)
                    o1(dve.tensor_tensor(R2[0:4, :], R(sq), R(ct), ALU.subtract))
                    for dst, row, m_ in zip(seg(R2[32:36, :]), seg(R2[0:4, :]), (minr[:, 0:NP], minr[:, NP:NSEG])):
                        o1(dve.tensor_tensor(dst, row, m_.unsqueeze(2).to_broadcast(row.shape), ALU.add))
                    o1(dve.tensor_scalar(R2[64:68, :], R(ct), -1.0, None, ALU.mult))
                    o1(dve.tensor_tensor(R(hf), R(stt), R(sq), ALU.subtract))
                    o1(dve.tensor_copy(R1[96:100, :], R(hf)))
                    for dst, row, end in zip(seg(R2[96:100, :]), seg(R(hf)), seg(R2[0:4, :], True)):
                        o1(dve.tensor_tensor(dst, row, end.to_broadcast(row.shape), ALU.add))
                    dve.sem_inc(rows_ready, 1)
                    for b in range(NA):
                        j = block_job[n + NA + 1 + b]
                        done(j)
                        mul(halves(qkv[:, s["pos"][NA + b], :]), P2(j), halves(r[:]))
                        free(j)
                    head_norms(s, [(qkv[:, q, :], float(DK) ** -0.5 if q < HA else 1.0) for q in range(2 * HA)])
                elif kind == "core":
                    for t in range(NTILE):
                        delta_tile(t)
                    for t in range(NTILE):
                        if t == NTILE - 1:
                            dve.wait_ge(states_loaded, 16 * (HA + 2 * HB))
                        mlstm_tile(t)
                    dve.wait_ge(core["tr"], 2 * NTILE + 1)
                    o1(dve.tensor_copy(nout[0:HB, 0:P], bank(0)[0:HB, 0:P]))
                    own(dve.tensor_copy(nout[0:DECB, P:], bank(1)[0:DECB, :]).then_inc(states_done, 1), states_done)
                elif kind == "even_z":
                    c1 = NV2 - 1 - HB
                    head_norms(s, [(qkv[:, 16 + q, :], vec2[:, NV2 - 1:NV2] if q < HA else vec2[:, c1 + q - HA:c1 + q - HA + 1])
                                   for q in range(HA + HB)])
                    for q in range(HA + HB):
                        j = block_job[s["n0"] + q]
                        done(j)
                        own(dve.tensor_tensor(halves(gt[:]), P2(j), halves(r[:]), ALU.mult).then_inc(gate_in, 1), gate_in)
                        free(j)
                        dve.wait_ge(act_out, s["act0"] + q + 1)
                        o = qkv[:, 16 + q, :]
                        mul(hf[:], stt[:], o)
                        o1(dve.tensor_tensor(hh[:, q, :], stt[:], o, ALU.mult))
                        own(dve.tensor_tensor(hl[:, q, :], hf[:], hh[:, q, :].bitcast(fp32), ALU.subtract).then_inc(h_ready, 1), h_ready)
                elif kind == "ple":
                    for o in range(KD):
                        j = block_job[s["n0"] + o]
                        if o == 0:
                            norm_recip(s)
                        done(j)
                        if o:
                            dve.wait_ge(act_out, s["act0"] + o)
                        own(dve.tensor_tensor(halves(gt[:]), P2(j), halves(r[:]), ALU.mult).then_inc(gate_in, 1), gate_in)
                        free(j)
                        if o == 0:
                            for q, j in enumerate(s["pT"]):
                                done(j)
                                for c, z in ((0, slice(0, SEQ)), (1, slice(SEQ, T))):
                                    w = z.stop - z.start
                                    o1(dve.tensor_copy(hh[:, q, z], ps[j % 4][:, c, 0:w]))
                                    sm = h_ready if c else dve_own
                                    own(dve.tensor_tensor(hl[:, 6 + q, z], ps[j % 4][:, c, 0:w], hh[:, q, z].bitcast(fp32),
                                                          ALU.subtract).then_inc(sm, 1), sm)
                                free(j)
                    for o in range(KD):
                        j = block_job[s["n0"] + KD + o]
                        done(j)
                        dve.wait_ge(act_out, s["act0"] + o + 1)
                        mul(halves(ut[:]), P2(j), halves(sig[:, o, :]))
                        free(j)
                        own(dve.tensor_tensor(x[:, o, :], x[:, o, :], ut[:], ALU.add).then_inc(x_new, 1), x_new)
                        produce(s["next"], o, s["g"] if s["i"] + 1 < DEPTH else None)
                elif kind == "odd_in":
                    n = s["n0"]
                    hs = hist[:, SEQ + CC:HISTC].rearrange("p (b t) -> p b t", t=DECT + CC)
                    o1(dve.memset(hist[:, 0:CC], 0.0))
                    for b in range(KD):
                        ja, jb = block_job[n + 2 * b], block_job[n + 2 * b + 1]
                        if b == 0:
                            norm_recip(s)
                        done(ja)
                        mul(halves(gt[:]), P2(ja), halves(r[:]))
                        free(ja)
                        done(jb)
                        mul(halves(ut[:]), P2(jb), halves(r[:]))
                        free(jb)
                        mul(hist[:, CC:CC + SEQ], gt[:, 0:SEQ], ut[:, 0:SEQ])
                        mul(hs[:, :, CC:], gt[:, SEQ:T].rearrange("p (b t) -> p b t", t=DECT),
                            ut[:, SEQ:T].rearrange("p (b t) -> p b t", t=DECT))
                        o1(dve.tensor_copy(hs[:, :, 0:CC], ccstate[:, b, :].rearrange("p (b t) -> p b t", t=CC)))
                        o1(dve.tensor_copy(cccoll[:, b, 0:CC], hist[:, SEQ:SEQ + CC]))
                        sm = coll_ready if b == KD - 1 else dve_own
                        own(dve.tensor_copy(cccoll[:, b, CC:].rearrange("p (b t) -> p b t", t=CC), hs[:, :, DECT:]).then_inc(sm, 1), sm)
                        C = HISTC - CC
                        wc = lambda w: vec2[:, KA * NA + w * KD + b:KA * NA + w * KD + b + 1]
                        o1(dve.tensor_scalar(ct[:, 0:C], hist[:, 0:C], wc(0), None, ALU.mult))
                        for w in range(1, KC):
                            o1(dve.scalar_tensor_tensor(ct[:, 0:C], hist[:, w:w + C], wc(w), ct[:, 0:C], ALU.mult, ALU.add))
                        o1(dve.tensor_copy(sig[:, b, 0:SEQ], ct[:, 0:SEQ]))
                        o1(dve.tensor_copy(sig[:, b, SEQ:T].rearrange("p (b t) -> p b t", t=DECT),
                                           ct[:, SEQ + CC:HISTC].rearrange("p (b t) -> p b t", t=DECT + CC)[:, :, 0:DECT]))
                    NR = CC + DECB * CC
                    j = s["coll"][0]
                    done(j)
                    for c in range(2):
                        sm = coll_out if c else dve_own
                        own(dve.tensor_copy(ccout[0:NR, c * 4 * P:(c + 1) * 4 * P], ps[j % 4][0:NR, c, :]).then_inc(sm, 1), sm)
                    free(j)
                    for b in range(KD):
                        j = block_job[n + 2 * KD + b]
                        done(j)
                        mul(halves(ut[:]), P2(j), halves(r[:]))
                        free(j)
                        mul(hf[:], sig[:, b, :], ut[:])
                        o1(dve.tensor_tensor(hh[:, b, :], sig[:, b, :], ut[:], ALU.mult))
                        own(dve.tensor_tensor(hl[:, b, :], hf[:], hh[:, b, :].bitcast(fp32), ALU.subtract).then_inc(h_ready, 1), h_ready)
                elif kind == "final":
                    norm_recip(s)
                    for q, j in enumerate(s["y"]):
                        if q >= 2:
                            done(s["y"][q - 2])
                        g = DEPTH * 4 * KD + q
                        own(dve.scalar_tensor_tensor([gt, ut][q % 2][:], x[:, q, :], vec1[:, g:g + 1], r[:], ALU.mult, ALU.mult).then_inc(y_in, 1), y_in)
                        if q >= 1:
                            y_evac(q - 1, s["y"][q - 1])
                    y_evac(KD - 1, s["y"][KD - 1])


def kernel(**inputs):
    import numpy as np
    import concourse.bacc as bacc
    from concourse.bass_utils import run_bass_kernel_spmd
    nc = bacc.Bacc("TRN2", target_bir_lowering=False, num_devices=1)
    arrays, ins = {}, {}
    for name, value in inputs.items():
        a = np.ascontiguousarray(value)
        arrays["in_" + name] = a
        ins[name] = nc.dram_tensor("in_" + name, a.shape, mybir.dt.from_np(a.dtype), kind="ExternalInput").ap()
    xp, xs = arrays["in_x_prompt"].shape, arrays["in_x_sample"].shape
    conv, S, C = (arrays["in_state_" + k].shape for k in ("gdn_conv", "gdn_S", "mlstm_C"))
    n, m, cc = (arrays["in_state_" + k].shape for k in ("mlstm_n", "mlstm_m", "conv"))
    one = lambda s: (s[0], xp[0]) + tuple(s[2:])
    shapes = dict(y_p=xp, y_s=xs, gdn_conv_p=one(conv), gdn_S_p=one(S), mlstm_C_p=one(C), mlstm_n_p=one(n),
                  mlstm_m_p=one(m), conv_p=one(cc), gdn_conv_s=conv, gdn_S_s=S, mlstm_C_s=C, mlstm_n_s=n,
                  mlstm_m_s=m, conv_s=cc)
    outs = {k: nc.dram_tensor("out_" + k, tuple(v), mybir.dt.float32, kind="ExternalOutput").ap() for k, v in shapes.items()}
    stream_step(nc, ins, outs)
    res = run_bass_kernel_spmd(nc, [arrays], core_ids=[0]).results[0]
    return tuple(res["out_" + k] for k in shapes)
```

```python
import concourse.bass as bass
from concourse import mybir
from contextlib import ExitStack


def stream_step(nc, ins, outs):
    fp32 = mybir.dt.float32
    fp32r = mybir.dt.float32r
    ALU = mybir.AluOpType
    ACT = mybir.ActivationFunctionType

    P = 128
    BATCH, SEQ, D = ins["x_prompt"].shape
    DECB, DECT, _ = ins["x_sample"].shape
    DEPTH = ins["norm_g"].shape[0]
    DFF = ins["ffn_w_d"].shape[2]
    DPLE = ins["w_ple"].shape[1]
    HA, DK = ins["state_gdn_S"].shape[2:4]
    HB = ins["state_mlstm_C"].shape[2]
    assert BATCH == 1 and DECB * DECT == P and SEQ % P == 0 and HA == HB == 4 and DK == P
    T = SEQ + P
    HT = T // 2
    NTILE = T // P
    KD = D // P
    NF = DFF // P
    PARTS = [8, 8, NF - 16]
    KP = DPLE // P
    KA, KC = ins["gdn_conv_w"].shape[1], ins["conv_c_w"].shape[1]
    EPS = 1e-6
    NA = 3 * HA
    LVL = 7
    LVLS = 4
    MW = P + 1

    ctx = ExitStack()
    with ctx:
        base = nc.sbuf_base
        arena = ctx.enter_context(nc.sbuf_tensor("arena", [P, (229344 - base - 64) // 4], fp32))
        place = [-(-base // 32) * 32]

        def at(name, shape, offset, dt=fp32):
            return nc.alloc_sbuf_tensor_at(name, shape, dt, offset=offset)

        def sb(name, shape, dt=fp32):
            size = 4
            for s in shape[1:]:
                size *= s
            place[0] = -(-place[0] // 32) * 32
            t = at(name, shape, place[0], dt)
            place[0] += size
            assert place[0] <= 229344, (name, place[0])
            return t

        def sem(name):
            return ctx.enter_context(nc.semaphore(name))

        x = sb("x", [P, KD, T])
        xh = sb("xh", [P, KD, T], fp32r)
        xl = sb("xl", [P, KD, T], fp32r)
        raw = sb("raw", [P, 4, KD, P])
        whi = sb("whi", [P, 2, KD, P], fp32r)
        wlo = sb("wlo", [P, 2, KD, P], fp32r)
        PIECE = 4 * T
        B0 = -(-place[0] // 32) * 32
        qkv = sb("qkv", [P, 2 * NA, T])
        hh = at("hh", [P, 8, T], B0, fp32r)
        hl = at("hl", [P, 8, T], B0 + 8 * PIECE, fp32r)
        sig = at("sig", [P, 8, T], B0 + 16 * PIECE)
        xstage = at("xstage", [P, NTILE, D], B0)
        vstage = at("vstage", [P, 2, P], B0 + 8 * PIECE)
        castage = at("castage", [P, NA * P], B0 + 9 * PIECE)
        ccstage = at("ccstage", [P, D], B0 + 12 * PIECE)
        ystage = at("ystage", [P, NTILE, D], B0 + 2 * PIECE)
        pstage = at("pstage", [P, NTILE, DPLE], B0 + 2 * PIECE)
        st = sb("st", [P, HB, DECB, MW])
        sg = at("sg", [P, HA, DECB, P], place[0] - 4 * HB * DECB * MW)
        S0 = place[0] - 4 * HB * DECB * MW
        castout = at("castout", [P, NA * P], S0)
        ccout = at("ccout", [P, D], S0)
        assert 4 * (NA * P + 4 * T) <= 4 * HB * DECB * MW
        rtmp = [at(f"rtmp{i}", [P, T], S0 + 4 * NA * P + i * PIECE) for i in range(4)]
        assert 8 * HA * MW == HB * DECB * MW
        V8 = at("V8", [P, 8, HA * MW], S0)
        pS = sb("pS", [P, HA, P])
        pC = sb("pC", [P, HB, MW])
        r = sb("r", [P, T])
        sumsq = sb("sumsq", [P, T])
        T0 = -(-place[0] // 32) * 32
        W9 = sb("W9", [P, 9, HA * MW])
        gt = at("gt", [P, T], T0)
        stt = at("stt", [P, T], T0 + PIECE)
        ut = at("ut", [P, T], T0 + 2 * PIECE)
        hf = at("hf", [P, T], T0 + 3 * PIECE)
        sq = at("sq", [P, T], T0 + 4 * PIECE)
        HISTA = SEQ + KA - 1 + DECB * (DECT + KA - 1)
        HISTC = SEQ + KC - 1 + DECB * (DECT + KC - 1)
        HISTB = -(-4 * HISTA // 32) * 32
        hist = at("hist", [P, HISTA], T0 + 5 * PIECE)
        ct = at("ct", [P, HISTA], T0 + 5 * PIECE + HISTB)
        root = at("root", [P, T], T0 + 5 * PIECE)
        inv = at("inv", [P, T], T0 + 5 * PIECE + HISTB)
        assert 5 * PIECE + 2 * HISTB <= 9 * HA * MW * 4
        R1 = sb("R1", [P, T])
        nout = at("nout", [P, (HB + 1) * P], place[0] - PIECE)
        R0 = place[0]
        R2 = sb("R2", [P, T])
        CA, CC = KA - 1, KC - 1
        castate = at("castate", [P, NA, DECB * CA], R0)
        cacoll = at("cacoll", [P, NA, CA + DECB * CA], R0 + 4 * NA * DECB * CA)
        ccstate = sb("ccstate", [P, KD, DECB * CC])
        cccoll = at("cccoll", [P, KD, CC + DECB * CC], R0)
        ident = sb("ident", [P, P])
        level = sb("level", [P, LVL, P])
        incl = sb("incl", [P, 2, P])
        bmask = sb("bmask", [P, DECB])
        NV1 = DEPTH * 4 * KD + KD
        NV2 = KA * NA + KC * KD + HB + 1
        vec1 = sb("vec1", [P, NV1])
        vec2 = sb("vec2", [P, NV2])
        one = sb("one", [P, 1])
        eps = sb("eps", [P, 1])
        wg = sb("wg", [P, KD, 16])
        gcol = sb("gcol", [P, 8])
        small = sb("small", [4, 8])
        m0 = sb("m0", [4, DECB])
        mfin = sb("mfin", [4, 1 + DECB])
        NSEG = SEQ // P + DECB
        minr = sb("minr", [4, NSEG])
        cend = sb("cend", [4, NSEG])

        ps = [ctx.enter_context(nc.psum_tensor(f"ps{i}", [P, 2, 512], fp32)) for i in range(4)]

        dt_, ig_, fg_, hf_ = rtmp
        sq_, hi_, ct_ = (qkv[:, 2 * NA - 4 + i, :] for i in range(3))

        def halves(tok):
            return tok.rearrange("p (a b) -> p a b", a=2)

        def bank(i):
            return ps[i // 2][:, i % 2, :]

        def heads(i):
            return bank(i).rearrange("p (h t) -> p h t", h=HA)

        def uexp(width):
            a = 6 if width == P else 7
            return W9[:, a:a + 2, :].rearrange("p a b -> p (a b)")[:, 0:DECB * width].rearrange("p (b c) -> p b c", b=DECB)

        def W(i):
            return W9[:, i, 0:HA * P].rearrange("p (h t) -> p h t", h=HA)

        def V(i):
            return V8[:, i, 0:HA * P].rearrange("p (h t) -> p h t", h=HA)

        raw_loaded = [sem(f"raw_loaded{i}") for i in range(4)]
        hi_ready = sem("hi_ready")
        lo_ready = sem("lo_ready")
        job_done = sem("job_done")
        slot_free = [sem(f"slot_free{i}") for i in range(4)]
        xg_hi = sem("xg_hi")
        xg_ready = sem("xg_ready")
        x_new = sem("x_new")
        sq_ready = sem("sq_ready")
        root_ready = sem("root_ready")
        gate_in = sem("gate_in")
        act_out = sem("act_out")
        h_ready = sem("h_ready")
        dve_own = sem("dve_own")
        act_own = sem("act_own")
        pool_own = sem("pool_own")
        consts_ready = sem("consts_ready")
        pool_consts = sem("pool_consts")
        in_loaded = [sem(f"in_loaded{i}") for i in range(6)]
        out_stored = sem("out_stored")
        p_loaded = sem("p_loaded")
        p_hi = sem("p_hi")
        stage_free = sem("stage_free")
        hn_sq = sem("hn_sq")
        hn_root = sem("hn_root")
        conv_in = sem("conv_in")
        conv_out = sem("conv_out")
        row_in = sem("row_in")
        row_act = sem("row_act")
        rows_ready = sem("rows_ready")
        coll_ready = sem("coll_ready")
        coll_out = sem("coll_out")
        states_loaded = sem("states_loaded")
        states_stored = sem("states_stored")
        states_done = sem("states_done")
        hn_used = sem("hn_used")
        m_final = sem("m_final")
        y_in = sem("y_in")
        y_out = sem("y_out")
        core = {k: sem("core_" + k) for k in
                "bcast prod expin gam eg np kend c0 tr ktok x0 ctl m1 m1c d xr ks rT rt rtok u utok o up state uexp sup vt vtok den".split()}

        ml_pe, ml_act, ml_dve = sem("ml_pe"), sem("ml_act"), sem("ml_dve")
        ML_PE = "gates qin qk floor vt kin kt num den up0 up1".split()
        ML_ACT = "gates qin floor vt kin kt den".split()
        ML_DVE = "gates qk q k out up0 up1".split()

        def ml(steps, t, name):
            return len(steps) * t + steps.index(name) + 1

        blocks = []
        jobs = []
        block_job = []

        def job(kind, n=None):
            jobs.append((kind, n))
            return len(jobs) - 1

        def blk(src, kt, kind):
            blocks.append((src, kt))
            block_job.append(job(kind, len(blocks) - 1))
            return len(blocks) - 1

        stages = []
        prod = 0

        def load_stage():
            nonlocal prod
            s = dict(kind="load", vec=job("vec"), cs=job("cs"), x=[job("xT") for _ in range(KD)], prod=0)
            stages.append(s)
            prod = 1

        def ffn_stage(i, f, first_pair):
            nonlocal prod
            gu, dn = ins["ffn_w_gu"][i, f], ins["ffn_w_d"][i, f]
            j0 = 0
            for part, cnt in enumerate(PARTS):
                s = dict(kind="gu", pair0=first_pair + j0, count=cnt, norm=None, prod=prod - 1, first=part == 0,
                         n0=len(blocks), src=gu, col0=j0)
                for q in range(cnt):
                    blk((gu, (j0 + q) * P), KD, "gate")
                    if part == 0 and q == 0:
                        s["norm"] = job("norm")
                    blk((gu, DFF + (j0 + q) * P), KD, "up")
                stages.append(s)
                last = part == len(PARTS) - 1
                s = dict(kind="down", n0=len(blocks), kt=cnt, last=last, scale=0.5, hbase=first_pair + j0,
                         prod=prod if last else None, g=(i * 4 + (1 if f == 0 else 3)) * KD)
                for o in range(KD):
                    blk((dn, o * P, j0 * P), cnt, "down")
                stages.append(s)
                j0 += cnt
            prod += 1

        pairs = 0
        load_stage()
        ffn_stage(0, 0, pairs)
        pairs += NF
        w_in = ins["w_in_even"][0]
        wcol = [0, HA * P, 2 * HA * P, 3 * HA * P]
        gcol0 = 4 * HA * P
        bcol = [gcol0 + 2 * HA + q * HB * P for q in range(4)]
        icol = bcol[3] + HB * P
        HN_LAG = NA - 2 * HA
        s = dict(kind="even_in", n0=len(blocks), prod=prod - 1, pos=[], l2=[])
        for q in range(3):
            for h in range(HA):
                blk((w_in, wcol[q] + h * P), KD, "conv")
                if q == 0 and h == 0:
                    s["norm"] = job("norm")
                s["pos"].append([0, 4, 16][q] + h)
        s["coll"] = [job("coll"), job("coll")]
        s["gates"] = blk((None, 0), KD, "gates")
        for q in range(3):
            for h in range(HB):
                blk((w_in, bcol[q] + h * P), KD, "plain")
                s["pos"].append([8, 12, 20][q] + h)
                if q * HB + h >= HN_LAG:
                    s["l2"].append(job("hn"))
        stages.append(s)
        stages.append(dict(kind="core"))
        s = dict(kind="even_z", onorm=[], n0=len(blocks))
        for c0 in (wcol[3], bcol[3]):
            for h in range(HA):
                s["onorm"].append(job("hn"))
                blk((w_in, c0 + h * P), KD, "z")
        stages.append(s)
        stages.append(dict(kind="down", n0=len(blocks), kt=KD, last=True, scale=1.0, hbase=pairs, prod=prod, g=2 * KD))
        for o in range(KD):
            blk((ins["w_out_even"][0], o * P, 0), KD, "down")
        prod += 1
        pairs += HA + HB
        ffn_stage(0, 1, pairs)
        pairs += NF

        def ple_stage(i):
            nonlocal prod, pairs
            s = dict(kind="ple", i=i, n0=len(blocks), prod=prod - 1, hbase=pairs)
            for o in range(KD):
                blk((ins["w_ple_gate"][i], o * P), KD, "pgate")
                if o == 0:
                    s["norm"] = job("norm")
                    s["pT"] = [job("pT") for _ in range(KP)]
            for o in range(KD):
                blk((ins["w_ple"][i], o * P), KP, "pemb")
            s["next"] = prod
            s["g"] = (i + 1) * 4 * KD
            stages.append(s)
            prod += 1
            pairs += KP

        ple_stage(0)
        ffn_stage(1, 0, pairs)
        pairs += NF
        w_odd = ins["w_in_odd"][0]
        s = dict(kind="odd_in", n0=len(blocks), prod=prod - 1, hbase=pairs)
        for q in range(KD):
            blk((w_odd, q * P), KD, "gate")
            if q == 0:
                s["norm"] = job("norm")
            blk((w_odd, 2 * D + q * P), KD, "up")
        s["coll"] = [job("coll")]
        for q in range(KD):
            blk((w_odd, D + q * P), KD, "bg")
        stages.append(s)
        stages.append(dict(kind="down", n0=len(blocks), kt=KD, last=True, scale=1.0, hbase=pairs, prod=prod, g=6 * KD))
        for o in range(KD):
            blk((ins["w_out_odd"][0], o * P, 0), KD, "down")
        prod += 1
        pairs += KD
        ffn_stage(1, 1, pairs)
        pairs += NF
        ple_stage(1)
        s = dict(kind="final", prod=prod - 1)
        s["norm"] = job("norm")
        s["y"] = [job("yT") for _ in range(KD)]
        stages.append(s)
        NB = len(blocks)

        hn0 = 0
        for s in stages:
            if s["kind"] == "even_in":
                s["hn0"] = hn0
                hn0 += 2 * HA
            if s["kind"] == "even_z":
                s["hn0"] = hn0
        act0 = 0
        for s in stages:
            s["act0"] = act0
            if s["kind"] == "gu":
                act0 += s["count"]
            elif s["kind"] == "even_z":
                act0 += HA + HB
            elif s["kind"] == "ple":
                act0 += KD

        core_jobs = next(s["onorm"][0] for s in stages if s["kind"] == "even_z")

        class Tally:

            def __init__(self, engine):
                self.engine, self.counts, self.turn, self.per = engine, {}, None, {}

            def __call__(self, _, s):
                self.counts[s.name] = self.counts.get(s.name, 0) + 1
                v = self.counts[s.name]
                self.engine.wait_ge(s, v if self.turn is None else self.turn * self.per[s.name] + v)

            def enter(self, turn, per):
                self.turn, self.per = turn, {k.name: v for k, v in per.items()}
                self.before = dict(self.counts)

            def leave(self, trips):
                for k, v in self.counts.items():
                    body = v - self.before.get(k, 0)
                    assert body == self.per.get(k, 0), (k, body)
                    self.counts[k] = self.before.get(k, 0) + body * trips
                self.turn = None

        def turns(value, turn, per):
            return value if turn is None else turn * per + value

        block = ctx.enter_context(nc.Block())

        @block.sync
        def _(sp):
            xs = xstage[:, :, :]
            sp.dma_start(xs[:, 0:NTILE - 1, :], ins["x_prompt"][0].rearrange("(t p) d -> p t d", p=P)).then_inc(in_loaded[0], 16)
            sp.dma_start(xs[:, NTILE - 1, :], ins["x_sample"].rearrange("b t d -> (b t) d")).then_inc(in_loaded[0], 16)
            sp.dma_start(vstage[0:DEPTH * 4 * KD, 0, :], ins["norm_g"].rearrange("i f (k p) -> (i f k) p", p=P)).then_inc(in_loaded[1], 16)
            sp.dma_start(vstage[DEPTH * 4 * KD:NV1, 0, :], ins["final_norm"].rearrange("(k p) -> k p", p=P)).then_inc(in_loaded[1], 16)
            a, b = KA * NA, KA * NA + KC * KD
            sp.dma_start(vstage[0:a, 1, :], ins["gdn_conv_w"][0].rearrange("j (k p) -> (j k) p", p=P)).then_inc(in_loaded[1], 16)
            sp.dma_start(vstage[a:b, 1, :], ins["conv_c_w"][0].rearrange("j (k p) -> (j k) p", p=P)).then_inc(in_loaded[1], 16)
            sp.dma_start(vstage[b:b + HB, 1, :], ins["mlstm_norm_w"][0].rearrange("(k p) -> k p", p=P)).then_inc(in_loaded[1], 16)
            sp.dma_start(vstage[b + HB:b + HB + 1, 1, :], ins["gdn_norm_w"]).then_inc(in_loaded[1], 16)
            sp.dma_start(castage[0:DECB * CA, :], ins["state_gdn_conv"][0].rearrange("b t c -> (b t) c")).then_inc(in_loaded[2], 16)
            sp.dma_start(ccstage[0:DECB * CC, :], ins["state_conv"][0].rearrange("b t c -> (b t) c")).then_inc(in_loaded[2], 16)
            with nc.allow_non_contiguous_dma(reason="a few words of gate parameters"):
                for q, name in enumerate(["gdn_a_log", "gdn_dt_bias", "mlstm_b_i", "mlstm_b_f"]):
                    sp.dma_start(small[0:4, q:q + 1], ins[name].rearrange("a h -> h a")).then_inc(in_loaded[3], 16)
                sp.dma_start(m0[0:4, :], ins["state_mlstm_m"][0].rearrange("b h -> h b")).then_inc(in_loaded[3], 16)
                wv = w_in.rearrange("(k p) c -> p k c", p=P)
                sp.dma_start(wg[:, :, 0:8], wv[:, :, gcol0:gcol0 + 8]).then_inc(in_loaded[4], 16)
                sp.dma_start(wg[:, :, 8:16], wv[:, :, icol:icol + 8]).then_inc(in_loaded[4], 16)

            def load(n, source, off=0):
                slot = n % 4
                if n >= 4:
                    sp.wait_ge(lo_ready, n - 3 + off)
                sp.dma_start(raw[:, slot, 0:source.shape[1], :], source).then_inc(raw_loaded[slot], 16)

            def source(n):
                src, kt = blocks[n]
                if len(src) == 2:
                    return src[0].rearrange("(k p) c -> p k c", p=P)[:, :, src[1]:src[1] + P]
                return src[0][src[2]:src[2] + kt * P, src[1]:src[1] + P].rearrange("(k p) c -> p k c", p=P)

            n = 0
            for s in stages:
                if s["kind"] == "gu":
                    gv = s["src"].rearrange("(k p) c -> p k c", p=P)
                    lead = 4
                    for n in range(s["n0"], s["n0"] + lead):
                        load(n, source(n))
                    trips = (2 * s["count"] - lead) // 4
                    with sp.Fori(0, trips) as i:
                        for u in range(4):
                            n = s["n0"] + lead + u
                            c = (s["col0"] + (lead + u) // 2) * P + (u % 2) * DFF
                            load(n, gv[:, :, bass.ds(i * (2 * P) + c, P)], i * 4)
                elif s["kind"] in ("down", "ple", "even_z", "odd_in", "even_in"):
                    count = {"down": KD, "ple": 2 * KD, "even_z": HA + HB, "odd_in": 3 * KD, "even_in": 2 * NA + 1}[s["kind"]]
                    if s["kind"] == "ple":
                        sp.wait_ge(job_done, block_job[s["n0"] - 1] + 1)
                        i = s["i"]
                        sp.dma_start(pstage[:, 0:NTILE - 1, :], ins["p_prompt"][i, 0].rearrange("(t p) d -> p t d", p=P)).then_inc(p_loaded, 16)
                        sp.dma_start(pstage[:, NTILE - 1, :], ins["p_sample"][i].rearrange("b t d -> (b t) d")).then_inc(p_loaded, 16)
                    for n in range(s["n0"] + (4 if s["kind"] == "even_z" else 0), s["n0"] + count):
                        if blocks[n][0][0] is None:
                            sp.wait_ge(lo_ready, n - 3)
                            sp.sem_inc(raw_loaded[n % 4], 16)
                        else:
                            load(n, source(n))
                    if s["kind"] == "even_in":
                        sp.wait_ge(coll_out, 1)
                        sp.dma_start(outs["gdn_conv_p"][0, 0], castout[0:CA, :]).then_inc(out_stored, 16)
                        sp.dma_start(outs["gdn_conv_s"][0].rearrange("b t c -> (b t) c"), castout[CA:CA + DECB * CA, :]).then_inc(out_stored, 16)
                    if s["kind"] == "odd_in":
                        sp.wait_ge(coll_out, 2)
                        sp.dma_start(outs["conv_p"][0, 0], ccout[0:CC, :]).then_inc(out_stored, 16)
                        sp.dma_start(outs["conv_s"][0].rearrange("b t c -> (b t) c"), ccout[CC:CC + DECB * CC, :]).then_inc(out_stored, 16)
                elif s["kind"] == "core":
                    z0 = next(z["n0"] for z in stages if z["kind"] == "even_z")
                    for n in range(z0, z0 + 4):
                        load(n, source(n))
                    sp.wait_ge(m_final, 1)
                    with nc.allow_non_contiguous_dma(reason="a few words"):
                        sp.dma_start(outs["mlstm_m_p"][0].rearrange("b h -> h b"), mfin[:, 0:1]).then_inc(out_stored, 16)
                        sp.dma_start(outs["mlstm_m_s"][0].rearrange("b h -> h b"), mfin[:, 1:]).then_inc(out_stored, 16)
                    sp.wait_ge(ml_dve, len(ML_DVE) * (NTILE - 1))
                    for h in range(HA):
                        sp.dma_start(sg[:, h], ins["state_gdn_S"][0, :, h].rearrange("b k v -> k b v")).then_inc(states_loaded, 16)
                    sp.wait_ge(core["up"], NTILE)
                    sp.dma_start(outs["gdn_S_p"][0, 0].rearrange("h k v -> k h v"), pS[:]).then_inc(states_stored, 16)
                    for h in range(HA):
                        sp.dma_start(outs["gdn_S_s"][0, :, h].rearrange("b k v -> k b v"), sg[:, h]).then_inc(states_stored, 16)
                    sp.wait_ge(states_stored, 16 * (1 + HA))
                    for h in range(HB):
                        sp.dma_start(st[:, h, :, 0:P], ins["state_mlstm_C"][0, :, h].rearrange("b k v -> k b v")).then_inc(states_loaded, 16)
                        with nc.allow_non_contiguous_dma(reason="normalisers as a column"):
                            sp.dma_start(st[:, h, :, P:MW], ins["state_mlstm_n"][0, :, h].rearrange("b (k o) -> k b o", o=1)).then_inc(states_loaded, 16)
                    sp.wait_ge(core["up"], NTILE + 1)
                    sp.dma_start(outs["mlstm_C_p"][0, 0].rearrange("h k v -> k h v"), pC[:, :, 0:P]).then_inc(out_stored, 16)
                    for h in range(HB):
                        sp.dma_start(outs["mlstm_C_s"][0, :, h].rearrange("b k v -> k b v"), st[:, h, :, 0:P]).then_inc(out_stored, 16)
                    sp.wait_ge(states_done, 1)
                    sp.dma_start(outs["mlstm_n_p"][0, 0], nout[0:HB, 0:P]).then_inc(out_stored, 16)
                    sp.dma_start(outs["mlstm_n_s"][0].rearrange("b h k -> b (h k)"), nout[0:DECB, P:]).then_inc(out_stored, 16)
            sp.wait_ge(y_out, KD)
            sp.dma_start(outs["y_p"][0].rearrange("(t p) d -> p t d", p=P), ystage[:, 0:NTILE - 1, :]).then_inc(out_stored, 16)
            sp.dma_start(outs["y_s"].rearrange("b t d -> (b t) d"), ystage[:, NTILE - 1, :]).then_inc(out_stored, 16)
            sp.wait_ge(out_stored, (2 + 2 + 2 + 1 + HB + 2 + 2) * 16)

        @block.gpsimd
        def _(pool):
            own = [0]

            def step(ins_):
                own[0] += 1
                ins_.then_inc(pool_own, 1)
                pool.wait_ge(pool_own, own[0])

            def select(out, pattern, base_, mult, op):
                step(pool.affine_select(out=out, in_=out, compare_op=op, fill=0.0, base=base_, pattern=pattern,
                                        channel_multiplier=mult))

            step(pool.memset(ident[:], 0.0))
            step(pool.affine_select(out=ident[:], in_=ident[:], compare_op=ALU.not_equal, fill=1.0, base=0,
                                    pattern=[[-1, P]], channel_multiplier=1))
            step(pool.memset(one[:], 1.0))
            step(pool.memset(R1[:], 0.0))
            step(pool.memset(incl[:], 1.0))
            for g in range(2):
                select(incl[:, g, :], [[1, P]], 0, -1, ALU.is_ge)
            select(incl[:, 1, :], [[-DECT, DECB], [0, DECT]], 0, 1, ALU.is_ge)
            step(pool.memset(bmask[:], 1.0))
            select(bmask[:], [[-DECT, DECB]], 0, 1, ALU.is_ge)
            select(bmask[:], [[DECT, DECB]], DECT - 1, -1, ALU.is_ge)
            step(pool.memset(level[:], 1.0))
            for l in range(LVL):
                w = 1 << l
                v = level[:, l, :]
                if P // (2 * w) > 1:
                    select(v, [[-2 * w, P // (2 * w)], [0, 2 * w]], 0, 1, ALU.is_ge)
                select(v, [[2 * w, P // (2 * w)], [0, 2 * w]], w - 1, -1, ALU.is_ge)
                step(pool.memset(v.rearrange("p (b w) -> p b w", w=2 * w)[:, :, 0:w], 0.0))
            pool.sem_inc(pool_consts, 1)

            def low(n, kt, off=0, src=None, dst_hi=None, dst=None):
                slot, ws = n % 4, n % 2
                pool.wait_ge(hi_ready, n + 1 + off)
                pool.tensor_tensor(wlo[:, ws, 0:kt, :], raw[:, slot, 0:kt, :], whi[:, ws, 0:kt, :].bitcast(fp32),
                                   ALU.subtract).then_inc(lo_ready, 1)

            n = 0
            while n < NB:
                kt = blocks[n][1]
                if blocks[n][0][0] is None:
                    pool.wait_ge(hi_ready, n + 1)
                    quad = wlo[:, n % 2].rearrange("p k (q c) -> p k q c", q=4)[:, :, :, 0:4]
                    quadh = whi[:, n % 2].rearrange("p k (q c) -> p k q c", q=4)[:, :, :, 0:4].bitcast(fp32)
                    pool.tensor_tensor(quad, wg[:].rearrange("p k (q c) -> p k q c", q=4), quadh,
                                       ALU.subtract).then_inc(lo_ready, 1)
                    n += 1
                    continue
                run = 0
                while n + run < NB and blocks[n + run][1] == kt and blocks[n + run][0][0] is not None:
                    run += 1
                if run >= 8:
                    with pool.Fori(0, run // 4) as i:
                        for u in range(4):
                            low(n + u, kt, i * 4)
                    n += run // 4 * 4
                    run %= 4
                for u in range(run):
                    low(n, kt)
                    n += 1

        @block.tensor
        def _(pe):
            def wait_slot(j, turn=None):
                if j >= 4:
                    pe.wait_ge(slot_free[j % 4], turns(j // 4, turn, 1))

            def mm(n, hi, lo, turn=None, first=None):
                j, kt, ws = block_job[n], blocks[n][1], n % 2
                wait_slot(j, turn)
                pe.wait_ge(lo_ready, turns(n + 1, turn, 4))
                for k in range(kt):
                    if first is not None:
                        pe.wait_ge(first[0], first[1] + k + 1)
                    for c in range(2):
                        cs = slice(c * HT, (c + 1) * HT)
                        pe.matmul(ps[j % 4][:, c, 0:HT], whi[:, ws, k], hi[:, k, cs], start=(k == 0), stop=False)
                        pe.matmul(ps[j % 4][:, c, 0:HT], whi[:, ws, k], lo[:, k, cs], start=False, stop=False)
                    for c in range(2):
                        cs = slice(c * HT, (c + 1) * HT)
                        last = pe.matmul(ps[j % 4][:, c, 0:HT], wlo[:, ws, k], hi[:, k, cs], start=False, stop=(k == kt - 1))
                last.then_inc(job_done, 1)

            def sum_job(j, src):
                wait_slot(j)
                for c in range(2):
                    last = pe.matmul(ps[j % 4][:, c, 0:HT], one[:].to_broadcast([P, P]), src[:, c * HT:(c + 1) * HT],
                                     start=True, stop=True)
                last.then_inc(job_done, 1)

            def norm_job(s):
                pe.wait_ge(xg_ready, 8 * s["prod"] + 8)
                sum_job(s["norm"], sumsq)

            def tposes(j, pieces):
                wait_slot(j)
                for c, col, src in pieces:
                    rows, cols = src.shape
                    last = pe.transpose(ps[j % 4][0:cols, c, col:col + rows], src, ident[0:rows, 0:rows])
                last.then_inc(job_done, 1)

            def tile(t):
                return slice(t * P, (t + 1) * P)

            def spread(b, rows, first_row, t):
                for h in range(HA):
                    c = first_row + h
                    last = pe.matmul(bank(b)[:, h * P:(h + 1) * P], ident[:, c:c + 1].to_broadcast([P, P]), rows[:, tile(t)],
                                     start=True, stop=True)
                return last

            def per_head(b, lhsT, rhs, N=P):
                for h in range(HA):
                    last = pe.matmul(bank(b)[:, h * P:(h + 1) * P], lhsT(h), rhs(h), start=True, stop=True)
                return last

            def delta_tile(t):
                sample = t == NTILE - 1
                L = LVLS if sample else LVL
                q, k = qkv[:, 0:HA, tile(t)], qkv[:, HA:2 * HA, tile(t)]
                li = (LVL - 1) * t
                if t:
                    pe.wait_ge(core["up"], t)
                spread(0, R1, 0, t)
                spread(1, R1, 32, t)
                spread(2, R1, 64, t)
                pe.transpose(bank(3)[:, 0:P], R1[:, tile(t)], ident[:]).then_inc(core["bcast"], 1)
                pe.wait_ge(core["prod"], t + 1)
                per_head(4, lambda h: k[:, h], lambda h: W(0)[:, h])
                per_head(5, lambda h: k[:, h], lambda h: q[:, h]).then_inc(core["np"], 1)
                if not sample:
                    mlstm_part(t, "gates")
                pe.wait_ge(core["kend"], t + 1)
                for h in range(HA):
                    pe.transpose(bank(5)[:, h * P:(h + 1) * P], W(3)[:, h], ident[:])
                pe.wait_ge(core["c0"], t + 1)
                for h in range(HA):
                    last = pe.transpose(bank(4)[:, h * P:(h + 1) * P], W(1)[:, h], ident[:])
                last.then_inc(core["tr"], 1)
                for l in range(1, L):
                    pe.wait_ge(core["ctl"], li + l)
                    if l == 1:
                        pe.wait_ge(core["x0"], t + 1)
                    else:
                        pe.wait_ge(core["xr"], li + l - 1)
                    per_head(0, lambda h: W(1)[:, h], lambda h: W(6)[:, h]).then_inc(core["m1"], 1)
                    if not sample:
                        for part in {1: ["qin"], 2: ["floor"], 3: ["kin"], 4: ["kt"], 5: ["den"], 6: ["up0"]}[l]:
                            mlstm_part(t, part)
                    pe.wait_ge(core["m1c"], li + l)
                    last = per_head(1, lambda h: W(8)[:, h], lambda h: W(7)[:, h])
                    if l < L - 1:
                        last = per_head(2, lambda h: W(7)[:, h], lambda h: W(8)[:, h])
                    last.then_inc(core["d"], 1)
                    if not sample:
                        for part in {1: ["qk"], 2: ["vt"], 4: ["num"]}.get(l, []):
                            mlstm_part(t, part)
                pe.wait_ge(core["xr"], li + L - 1)
                if sample:
                    pe.wait_ge(states_loaded, 16 * HA)
                NBK = DECB if sample else 1
                w = P // NBK

                def state(h, b):
                    return sg[:, h, b, :] if sample else pS[:, h, :]

                for h in range(HA):
                    for b in range(NBK):
                        last = pe.matmul(bank(3)[:, h * P + b * w:h * P + (b + 1) * w], state(h, b), W(0)[:, h, b * w:(b + 1) * w],
                                         start=True, stop=True)
                last.then_inc(core["ks"], 1)
                pe.wait_ge(core["rT"], t + 1)
                for h in range(HA):
                    last = pe.transpose(bank(4)[:, h * P:(h + 1) * P], W(6)[:, h], ident[:])
                last.then_inc(core["rt"], 1)
                pe.wait_ge(core["rtok"], t + 1)
                per_head(5, lambda h: W(7)[:, h], lambda h: W(8)[:, h]).then_inc(core["u"], 1)
                pe.wait_ge(core["utok"], t + 1)
                for h in range(HA):
                    pe.matmul(bank(2)[:, h * P:(h + 1) * P], W(1)[:, h], W(5)[:, h], start=True, stop=False)
                    for b in range(NBK):
                        last = pe.matmul(bank(2)[:, h * P + b * w:h * P + (b + 1) * w], state(h, b), q[:, h, b * w:(b + 1) * w],
                                         start=False, stop=(b == NBK - 1))
                if sample:
                    last.then_inc(core["o"], 1)
                    for h in range(HA):
                        pe.wait_ge(core["uexp"], h + 1)
                        for c in range(2):
                            last = pe.matmul(ps[h % 2][:, c, :], W(3)[:, h], uexp(P)[:, c * 4:(c + 1) * 4, :], start=True, stop=True)
                        last.then_inc(core["sup"], 1)
                else:
                    per_head(3, lambda h: W(3)[:, h], lambda h: W(1)[:, h]).then_inc(core["o"], 1)
                    mlstm_part(t, "up1")

            def mlstm_part(t, part):
                q, k, v = (qkv[:, a:a + HB, tile(t)] for a in (8, 12, 20))

                def state_update(b, h0):
                    for h in (h0, h0 + 1):
                        last = pe.matmul(bank(b)[:, (h - h0) * MW:(h - h0 + 1) * MW], V(6)[:, h], V8[:, 5, h * MW:(h + 1) * MW],
                                         start=True, stop=True)
                    return last

                if part == "gates":
                    if t:
                        pe.wait_ge(ml_dve, ml(ML_DVE, t - 1, "up1"))
                    spread(6, R2, 0, t)
                    last = pe.transpose(bank(7)[:, 0:P], R1[:, tile(t)], ident[:])
                elif part in ("qin", "floor", "kin"):
                    if part == "qin":
                        pe.wait_ge(ml_dve, ml(ML_DVE, t, "gates"))
                    else:
                        pe.wait_ge(ml_act, ml(ML_ACT, t, "qin" if part == "floor" else "floor"))
                    last = spread(7, R2, {"qin": 32, "floor": 64, "kin": 96}[part], t)
                elif part == "qk":
                    last = per_head(6, lambda h: k[:, h], lambda h: q[:, h])
                elif part == "vt":
                    pe.wait_ge(ml_dve, ml(ML_DVE, t, "qk"))
                    for h in range(HB):
                        last = pe.transpose(bank(6)[:, h * P:(h + 1) * P], v[:, h], ident[:])
                elif part == "kt":
                    pe.wait_ge(ml_dve, ml(ML_DVE, t, "k"))
                    for h in range(HB):
                        last = pe.transpose(bank(6)[:, h * P:(h + 1) * P], V(4)[:, h], ident[:])
                elif part == "num":
                    for h in range(HB):
                        pe.matmul(bank(7)[:, h * P:(h + 1) * P], V8[:, 5, h * MW:h * MW + P], V(3)[:, h], start=True, stop=False)
                        last = pe.matmul(bank(7)[:, h * P:(h + 1) * P], pC[:, h, 0:P], q[:, h], start=False, stop=True)
                elif part == "den":
                    pe.wait_ge(ml_act, ml(ML_ACT, t, "kt"))
                    for h in range(HB):
                        pe.matmul(bank(6)[:, h * P:(h + 1) * P], one[:].to_broadcast([P, P]), V(3)[:, h], start=True, stop=False)
                        last = pe.matmul(bank(6)[:, h * P:(h + 1) * P], pC[:, h, P:MW].to_broadcast([P, P]), q[:, h],
                                         start=False, stop=True)
                elif part == "up0":
                    pe.wait_ge(ml_act, ml(ML_ACT, t, "den"))
                    last = state_update(6, 0)
                else:
                    pe.wait_ge(ml_dve, ml(ML_DVE, t, "out"))
                    last = state_update(7, 2)
                last.then_inc(ml_pe, 1)

            def mlstm_sample():
                t = NTILE - 1
                q, k, v = (qkv[:, a:a + HB, tile(t)] for a in (8, 12, 20))
                pe.wait_ge(core["up"], NTILE)
                spread(0, R2, 0, t)
                spread(1, R2, 32, t)
                spread(2, R2, 64, t)
                spread(3, R2, 96, t)
                pe.transpose(bank(4)[:, 0:P], R1[:, tile(t)], ident[:])
                per_head(5, lambda h: k[:, h], lambda h: q[:, h])
                for h in range(HB):
                    last = pe.transpose(bank(6)[:, h * P:(h + 1) * P], v[:, h], ident[:])
                last.then_inc(core["bcast"], 1)
                pe.wait_ge(core["kend"], NTILE + 1)
                for h in range(HB):
                    last = pe.transpose(bank(0)[:, h * P:(h + 1) * P], W(4)[:, h], ident[:])
                last.then_inc(core["tr"], 1)
                pe.wait_ge(states_loaded, 16 * (HA + 2 * HB))
                w = DECT
                pe.wait_ge(core["vt"], 1)
                for h in range(HB):
                    hs = h * P
                    pe.matmul(bank(1)[:, hs:hs + P], W9[:, 5, h * MW:h * MW + P], W(3)[:, h], start=True, stop=False)
                    for b in range(DECB):
                        pe.matmul(bank(1)[:, hs + b * w:hs + (b + 1) * w], st[:, h, b, 0:P], q[:, h, b * w:(b + 1) * w],
                                  start=False, stop=(b == DECB - 1))
                    pe.matmul(bank(2)[:, hs:hs + P], one[:].to_broadcast([P, P]), W(3)[:, h], start=True, stop=False)
                    for b in range(DECB):
                        last = pe.matmul(bank(2)[:, hs + b * w:hs + (b + 1) * w], st[:, h, b, P:MW].to_broadcast([P, P]),
                                         q[:, h, b * w:(b + 1) * w], start=False, stop=(b == DECB - 1))
                last.then_inc(core["np"], 1)
                pe.wait_ge(core["ktok"], 1)
                for h in range(HB):
                    pe.wait_ge(core["uexp"], HA + h + 1)
                    for c, (a, b) in enumerate([(0, 3), (3, 6), (6, 8)]):
                        last = pe.matmul(bank(3 + c)[:, 0:(b - a) * MW], W(6)[:, h], uexp(MW)[:, a:b, :], start=True, stop=True)
                    last.then_inc(core["sup"], 1)

            pe.wait_ge(pool_consts, 1)
            for s in stages:
                kind = s["kind"]
                if kind == "load":
                    pe.wait_ge(in_loaded[1], 6 * 16)
                    tposes(s["vec"], [(0, 0, vstage[0:NV1, 0, :]), (1, 0, vstage[0:NV2, 1, :])])
                    pe.wait_ge(in_loaded[2], 2 * 16)
                    tposes(s["cs"], [(0, b * DECB * CA, castage[0:DECB * CA, b * P:(b + 1) * P]) for b in range(NA)] +
                           [(1, b * DECB * CC, ccstage[0:DECB * CC, b * P:(b + 1) * P]) for b in range(KD)])
                    pe.wait_ge(in_loaded[0], 2 * 16)
                    for q, j in enumerate(s["x"]):
                        tposes(j, [(t // 4, t % 4 * P, xstage[:, t, q * P:(q + 1) * P]) for t in range(NTILE)])
                elif kind == "gu":
                    n0, count, lead = s["n0"], 2 * s["count"], 4
                    for u in range(lead):
                        mm(n0 + u, xh, xl, first=(xg_ready, 8 * s["prod"]) if u == 0 and s["first"] else None)
                        if u == 0 and s["norm"] is not None:
                            norm_job(s)
                    with pe.Fori(0, (count - lead) // 4) as i:
                        for u in range(4):
                            mm(n0 + lead + u, xh, xl, turn=i)
                elif kind == "down":
                    for o in range(KD):
                        mm(s["n0"] + o, hh, hl, first=(h_ready, s["hbase"]) if o == 0 else None)
                elif kind == "even_in":
                    n = s["n0"]
                    for b in range(NA):
                        mm(n + b, xh, xl, first=(xg_ready, 8 * s["prod"]) if b == 0 else None)
                        if b == 0:
                            norm_job(s)
                    pe.wait_ge(coll_ready, 1)
                    for j, first, last in ((s["coll"][0], 0, 8), (s["coll"][1], 8, NA)):
                        tposes(j, [((b - first) // 4, b % 4 * P, cacoll[:, b, :]) for b in range(first, last)])
                    mm(n + NA, xh, xl)
                    for b in range(NA):
                        mm(n + NA + 1 + b, xh, xl)
                        if b >= HN_LAG:
                            q = b - HN_LAG
                            pe.wait_ge(hn_sq, s["hn0"] + q + 1)
                            sum_job(s["l2"][q], [sq, ut][q % 2])
                elif kind == "core":
                    for c in range(4):
                        pe.wait_ge(slot_free[c], (core_jobs + 3 - c) // 4)
                    pe.wait_ge(rows_ready, 1)
                    for t in range(NTILE):
                        delta_tile(t)
                    mlstm_sample()
                    pe.wait_ge(core["up"], NTILE + 1)
                    pe.transpose(bank(0)[0:HB, 0:P], pC[:, :, P], ident[:])
                    for h in range(HB):
                        last = pe.transpose(bank(1)[0:DECB, h * P:(h + 1) * P], st[:, h, :, P], ident[:])
                    last.then_inc(core["tr"], 1)
                elif kind == "even_z":
                    pe.wait_ge(states_done, 1)
                    for q, j in enumerate(s["onorm"]):
                        pe.wait_ge(hn_sq, s["hn0"] + q + 1)
                        sum_job(j, [sq, ut][q % 2])
                        mm(s["n0"] + q, xh, xl)
                elif kind == "ple":
                    mm(s["n0"], xh, xl, first=(xg_ready, 8 * s["prod"]))
                    norm_job(s)
                    pe.wait_ge(p_loaded, 32 * (s["i"] + 1))
                    for q, j in enumerate(s["pT"]):
                        tposes(j, [(t // 4, t % 4 * P, pstage[:, t, q * P:(q + 1) * P]) for t in range(NTILE)])
                    for o in range(1, KD):
                        mm(s["n0"] + o, xh, xl)
                    pe.wait_ge(h_ready, s["hbase"] + KP)
                    for o in range(KD):
                        mm(s["n0"] + KD + o, hh, hl[:, 6:8, :])
                elif kind == "odd_in":
                    n = s["n0"]
                    for b in range(2 * KD):
                        mm(n + b, xh, xl, first=(xg_ready, 8 * s["prod"]) if b == 0 else None)
                        if b == 0:
                            norm_job(s)
                    pe.wait_ge(coll_ready, 2)
                    tposes(s["coll"][0], [(b // 4, b % 4 * P, cccoll[:, b, :]) for b in range(KD)])
                    for b in range(KD):
                        mm(n + 2 * KD + b, xh, xl)
                elif kind == "final":
                    norm_job(s)
                    for q, j in enumerate(s["y"]):
                        pe.wait_ge(y_in, q + 1)
                        tposes(j, [(t // 4, t % 4 * P, [gt, ut][q % 2][:, t * P:(t + 1) * P]) for t in range(NTILE)])

        @block.scalar
        def _(act):
            own = Tally(act)

            def prep(n, turn=None):
                if n >= NB:
                    return
                kt = blocks[n][1]
                act.wait_ge(raw_loaded[n % 4], turns(16 * (n // 4 + 1), turn, 16))
                if n >= 2:
                    act.wait_ge(job_done, turns(block_job[n - 2] + 1, turn, 4))
                if blocks[n][0][0] is None:
                    act.wait_ge(in_loaded[4], 2 * 16)
                    act.copy(whi[:, n % 2].rearrange("p k (q c) -> p k q c", q=4)[:, :, :, 0:4],
                             wg[:].rearrange("p k (q c) -> p k q c", q=4)).then_inc(hi_ready, 1)
                else:
                    act.copy(whi[:, n % 2, 0:kt, :], raw[:, n % 4, 0:kt, :]).then_inc(hi_ready, 1)

            def produce(p, j, g):
                act.wait_ge(x_new, 8 * p + j + 1)
                act.activation([sq, stt][j % 2][:], x[:, j, :], ACT.Square).then_inc(sq_ready, 1)
                if g is not None:
                    act.activation(xh[:, j, :], x[:, j, :], ACT.Copy, scale=vec1[:, g + j:g + j + 1]).then_inc(xg_hi, 1)

            def norm_root(s):
                j = s["norm"]
                act.wait_ge(job_done, j + 1)
                own(act.activation(halves(r[:]), ps[j % 4][:, :, 0:HT], ACT.Sqrt, scale=1.0 / D, bias=eps[:]).then_inc(root_ready, 1), root_ready)
                act.sem_inc(slot_free[j % 4], 1)

            def head_squares(s, q, jobs_, piece):
                if q >= 2:
                    act.wait_ge(job_done, jobs_[q - 2] + 1)
                act.activation([sq, ut][q % 2][:], piece, ACT.Square).then_inc(hn_sq, 1)

            def head_root(s, q, j, scale):
                act.wait_ge(job_done, j + 1)
                if q >= 1:
                    act.wait_ge(hn_used, s["hn0"] + q)
                own(act.activation(halves(root[:]), ps[j % 4][:, :, 0:HT], ACT.Sqrt, scale=scale, bias=eps[:]).then_inc(hn_root, 1), hn_root)
                act.sem_inc(slot_free[j % 4], 1)

            def mlstm_part(t, part):
                if part == "gates":
                    act.wait_ge(ml_dve, ml(ML_DVE, t, "gates"))
                else:
                    act.wait_ge(ml_pe, ml(ML_PE, t, part))
                if part == "gates":
                    last = act.activation(V(0), V(0), ACT.Exp)
                elif part in ("qin", "floor", "kin"):
                    last = act.activation(V({"qin": 1, "floor": 2, "kin": 4}[part]), heads(7), ACT.Exp)
                elif part == "vt":
                    last = act.copy(V8[:, 5, :].rearrange("p (h c) -> p h c", h=HB)[:, :, 0:P], heads(6))
                elif part == "kt":
                    last = act.copy(V(6), heads(6))
                else:
                    last = act.activation(V(7), heads(6), ACT.Abs)
                last.then_inc(ml_act, 1)

            prep(0)
            prep(1)
            act.wait_ge(pool_consts, 1)
            for s in stages:
                kind = s["kind"]
                if kind == "load":
                    for q in range(KD):
                        produce(0, q, 0)
                elif kind == "gu":
                    n0, count, lead = s["n0"], 2 * s["count"], 4

                    def step(u, turn=None):
                        prep(n0 + u + 2, turn)
                        if u == 0 and s["norm"] is not None:
                            norm_root(s)
                        if u % 2 == 0:
                            act.wait_ge(gate_in, turns(s["act0"] + u // 2 + 1, turn, 2))
                            act.activation(stt[:], gt[:], ACT.Silu).then_inc(act_out, 1)

                    for u in range(lead):
                        step(u)
                    trips = (count - lead - 2) // 4
                    with act.Fori(0, trips) as i:
                        for u in range(4):
                            step(lead + u, i)
                    for u in range(lead + 4 * trips, count):
                        step(u)
                elif kind == "down":
                    for o in range(KD):
                        prep(s["n0"] + o + 2)
                        if s["last"]:
                            produce(s["prod"], o, s["g"])
                elif kind == "even_in":
                    n = s["n0"]
                    for b in range(NA):
                        prep(n + b + 2)
                        if b == 0:
                            norm_root(s)
                        act.wait_ge(conv_in, b + 1)
                        pos = s["pos"][b]
                        act.activation(qkv[:, pos, 0:SEQ], ct[:, 0:SEQ], ACT.Silu)
                        act.activation(qkv[:, pos, SEQ:T].rearrange("p (b t) -> p b t", t=DECT),
                                       ct[:, SEQ + CA:HISTA].rearrange("p (b t) -> p b t", t=DECT + CA)[:, :, 0:DECT],
                                       ACT.Silu).then_inc(conv_out, 1)
                    prep(n + NA + 2)
                    act.wait_ge(row_in, 1)
                    own(act.activation(R1[0:4, :], R1[0:4, :], ACT.Sigmoid).then_inc(act_own, 1), act_own)
                    own(act.activation(small[0:4, 4:5], small[0:4, 0:1], ACT.Exp).then_inc(act_own, 1), act_own)
                    for src, t1, t2, bias, sgn in ((dt_, hf_, sq_, small[0:4, 1:2], 1.0), (fg_, hi_, ct_, small[0:4, 5:6], -1.0)):
                        a, b_, c = src[0:4, 0:T], t1[0:4, 0:T], t2[0:4, 0:T]
                        own(act.activation(b_, a, ACT.Abs, bias=bias, scale=sgn).then_inc(act_own, 1), act_own)
                        own(act.activation(b_, b_, ACT.Exp, scale=-1.0).then_inc(act_own, 1), act_own)
                        own(act.activation(b_, b_, ACT.Ln, bias=1.0).then_inc(act_own, 1), act_own)
                        own(act.activation(c, a, ACT.Relu, bias=bias, scale=sgn).then_inc(row_act, 1), row_act)
                    for b in range(NA):
                        q = b - HN_LAG
                        if q >= 0:
                            if q == 0:
                                act.wait_ge(conv_out, NA)
                            head_squares(s, q, s["l2"], qkv[:, q, :])
                        prep(n + NA + 1 + b + 2)
                        if q >= 0:
                            head_root(s, q, s["l2"][q], 1.0)
                elif kind == "core":
                    for t in range(NTILE):
                        L = LVLS if t == NTILE - 1 else LVL
                        li = (LVL - 1) * t
                        act.wait_ge(core["expin"], t + 1)
                        act.activation(W(1), W(1), ACT.Exp).then_inc(core["gam"], 1)
                        act.activation(W(2), heads(1), ACT.Exp)
                        act.activation(W(3), heads(2), ACT.Exp).then_inc(core["eg"], 1)
                        if t < NTILE - 1:
                            mlstm_part(t, "gates")
                        for l in range(1, L):
                            act.wait_ge(core["m1"], li + l)
                            act.copy(W(8), heads(0)).then_inc(core["m1c"], 1)
                            if t < NTILE - 1:
                                for part in {1: ["qin"], 2: ["floor"], 3: ["vt", "kin"], 4: ["kt"], 5: ["den"]}.get(l, []):
                                    mlstm_part(t, part)
                        act.wait_ge(core["rt"], t + 1)
                        act.copy(W(8), heads(4)).then_inc(core["rtok"], 1)
                        act.wait_ge(core["u"], t + 1)
                        act.copy(W(1), heads(5)).then_inc(core["utok"], 1)
                    g = NTILE
                    act.wait_ge(core["bcast"], g + 1)
                    act.copy(W9[:, 5, :].rearrange("p (h c) -> p h c", h=HB)[:, :, 0:P], heads(6)).then_inc(core["vt"], 1)
                    act.wait_ge(core["expin"], g + 1)
                    act.activation(W(0), W(0), ACT.Exp).then_inc(core["gam"], 1)
                    act.activation(W(1), heads(1), ACT.Exp)
                    act.activation(W(2), heads(2), ACT.Exp)
                    act.activation(W(4), heads(3), ACT.Exp).then_inc(core["eg"], 1)
                    act.wait_ge(core["tr"], g + 1)
                    act.copy(W(6), heads(0)).then_inc(core["ktok"], 1)
                elif kind == "even_z":
                    act.wait_ge(states_done, 1)
                    head_squares(s, 0, s["onorm"], qkv[:, 16, :])
                    for q in range(HA + HB):
                        if q + 1 < HA + HB:
                            head_squares(s, q + 1, s["onorm"], qkv[:, 17 + q, :])
                        head_root(s, q, s["onorm"][q], 1.0 / P)
                        prep(s["n0"] + q + 2)
                        act.wait_ge(gate_in, s["act0"] + q + 1)
                        act.activation(stt[:], gt[:], ACT.Silu if q < HA else ACT.Sigmoid).then_inc(act_out, 1)
                elif kind == "ple":
                    for o in range(KD):
                        prep(s["n0"] + o + 2)
                        if o == 0:
                            norm_root(s)
                        act.wait_ge(gate_in, s["act0"] + o + 1)
                        act.activation(sig[:, o, :], gt[:], ACT.Sigmoid).then_inc(act_out, 1)
                        if o == 0:
                            pass
                    for o in range(KD):
                        prep(s["n0"] + KD + o + 2)
                        produce(s["next"], o, s["g"] if s["i"] + 1 < DEPTH else None)
                elif kind == "odd_in":
                    for b in range(3 * KD):
                        prep(s["n0"] + b + 2)
                        if b == 0:
                            norm_root(s)
                elif kind == "final":
                    norm_root(s)

        @block.vector
        def _(dve):
            own = Tally(dve)

            def o1(i):
                own(i.then_inc(dve_own, 1), dve_own)

            def mul(out, a, b):
                o1(dve.tensor_tensor(out, a, b, ALU.mult))

            def free(j):
                dve.sem_inc(slot_free[j % 4], 1)

            def P2(j):
                return ps[j % 4][:, :, 0:HT]

            def done(j, turn=None):
                dve.wait_ge(job_done, turns(j + 1, turn, 4))

            def produce(p, j, g):
                dve.wait_ge(sq_ready, 8 * p + j + 1)
                src = [sq, stt][j % 2][:]
                if j == 0:
                    o1(dve.tensor_copy(sumsq[:], src))
                elif g is None:
                    own(dve.tensor_tensor(sumsq[:], sumsq[:], src, ALU.add).then_inc(xg_ready, 1), xg_ready)
                else:
                    o1(dve.tensor_tensor(sumsq[:], sumsq[:], src, ALU.add))
                if g is None:
                    if j == 0:
                        dve.sem_inc(xg_ready, 1)
                        own.counts[xg_ready.name] += 1
                    return
                dve.wait_ge(xg_hi, 8 * p + j + 1)
                own(dve.scalar_tensor_tensor(xl[:, j, :], x[:, j, :], vec1[:, g + j:g + j + 1], xh[:, j, :].bitcast(fp32),
                                             ALU.mult, ALU.subtract).then_inc(xg_ready, 1), xg_ready)

            def norm_recip(s):
                dve.wait_ge(root_ready, own_norms[0] + 1)
                own_norms[0] += 1
                o1(dve.reciprocal(r[:], r[:]))

            own_norms = [0]

            def split_hidden(slot, turn=None, step=None):
                mul(hf[:], stt[:], ut[:])
                at_ = slice(slot, slot + 1) if turn is None else bass.ds(turn * step + slot, 1)
                o1(dve.tensor_tensor(hh[:, at_, :], stt[:].unsqueeze(1), ut[:].unsqueeze(1), ALU.mult))
                own(dve.tensor_tensor(hl[:, at_, :], hf[:].unsqueeze(1), hh[:, at_, :].bitcast(fp32), ALU.subtract).then_inc(h_ready, 1), h_ready)

            def head_norm(s, q, piece, scalar):
                dve.wait_ge(hn_root, s["hn0"] + q + 1)
                o1(dve.reciprocal(inv[:], root[:]))
                own(dve.scalar_tensor_tensor(piece, piece, scalar, inv[:], ALU.mult, ALU.mult).then_inc(hn_used, 1), hn_used)

            def y_evac(q, j):
                done(j)
                o1(dve.tensor_copy(ystage[:, 0:4, q * P:(q + 1) * P], ps[j % 4][:, 0, :].rearrange("p (t c) -> p t c", c=P)))
                own(dve.tensor_copy(ystage[:, 4, q * P:(q + 1) * P], ps[j % 4][:, 1, 0:P]).then_inc(y_out, 1), y_out)
                free(j)

            def delta_tile(t):
                sample = t == NTILE - 1
                L = LVLS if sample else LVL
                li = (LVL - 1) * t
                z = slice(t * P, (t + 1) * P)
                q, k, v = (qkv[:, a:a + HA, z] for a in (0, 4, 16))
                over_heads = lambda m: m.unsqueeze(1).to_broadcast([P, HA, P])
                dve.wait_ge(core["bcast"], t + 1)
                o1(dve.tensor_copy(gcol[:, 0:4], bank(3)[:, 32:36]))
                own(dve.tensor_tensor(W(0), k, heads(0), ALU.mult).then_inc(core["prod"], 1), core["prod"])
                for h in range(HA):
                    sm = core["expin"] if h == HA - 1 else dve_own
                    own(dve.tensor_scalar(W(1)[:, h], heads(1)[:, h], gcol[:, h:h + 1], 0.0, ALU.subtract, ALU.min).then_inc(sm, 1), sm)
                mul(v, v, heads(0))
                dve.wait_ge(core["gam"], t + 1)
                mul(W(1), W(1), over_heads(incl[:, 1 if sample else 0, :]))
                dve.wait_ge(core["np"], t + 1)
                mul(W(4), heads(4), W(1))
                mul(W(5), heads(5), W(1))
                dve.wait_ge(core["eg"], t + 1)
                own(dve.tensor_tensor(W(3), W(3), k, ALU.mult).then_inc(core["kend"], 1), core["kend"])
                own(dve.tensor_tensor(W(1), W(4), over_heads(level[:, 0, :]), ALU.mult).then_inc(core["c0"], 1), core["c0"])
                o1(dve.tensor_tensor(W(7), over_heads(ident[:]), W(1), ALU.subtract))
                mul(W(0), W(0), W(2))
                mul(q, q, W(2))
                if not sample:
                    mlstm_part(t, "gates")
                dve.wait_ge(core["tr"], t + 1)
                own(dve.tensor_tensor(W(6), over_heads(ident[:]), heads(4), ALU.subtract).then_inc(core["x0"], 1), core["x0"])

                def masked(l):
                    own(dve.tensor_tensor(W(1), W(4), over_heads(level[:, l, :]), ALU.mult).then_inc(core["ctl"], 1), core["ctl"])

                masked(1)
                o1(dve.tensor_copy(W(3), heads(5)))
                for l in range(1, L):
                    if l < L - 1:
                        dve.wait_ge(core["m1c"], li + l)
                        masked(l + 1)
                    dve.wait_ge(core["d"], li + l)
                    if l < L - 1:
                        o1(dve.tensor_tensor(W(7), W(7), heads(1), ALU.subtract))
                        own(dve.tensor_tensor(W(6), W(6), heads(2), ALU.subtract).then_inc(core["xr"], 1), core["xr"])
                    else:
                        own(dve.tensor_tensor(W(7), W(7), heads(1), ALU.subtract).then_inc(core["xr"], 1), core["xr"])
                    if not sample:
                        for part in {1: ["qk"], 2: ["q"], 3: ["k"]}.get(l, []):
                            mlstm_part(t, part)
                dve.wait_ge(core["ks"], t + 1)
                own(dve.tensor_tensor(W(6), v, heads(3), ALU.subtract).then_inc(core["rT"], 1), core["rT"])
                if not sample:
                    mlstm_part(t, "out")
                    mlstm_part(t, "up0")
                dve.wait_ge(core["o"], t + 1)
                o1(dve.tensor_copy(v, heads(2)))
                for h in range(HA):
                    sm = core["up"] if h == HA - 1 else dve_own
                    if not sample:
                        own(dve.scalar_tensor_tensor(pS[:, h], pS[:, h], W(2)[:, h, P - 1:P], heads(3)[:, h], ALU.mult, ALU.add).then_inc(sm, 1), sm)
                        continue
                    own(dve.tensor_tensor(uexp(P), W(1)[:, h].unsqueeze(1).to_broadcast([P, DECB, P]),
                                          bmask[:].unsqueeze(2).to_broadcast([P, DECB, P]), ALU.mult).then_inc(core["uexp"], 1), core["uexp"])
                    ends = W(2)[:, h].rearrange("p (b t) -> p b t", t=DECT)[:, :, DECT - 1:DECT].to_broadcast([P, DECB, P])
                    mul(sg[:, h], sg[:, h], ends)
                    dve.wait_ge(core["sup"], h + 1)
                    for c in range(2):
                        sc = sm if c else dve_own
                        own(dve.tensor_tensor(sg[:, h, 4 * c:4 * c + 4], sg[:, h, 4 * c:4 * c + 4],
                                              ps[h % 2][:, c, :].rearrange("p (b v) -> p b v", v=P), ALU.add).then_inc(sc, 1), sc)
                if not sample:
                    mlstm_part(t, "up1")

            def mlstm_part(t, part):
                z = slice(t * P, (t + 1) * P)
                q, k, v = (qkv[:, a:a + HB, z] for a in (8, 12, 20))
                scale = float(DK) ** -0.5
                if part == "gates":
                    dve.wait_ge(ml_pe, ml(ML_PE, t, "gates"))
                    o1(dve.tensor_copy(gcol[:, 4:8], bank(7)[:, 96:100]))
                    for h in range(HB):
                        sm = ml_dve if h == HB - 1 else dve_own
                        own(dve.tensor_scalar(V(0)[:, h], heads(6)[:, h], gcol[:, 4 + h:5 + h], 0.0, ALU.add, ALU.min).then_inc(sm, 1), sm)
                elif part == "qk":
                    dve.wait_ge(ml_act, ml(ML_ACT, t, "gates"))
                    mul(V(0), V(0), incl[:, 0, :].unsqueeze(1).to_broadcast([P, HB, P]))
                    dve.wait_ge(ml_pe, ml(ML_PE, t, "qk"))
                    own(dve.scalar_tensor_tensor(V(3), heads(6), scale, V(0), ALU.mult, ALU.mult).then_inc(ml_dve, 1), ml_dve)
                elif part == "q":
                    dve.wait_ge(ml_act, ml(ML_ACT, t, "qin"))
                    o1(dve.memset(V8[:, 5, :].rearrange("p (h c) -> p h c", h=HB)[:, :, P:MW], 1.0))
                    own(dve.scalar_tensor_tensor(q, q, scale, V(1), ALU.mult, ALU.mult).then_inc(ml_dve, 1), ml_dve)
                elif part == "k":
                    dve.wait_ge(ml_act, ml(ML_ACT, t, "kin"))
                    own(dve.tensor_tensor(V(4), V(4), k, ALU.mult).then_inc(ml_dve, 1), ml_dve)
                elif part == "out":
                    dve.wait_ge(ml_act, ml(ML_ACT, t, "den"))
                    o1(dve.tensor_tensor(V(7), V(7), V(2), ALU.max))
                    o1(dve.reciprocal(V(7), V(7)))
                    own(dve.tensor_tensor(v, heads(7), V(7), ALU.mult).then_inc(ml_dve, 1), ml_dve)
                else:
                    dve.wait_ge(ml_pe, ml(ML_PE, t, part))
                    b, h0 = (6, 0) if part == "up0" else (7, 2)
                    for h in (h0, h0 + 1):
                        sm = dve_own if h == h0 else ml_dve
                        own(dve.scalar_tensor_tensor(pC[:, h], pC[:, h], V(1)[:, h, P - 1:P], bank(b)[:, (h - h0) * MW:(h - h0 + 1) * MW],
                                                     ALU.mult, ALU.add).then_inc(sm, 1), sm)

            def mlstm_sample():
                z = slice(SEQ, T)
                q, k, v = (qkv[:, a:a + HB, z] for a in (8, 12, 20))
                scale = float(DK) ** -0.5
                dve.wait_ge(core["bcast"], NTILE + 1)
                o1(dve.tensor_copy(gcol[:, 4:8], bank(4)[:, 96:100]))
                for h in range(HB):
                    sm = core["expin"] if h == HB - 1 else dve_own
                    own(dve.tensor_scalar(W(0)[:, h], heads(0)[:, h], gcol[:, 4 + h:5 + h], 0.0, ALU.add, ALU.min).then_inc(sm, 1), sm)
                dve.wait_ge(core["gam"], NTILE + 1)
                mul(W(0), W(0), incl[:, 1, :].unsqueeze(1).to_broadcast([P, HB, P]))
                o1(dve.scalar_tensor_tensor(W(3), heads(5), scale, W(0), ALU.mult, ALU.mult))
                dve.wait_ge(core["eg"], NTILE + 1)
                o1(dve.scalar_tensor_tensor(q, q, scale, W(1), ALU.mult, ALU.mult))
                o1(dve.memset(W9[:, 5, :].rearrange("p (h c) -> p h c", h=HB)[:, :, P:MW], 1.0))
                own(dve.tensor_tensor(W(4), W(4), k, ALU.mult).then_inc(core["kend"], 1), core["kend"])
                dve.wait_ge(core["np"], NTILE + 1)
                o1(dve.tensor_scalar(W(7), heads(2), -1.0, None, ALU.mult))
                o1(dve.tensor_tensor(W(7), W(7), heads(2), ALU.max))
                o1(dve.tensor_tensor(W(7), W(7), W(2), ALU.max))
                o1(dve.reciprocal(W(7), W(7)))
                mul(v, heads(1), W(7))
                for h in range(HB):
                    sm = core["up"] if h == HB - 1 else dve_own
                    own(dve.tensor_tensor(uexp(MW), W9[:, 5, h * MW:(h + 1) * MW].unsqueeze(1).to_broadcast([P, DECB, MW]),
                                          bmask[:].unsqueeze(2).to_broadcast([P, DECB, MW]), ALU.mult).then_inc(core["uexp"], 1), core["uexp"])
                    ends = W(1)[:, h].rearrange("p (b t) -> p b t", t=DECT)[:, :, DECT - 1:DECT].to_broadcast([P, DECB, MW])
                    mul(st[:, h], st[:, h], ends)
                    dve.wait_ge(core["sup"], HA + h + 1)
                    for c, (a, b) in enumerate([(0, 3), (3, 6), (6, 8)]):
                        sc = sm if c == 2 else dve_own
                        own(dve.tensor_tensor(st[:, h, a:b], st[:, h, a:b],
                                              bank(3 + c)[:, 0:(b - a) * MW].rearrange("p (b v) -> p b v", v=MW), ALU.add).then_inc(sc, 1), sc)

            o1(dve.memset(eps[:], EPS))
            o1(dve.memset(pS[:], 0.0))
            o1(dve.memset(pC[:], 0.0))
            for s in stages:
                kind = s["kind"]
                if kind == "load":
                    j = s["vec"]
                    done(j)
                    o1(dve.tensor_copy(vec1[:], ps[j % 4][:, 0, 0:NV1]))
                    o1(dve.tensor_copy(vec2[:], ps[j % 4][:, 1, 0:NV2]))
                    free(j)
                    j = s["cs"]
                    done(j)
                    o1(dve.tensor_copy(castate[:].rearrange("p a b -> p (a b)"), ps[j % 4][:, 0, 0:NA * DECB * CA]))
                    o1(dve.tensor_copy(ccstate[:].rearrange("p a b -> p (a b)"), ps[j % 4][:, 1, 0:KD * DECB * CC]))
                    free(j)
                    for q, j in enumerate(s["x"]):
                        done(j)
                        o1(dve.tensor_copy(x[:, q, 0:SEQ], ps[j % 4][:, 0, :]))
                        own(dve.tensor_copy(x[:, q, SEQ:T], ps[j % 4][:, 1, 0:P]).then_inc(x_new, 1), x_new)
                        free(j)
                        produce(0, q, 0)
                elif kind == "gu":
                    n0, lead = s["n0"], 4

                    def pair(q, turn=None):
                        ja, jb = block_job[n0 + 2 * q], block_job[n0 + 2 * q + 1]
                        if q == 0 and s["norm"] is not None:
                            norm_recip(s)
                        done(ja, turn)
                        own(dve.tensor_tensor(halves(gt[:]), P2(ja), halves(r[:]), ALU.mult).then_inc(gate_in, 1), gate_in)
                        free(ja)
                        done(jb, turn)
                        mul(halves(ut[:]), P2(jb), halves(r[:]))
                        free(jb)
                        dve.wait_ge(act_out, turns(s["act0"] + q + 1, turn, 2))
                        split_hidden(q, turn, 2)

                    pair(0)
                    pair(1)
                    trips = (s["count"] - 2) // 2
                    with dve.Fori(0, trips) as i:
                        own.enter(i, {gate_in: 2, dve_own: 6, h_ready: 2})
                        pair(2, i)
                        pair(3, i)
                    own.leave(trips)
                elif kind == "down":
                    for o in range(KD):
                        j = block_job[s["n0"] + o]
                        done(j)
                        sm = x_new if s["last"] else dve_own
                        own(dve.scalar_tensor_tensor(halves(x[:, o, :]), P2(j), s["scale"], halves(x[:, o, :]),
                                                     ALU.mult, ALU.add).then_inc(sm, 1), sm)
                        free(j)
                        if s["last"]:
                            produce(s["prod"], o, s["g"])
                elif kind == "even_in":
                    n = s["n0"]
                    NR = CA + DECB * CA
                    hs = hist[:, SEQ + CA:HISTA].rearrange("p (b t) -> p b t", t=DECT + CA)
                    o1(dve.memset(hist[:, 0:CA], 0.0))
                    for b in range(NA):
                        j = block_job[n + b]
                        if b == 0:
                            norm_recip(s)
                        done(j)
                        p_ = ps[j % 4]
                        mul(hist[:, CA:CA + HT], p_[:, 0, 0:HT], r[:, 0:HT])
                        mul(hist[:, CA + HT:CA + SEQ], p_[:, 1, 0:SEQ - HT], r[:, HT:SEQ])
                        mul(hs[:, :, CA:], p_[:, 1, SEQ - HT:HT].rearrange("p (b t) -> p b t", t=DECT),
                            r[:, SEQ:T].rearrange("p (b t) -> p b t", t=DECT))
                        free(j)
                        o1(dve.tensor_copy(hs[:, :, 0:CA], castate[:, b, :].rearrange("p (b t) -> p b t", t=CA)))
                        o1(dve.tensor_copy(cacoll[:, b, 0:CA], hist[:, SEQ:SEQ + CA]))
                        sm = coll_ready if b == NA - 1 else dve_own
                        own(dve.tensor_copy(cacoll[:, b, CA:].rearrange("p (b t) -> p b t", t=CA), hs[:, :, DECT:]).then_inc(sm, 1), sm)
                        C = HISTA - CA
                        if b:
                            dve.wait_ge(conv_out, b)
                        o1(dve.tensor_scalar(ct[:, 0:C], hist[:, 0:C], vec2[:, b:b + 1], None, ALU.mult))
                        for w in range(1, KA):
                            sm = conv_in if w == KA - 1 else dve_own
                            own(dve.scalar_tensor_tensor(ct[:, 0:C], hist[:, w:w + C], vec2[:, w * NA + b:w * NA + b + 1],
                                                         ct[:, 0:C], ALU.mult, ALU.add).then_inc(sm, 1), sm)
                    for j, a, b in ((s["coll"][0], 0, 8), (s["coll"][1], 8, NA)):
                        done(j)
                        for c in range((b - a) // 4):
                            sm = dve_own
                            last = dve.tensor_copy(castout[0:NR, (a + 4 * c) * P:(a + 4 * c + 4) * P], ps[j % 4][0:NR, c, :])
                            if b == NA:
                                own(last.then_inc(coll_out, 1), coll_out)
                            else:
                                o1(last)
                        free(j)
                    dve.wait_ge(conv_out, NA)
                    j = block_job[n + NA]
                    done(j)
                    for q, dst in enumerate((R1, dt_, ig_, fg_)):
                        mul(halves(dst[0:4, :]), ps[j % 4][32 * q:32 * q + 4, :, 0:HT], halves(r[32 * q:32 * q + 4, :]))
                    free(j)
                    dve.wait_ge(in_loaded[3], 5 * 16)
                    own(dve.tensor_scalar(small[0:4, 5:6], small[0:4, 3:4], -1.0, None, ALU.mult).then_inc(row_in, 1), row_in)
                    reset = sumsq[0:4, :]
                    R = lambda t_: t_[0:4, 0:T]
                    NP = SEQ // P

                    def seg(row, last=False):
                        a = row[:, 0:SEQ].rearrange("p (c t) -> p c t", t=P)
                        b = row[:, SEQ:T].rearrange("p (c t) -> p c t", t=DECT)
                        return (a[:, :, P - 1:P], b[:, :, DECT - 1:DECT]) if last else (a, b)

                    def resets():
                        o1(dve.memset(R2[:], 0.0))
                        o1(dve.memset(reset, 1.0))
                        o1(dve.memset(reset[:, 0:SEQ].rearrange("p (c t) -> p c t", t=P)[:, :, 0:1], 0.0))
                        o1(dve.memset(reset[:, SEQ:T].rearrange("p (c t) -> p c t", t=DECT)[:, :, 0:1], 0.0))

                    def decay_rows():
                        dve.wait_ge(row_act, 1)
                        o1(dve.tensor_scalar(small[0:4, 6:7], small[0:4, 4:5], -1.0, None, ALU.mult))
                        o1(dve.tensor_tensor(R(hf_), R(hf_), R(sq_), ALU.add))
                        o1(dve.tensor_scalar(R(dt_), R(hf_), small[0:4, 6:7], None, ALU.mult))
                        o1(dve.tensor_tensor_scan(R(hf_), reset, R(dt_), 0.0, ALU.mult, ALU.add))
                        o1(dve.tensor_copy(R1[32:36, :], R(hf_)))
                        for dst, row, end in zip(seg(R1[64:68, :]), seg(R(hf_)), seg(R(hf_), True)):
                            o1(dve.tensor_tensor(dst, end.to_broadcast(row.shape), row, ALU.subtract))

                    def forget_rows():
                        dve.wait_ge(row_act, 2)
                        o1(dve.scalar_tensor_tensor(R(fg_), R(hi_), -1.0, R(ct_), ALU.mult, ALU.subtract))
                        o1(dve.tensor_scalar(R(ig_), R(ig_), small[0:4, 2:3], None, ALU.add))
                        o1(dve.tensor_tensor_scan(R(sq_), reset, R(fg_), 0.0, ALU.mult, ALU.add))
                        o1(dve.tensor_tensor_scan(ct_[0:4, 0:SEQ], fg_[0:4, 0:SEQ], ig_[0:4, 0:SEQ], 0.0, ALU.add, ALU.max))
                        for b in range(DECB):
                            z = slice(SEQ + b * DECT, SEQ + (b + 1) * DECT)
                            o1(dve.tensor_tensor_scan(ct_[0:4, z], fg_[0:4, z], ig_[0:4, z], m0[0:4, b:b + 1], ALU.add, ALU.max))

                    def maximum_rows():
                        o1(dve.memset(minr[:, 0:1], 0.0))
                        o1(dve.tensor_copy(minr[:, 1:NP].unsqueeze(2), seg(R(ct_), True)[0][:, 0:NP - 1]))
                        o1(dve.tensor_copy(minr[:, NP:NSEG], m0[:, :]))
                        o1(dve.tensor_copy(mfin[:, 0:1], ct_[0:4, SEQ - 1:SEQ]))
                        own(dve.tensor_copy(mfin[:, 1:].unsqueeze(2), seg(R(ct_), True)[1]).then_inc(m_final, 1), m_final)
                        o1(dve.tensor_tensor(R2[0:4, :], R(sq_), R(ct_), ALU.subtract))
                        for dst, row, m_ in zip(seg(R2[32:36, :]), seg(R2[0:4, :]), (minr[:, 0:NP], minr[:, NP:NSEG])):
                            o1(dve.tensor_tensor(dst, row, m_.unsqueeze(2).to_broadcast(row.shape), ALU.add))

                    def key_rows():
                        o1(dve.tensor_scalar(R2[64:68, :], R(ct_), -1.0, None, ALU.mult))
                        o1(dve.tensor_tensor(R(hf_), R(ig_), R(sq_), ALU.subtract))
                        o1(dve.tensor_copy(R1[96:100, :], R(hf_)))
                        for dst, row, end in zip(seg(R2[96:100, :]), seg(R(hf_)), seg(R2[0:4, :], True)):
                            o1(dve.tensor_tensor(dst, row, end.to_broadcast(row.shape), ALU.add))
                        dve.sem_inc(rows_ready, 1)

                    row_steps = [resets, decay_rows, forget_rows, maximum_rows, key_rows]
                    assert len(row_steps) <= NA - 4
                    for b in range(NA):
                        j = block_job[n + NA + 1 + b]
                        done(j)
                        mul(halves(qkv[:, s["pos"][NA + b], :]), P2(j), halves(r[:]))
                        free(j)
                        if b < len(row_steps):
                            row_steps[b]()
                        q = b - HN_LAG
                        if q >= 0:
                            head_norm(s, q, qkv[:, q, :], float(DK) ** -0.5 if q < HA else 1.0)
                elif kind == "core":
                    dve.wait_ge(out_stored, 4 * 16)
                    for t in range(NTILE):
                        delta_tile(t)
                    dve.wait_ge(states_loaded, 16 * (HA + 2 * HB))
                    mlstm_sample()
                    dve.wait_ge(core["tr"], NTILE + 2)
                    o1(dve.tensor_copy(nout[0:HB, 0:P], bank(0)[0:HB, 0:P]))
                    own(dve.tensor_copy(nout[0:DECB, P:], bank(1)[0:DECB, :]).then_inc(states_done, 1), states_done)
                elif kind == "even_z":
                    c1 = NV2 - 1 - HB
                    for q in range(HA + HB):
                        head_norm(s, q, qkv[:, 16 + q, :],
                                  vec2[:, NV2 - 1:NV2] if q < HA else vec2[:, c1 + q - HA:c1 + q - HA + 1])
                        j = block_job[s["n0"] + q]
                        done(j)
                        own(dve.tensor_tensor(halves(gt[:]), P2(j), halves(r[:]), ALU.mult).then_inc(gate_in, 1), gate_in)
                        free(j)
                        dve.wait_ge(act_out, s["act0"] + q + 1)
                        o = qkv[:, 16 + q, :]
                        mul(hf[:], stt[:], o)
                        o1(dve.tensor_tensor(hh[:, q, :], stt[:], o, ALU.mult))
                        own(dve.tensor_tensor(hl[:, q, :], hf[:], hh[:, q, :].bitcast(fp32), ALU.subtract).then_inc(h_ready, 1), h_ready)
                elif kind == "ple":
                    for o in range(KD):
                        j = block_job[s["n0"] + o]
                        if o == 0:
                            norm_recip(s)
                        done(j)
                        if o:
                            dve.wait_ge(act_out, s["act0"] + o)
                        own(dve.tensor_tensor(halves(gt[:]), P2(j), halves(r[:]), ALU.mult).then_inc(gate_in, 1), gate_in)
                        free(j)
                        if o == 0:
                            for q, j in enumerate(s["pT"]):
                                done(j)
                                for c, z in ((0, slice(0, SEQ)), (1, slice(SEQ, T))):
                                    w = z.stop - z.start
                                    o1(dve.tensor_copy(hh[:, q, z], ps[j % 4][:, c, 0:w]))
                                    sm = h_ready if c else dve_own
                                    own(dve.tensor_tensor(hl[:, 6 + q, z], ps[j % 4][:, c, 0:w], hh[:, q, z].bitcast(fp32),
                                                          ALU.subtract).then_inc(sm, 1), sm)
                                free(j)
                    for o in range(KD):
                        j = block_job[s["n0"] + KD + o]
                        done(j)
                        dve.wait_ge(act_out, s["act0"] + o + 1)
                        mul(halves(ut[:]), P2(j), halves(sig[:, o, :]))
                        free(j)
                        own(dve.tensor_tensor(x[:, o, :], x[:, o, :], ut[:], ALU.add).then_inc(x_new, 1), x_new)
                        produce(s["next"], o, s["g"] if s["i"] + 1 < DEPTH else None)
                elif kind == "odd_in":
                    n = s["n0"]
                    hs = hist[:, SEQ + CC:HISTC].rearrange("p (b t) -> p b t", t=DECT + CC)
                    o1(dve.memset(hist[:, 0:CC], 0.0))
                    for b in range(KD):
                        ja, jb = block_job[n + 2 * b], block_job[n + 2 * b + 1]
                        if b == 0:
                            norm_recip(s)
                        done(ja)
                        mul(halves(gt[:]), P2(ja), halves(r[:]))
                        free(ja)
                        done(jb)
                        mul(halves(ut[:]), P2(jb), halves(r[:]))
                        free(jb)
                        mul(hist[:, CC:CC + SEQ], gt[:, 0:SEQ], ut[:, 0:SEQ])
                        mul(hs[:, :, CC:], gt[:, SEQ:T].rearrange("p (b t) -> p b t", t=DECT),
                            ut[:, SEQ:T].rearrange("p (b t) -> p b t", t=DECT))
                        o1(dve.tensor_copy(hs[:, :, 0:CC], ccstate[:, b, :].rearrange("p (b t) -> p b t", t=CC)))
                        o1(dve.tensor_copy(cccoll[:, b, 0:CC], hist[:, SEQ:SEQ + CC]))
                        sm = coll_ready if b == KD - 1 else dve_own
                        own(dve.tensor_copy(cccoll[:, b, CC:].rearrange("p (b t) -> p b t", t=CC), hs[:, :, DECT:]).then_inc(sm, 1), sm)
                        C = HISTC - CC
                        wc = lambda w: vec2[:, KA * NA + w * KD + b:KA * NA + w * KD + b + 1]
                        o1(dve.tensor_scalar(ct[:, 0:C], hist[:, 0:C], wc(0), None, ALU.mult))
                        for w in range(1, KC):
                            o1(dve.scalar_tensor_tensor(ct[:, 0:C], hist[:, w:w + C], wc(w), ct[:, 0:C], ALU.mult, ALU.add))
                        o1(dve.tensor_copy(sig[:, b, 0:SEQ], ct[:, 0:SEQ]))
                        o1(dve.tensor_copy(sig[:, b, SEQ:T].rearrange("p (b t) -> p b t", t=DECT),
                                           ct[:, SEQ + CC:HISTC].rearrange("p (b t) -> p b t", t=DECT + CC)[:, :, 0:DECT]))
                    NR = CC + DECB * CC
                    j = s["coll"][0]
                    done(j)
                    for c in range(2):
                        sm = coll_out if c else dve_own
                        own(dve.tensor_copy(ccout[0:NR, c * 4 * P:(c + 1) * 4 * P], ps[j % 4][0:NR, c, :]).then_inc(sm, 1), sm)
                    free(j)
                    for b in range(KD):
                        j = block_job[n + 2 * KD + b]
                        done(j)
                        mul(halves(ut[:]), P2(j), halves(r[:]))
                        free(j)
                        mul(hf[:], sig[:, b, :], ut[:])
                        o1(dve.tensor_tensor(hh[:, b, :], sig[:, b, :], ut[:], ALU.mult))
                        own(dve.tensor_tensor(hl[:, b, :], hf[:], hh[:, b, :].bitcast(fp32), ALU.subtract).then_inc(h_ready, 1), h_ready)
                elif kind == "final":
                    norm_recip(s)
                    for q, j in enumerate(s["y"]):
                        if q >= 2:
                            done(s["y"][q - 2])
                        g = DEPTH * 4 * KD + q
                        own(dve.scalar_tensor_tensor([gt, ut][q % 2][:], x[:, q, :], vec1[:, g:g + 1], r[:], ALU.mult, ALU.mult).then_inc(y_in, 1), y_in)
                        if q >= 1:
                            y_evac(q - 1, s["y"][q - 1])
                    y_evac(KD - 1, s["y"][KD - 1])


def kernel(**inputs):
    import numpy as np
    import concourse.bacc as bacc
    from concourse.bass_utils import run_bass_kernel_spmd
    nc = bacc.Bacc("TRN2", target_bir_lowering=False, num_devices=1)
    arrays, ins = {}, {}
    for name, value in inputs.items():
        a = np.ascontiguousarray(value)
        arrays["in_" + name] = a
        ins[name] = nc.dram_tensor("in_" + name, a.shape, mybir.dt.from_np(a.dtype), kind="ExternalInput").ap()
    xp, xs = arrays["in_x_prompt"].shape, arrays["in_x_sample"].shape
    conv, S, C = (arrays["in_state_" + k].shape for k in ("gdn_conv", "gdn_S", "mlstm_C"))
    n, m, cc = (arrays["in_state_" + k].shape for k in ("mlstm_n", "mlstm_m", "conv"))
    one = lambda s: (s[0], xp[0]) + tuple(s[2:])
    shapes = dict(y_p=xp, y_s=xs, gdn_conv_p=one(conv), gdn_S_p=one(S), mlstm_C_p=one(C), mlstm_n_p=one(n),
                  mlstm_m_p=one(m), conv_p=one(cc), gdn_conv_s=conv, gdn_S_s=S, mlstm_C_s=C, mlstm_n_s=n,
                  mlstm_m_s=m, conv_s=cc)
    outs = {k: nc.dram_tensor("out_" + k, tuple(v), mybir.dt.float32, kind="ExternalOutput").ap() for k, v in shapes.items()}
    stream_step(nc, ins, outs)
    res = run_bass_kernel_spmd(nc, [arrays], core_ids=[0]).results[0]
    return tuple(res["out_" + k] for k in shapes)
```

```python
import concourse.bass as bass
from concourse import mybir
from contextlib import ExitStack


def stream_step(nc, ins, outs):
    fp32 = mybir.dt.float32
    fp32r = mybir.dt.float32r
    ALU = mybir.AluOpType
    ACT = mybir.ActivationFunctionType

    P = 128
    BATCH, SEQ, D = ins["x_prompt"].shape
    DECB, DECT, _ = ins["x_sample"].shape
    DEPTH = ins["norm_g"].shape[0]
    DFF = ins["ffn_w_d"].shape[2]
    DPLE = ins["w_ple"].shape[1]
    HA, DK = ins["state_gdn_S"].shape[2:4]
    HB = ins["state_mlstm_C"].shape[2]
    assert BATCH == 1 and DECB * DECT == P and SEQ % P == 0 and HA == HB == 4 and DK == P
    T = SEQ + P
    HT = T // 2
    NTILE = T // P
    KD = D // P
    NF = DFF // P
    PARTS = [8, 8, NF - 16]
    KP = DPLE // P
    KA, KC = ins["gdn_conv_w"].shape[1], ins["conv_c_w"].shape[1]
    EPS = 1e-6
    NA = 3 * HA
    LVL = 7
    LVLS = 4
    MW = P + 1

    ctx = ExitStack()
    with ctx:
        base = nc.sbuf_base
        arena = ctx.enter_context(nc.sbuf_tensor("arena", [P, (229344 - base - 64) // 4], fp32))
        place = [-(-base // 32) * 32]

        def at(name, shape, offset, dt=fp32):
            return nc.alloc_sbuf_tensor_at(name, shape, dt, offset=offset)

        def sb(name, shape, dt=fp32):
            size = 4
            for s in shape[1:]:
                size *= s
            place[0] = -(-place[0] // 32) * 32
            t = at(name, shape, place[0], dt)
            place[0] += size
            assert place[0] <= 229344, (name, place[0])
            return t

        def sem(name):
            return ctx.enter_context(nc.semaphore(name))

        x = sb("x", [P, KD, T])
        xh = sb("xh", [P, KD, T], fp32r)
        xl = sb("xl", [P, KD, T], fp32r)
        raw = sb("raw", [P, 4, KD, P])
        whi = sb("whi", [P, 2, KD, P], fp32r)
        wlo = sb("wlo", [P, 2, KD, P], fp32r)
        PIECE = 4 * T
        B0 = -(-place[0] // 32) * 32
        qkv = sb("qkv", [P, 2 * NA, T])
        hh = at("hh", [P, 8, T], B0, fp32r)
        hl = at("hl", [P, 8, T], B0 + 8 * PIECE, fp32r)
        sig = at("sig", [P, 8, T], B0 + 16 * PIECE)
        xstage = at("xstage", [P, NTILE, D], B0)
        vstage = at("vstage", [P, 2, P], B0 + 8 * PIECE)
        castage = at("castage", [P, NA * P], B0 + 9 * PIECE)
        ccstage = at("ccstage", [P, D], B0 + 12 * PIECE)
        ystage = at("ystage", [P, NTILE, D], B0)
        yg = at("yg", [P, KD, T], B0 + 8 * PIECE)
        PH = PARTS[-1]
        assert PH + KP <= 8
        pstage = at("pstage", [P, NTILE, DPLE], B0 + 22 * PIECE)
        st = sb("st", [P, HB, DECB, MW])
        sg = at("sg", [P, HA, DECB, P], place[0] - 4 * HB * DECB * MW)
        S0 = place[0] - 4 * HB * DECB * MW
        castout = at("castout", [P, NA * P], S0)
        ccout = at("ccout", [P, D], S0)
        assert 4 * (NA * P + 4 * T) <= 4 * HB * DECB * MW
        rtmp = [at(f"rtmp{i}", [P, T], S0 + 4 * NA * P + i * PIECE) for i in range(4)]
        assert 8 * HA * MW == HB * DECB * MW
        V8 = at("V8", [P, 8, HA * MW], S0)
        pS = sb("pS", [P, HA, P])
        pC = sb("pC", [P, HB, MW])
        r = sb("r", [P, T])
        sumsq = sb("sumsq", [P, T])
        T0 = -(-place[0] // 32) * 32
        W9 = sb("W9", [P, 9, HA * MW])
        gt = at("gt", [P, T], T0)
        stt = at("stt", [P, T], T0 + PIECE)
        ut = at("ut", [P, T], T0 + 2 * PIECE)
        hf = at("hf", [P, T], T0 + 3 * PIECE)
        sq = at("sq", [P, T], T0 + 4 * PIECE)
        HISTA = SEQ + KA - 1 + DECB * (DECT + KA - 1)
        HISTC = SEQ + KC - 1 + DECB * (DECT + KC - 1)
        HISTB = -(-4 * HISTA // 32) * 32
        hist = at("hist", [P, HISTA], T0 + 5 * PIECE)
        ct = at("ct", [P, HISTA], T0 + 5 * PIECE + HISTB)
        root = at("root", [P, T], T0 + 5 * PIECE)
        inv = at("inv", [P, T], T0 + 5 * PIECE + HISTB)
        assert 5 * PIECE + 2 * HISTB <= 9 * HA * MW * 4
        R1 = sb("R1", [P, T])
        nout = at("nout", [P, (HB + 1) * P], place[0] - PIECE)
        R0 = place[0]
        R2 = sb("R2", [P, T])
        CA, CC = KA - 1, KC - 1
        castate = at("castate", [P, NA, DECB * CA], R0)
        cacoll = at("cacoll", [P, NA, CA + DECB * CA], R0 + 4 * NA * DECB * CA)
        ccstate = sb("ccstate", [P, KD, DECB * CC])
        cccoll = at("cccoll", [P, KD, CC + DECB * CC], R0)
        ident = sb("ident", [P, P])
        level = sb("level", [P, LVL, P])
        incl = sb("incl", [P, 2, P])
        bmask = sb("bmask", [P, DECB])
        NV1 = DEPTH * 4 * KD + KD
        NV2 = KA * NA + KC * KD + HB + 1
        vec1 = sb("vec1", [P, NV1])
        vec2 = sb("vec2", [P, NV2])
        one = sb("one", [P, 1])
        eps = sb("eps", [P, 1])
        wg = sb("wg", [P, KD, 16])
        gcol = sb("gcol", [P, 8])
        GC = 64 + HA - 32
        gcols = sb("gcols", [P, GC])
        kcol = sb("kcol", [P, 8])
        small = sb("small", [4, 8])
        m0 = sb("m0", [4, DECB])
        mfin = sb("mfin", [4, 1 + DECB])
        NSEG = SEQ // P + DECB
        minr = sb("minr", [4, NSEG])

        ps = [ctx.enter_context(nc.psum_tensor(f"ps{i}", [P, 2, 512], fp32)) for i in range(4)]

        osq = [sq, ut, gt, stt]
        oroot = [root, inv, hf, sq]

        dt_, ig_, fg_, hf_ = rtmp
        sq_, hi_, ct_ = (qkv[:, 2 * NA - 4 + i, :] for i in range(3))

        def halves(tok):
            return tok.rearrange("p (a b) -> p a b", a=2)

        def bank(i):
            return ps[i // 2][:, i % 2, :]

        def heads(i):
            return bank(i).rearrange("p (h t) -> p h t", h=HA)

        def uexp(width, h):
            a = ((6, 4) if width == P else (7, 2))[h % 2]
            return W9[:, a:a + 2, :].rearrange("p a b -> p (a b)")[:, 0:DECB * width].rearrange("p (b c) -> p b c", b=DECB)

        def W(i):
            return W9[:, i, 0:HA * P].rearrange("p (h t) -> p h t", h=HA)

        UPCUTS = [(0, 3), (3, 6), (6, DECB)]
        UPBANKS = [(3, 4, 5), (0, 6, 7)]

        def state_products(h):
            return bank(2 + h // 2).rearrange("p (h w t) -> p h w t", h=2, w=2)[:, h % 2]

        def V(i):
            return V8[:, i, 0:HA * P].rearrange("p (h t) -> p h t", h=HA)

        raw_loaded = [sem(f"raw_loaded{i}") for i in range(4)]
        hi_ready = sem("hi_ready")
        lo_ready = sem("lo_ready")
        job_done = sem("job_done")
        slot_free = [sem(f"slot_free{i}") for i in range(4)]
        xg_hi = sem("xg_hi")
        xg_ready = sem("xg_ready")
        x_new = sem("x_new")
        x_copied = sem("x_copied")
        vec_ready = sem("vec_ready")
        sq_ready = sem("sq_ready")
        root_ready = sem("root_ready")
        gate_in = sem("gate_in")
        act_out = sem("act_out")
        h_ready = sem("h_ready")
        dve_own = sem("dve_own")
        act_own = sem("act_own")
        pool_own = sem("pool_own")
        pool_consts = sem("pool_consts")
        in_loaded = [sem(f"in_loaded{i}") for i in range(6)]
        out_stored = sem("out_stored")
        p_loaded = sem("p_loaded")
        emb_copied = sem("emb_copied")
        hn_sq = sem("hn_sq")
        hn_root = sem("hn_root")
        conv_in = sem("conv_in")
        conv_out = sem("conv_out")
        row_in = sem("row_in")
        row_act = sem("row_act")
        rows_ready = sem("rows_ready")
        coll_ready = sem("coll_ready")
        coll_out = sem("coll_out")
        states_loaded = sem("states_loaded")
        states_stored = sem("states_stored")
        states_done = sem("states_done")
        hn_used = sem("hn_used")
        o_high = sem("o_high")
        o_sq_act = sem("o_sq_act")
        o_sq_dve = sem("o_sq_dve")
        m_final = sem("m_final")
        y_in = sem("y_in")
        y_copied = sem("y_copied")
        col_root = sem("col_root")
        y_dve = sem("y_dve")
        y_act = sem("y_act")
        ident_ready = sem("ident_ready")
        core = {k: sem("core_" + k) for k in (
            "bcast",
            "prod", "expin", "c0", "x0", "xt0",
            "gam", "eg",
            "kk", "np", "tr", "ktr",
            "kend", "ctl", "x6", "xr",
            "m1", "d2", "d", "ks",
            "m1c", "rtok", "utok",
            "rT", "rt", "u", "o",
            "uexp", "sup", "decay", "up",
            "vt", "ktok", "nq")}

        ml_pe, ml_act, ml_dve = sem("ml_pe"), sem("ml_act"), sem("ml_dve")
        ML_PE = "gates qin qk floor vt kin kt num den up0 up1".split()
        ML_ACT = "gates qin floor vt kin kt den".split()
        ML_DVE = "gates qk q out up0 up1".split()

        def ml(steps, t, name):
            return len(steps) * t + steps.index(name) + 1

        blocks = []
        jobs = []
        block_job = []

        def job(kind, n=None):
            jobs.append((kind, n))
            return len(jobs) - 1

        def blk(src, kt, kind):
            blocks.append((src, kt))
            block_job.append(job(kind, len(blocks) - 1))
            return len(blocks) - 1

        stages = []
        prod = 0

        def load_stage():
            nonlocal prod
            s = dict(kind="load", vec=job("vec"), x=[job("xT") for _ in range(KD)], cs=job("cs"), prod=0)
            stages.append(s)
            prod = 1

        def ffn_stage(i, f, first_pair):
            nonlocal prod
            gu, dn = ins["ffn_w_gu"][i, f], ins["ffn_w_d"][i, f]
            j0 = 0
            for part, cnt in enumerate(PARTS):
                s = dict(kind="gu", count=cnt, norm=None, prod=prod - 1, first=part == 0,
                         n0=len(blocks), src=gu, col0=j0)
                for q in range(cnt):
                    blk((gu, (j0 + q) * P), KD, "gate")
                    if part == 0 and q == 0:
                        s["norm"] = job("norm")
                    blk((gu, DFF + (j0 + q) * P), KD, "up")
                stages.append(s)
                last = part == len(PARTS) - 1
                s = dict(kind="down", n0=len(blocks), kt=cnt, last=last, scale=0.5, hbase=first_pair + j0, layer=i,
                         prod=prod if last else None, g=(i * 4 + (1 if f == 0 else 3)) * KD)
                for o in range(KD):
                    blk((dn, o * P, j0 * P), cnt, "down")
                    if last and f == 1 and o == 0:
                        s["pT"] = [job("pT") for _ in range(KP)]
                if last and f == 1:
                    stages[-1]["p_layer"] = i
                stages.append(s)
                j0 += cnt
            prod += 1

        pairs = 0
        load_stage()
        ffn_stage(0, 0, pairs)
        pairs += NF
        w_in = ins["w_in_even"][0]
        wcol = [0, HA * P, 2 * HA * P, 3 * HA * P]
        gcol0 = 4 * HA * P
        bcol = [gcol0 + 2 * HA + q * HB * P for q in range(4)]
        icol = bcol[3] + HB * P
        HN_LAG = NA - 2 * HA
        s = dict(kind="even_in", n0=len(blocks), prod=prod - 1, pos=[], l2=[])
        for q in range(3):
            for h in range(HA):
                blk((w_in, wcol[q] + h * P), KD, "conv")
                if q == 0 and h == 0:
                    s["norm"] = job("norm")
                s["pos"].append([0, 4, 16][q] + h)
        s["gates"] = blk((None, 0), KD, "gates")
        s["coll"] = [job("coll"), job("coll")]
        for q in range(3):
            for h in range(HB):
                blk((w_in, bcol[q] + h * P), KD, "plain")
                s["pos"].append([8, 12, 20][q] + h)
                if q * HB + h >= HN_LAG:
                    s["l2"].append(job("hn"))
        stages.append(s)
        for c0, first in ((wcol[3], 0), (bcol[3], HA)):
            stages.append(dict(kind="core" if first == 0 else "mlstm_sample", jobs=len(jobs)))
            s = dict(kind="even_z", onorm=[job("hn") for _ in range(HA)], n0=len(blocks), first=first)
            for h in range(HA):
                blk((w_in, c0 + h * P), KD, "z")
            stages.append(s)
        stages.append(dict(kind="down", n0=len(blocks), kt=KD, last=True, scale=1.0, hbase=pairs, prod=prod, g=2 * KD))
        for o in range(KD):
            blk((ins["w_out_even"][0], o * P, 0), KD, "down")
        prod += 1
        pairs += HA + HB
        ffn_stage(0, 1, pairs)
        pairs += NF

        Y_LAG = 2

        def ple_stage(i):
            nonlocal prod, pairs
            s = dict(kind="ple", i=i, n0=len(blocks), prod=prod - 1, hbase=pairs, y=[])
            for o in range(KD):
                blk((ins["w_ple"][i], o * P), KP, "pemb")
            for o in range(KD):
                blk((ins["w_ple_gate"][i], o * P), KD, "pgate")
                if o == 0:
                    s["norm"] = job("norm")
                if i == DEPTH - 1 and o >= Y_LAG:
                    s["y"].append(job("yT"))
            if i == DEPTH - 1:
                s["y"] += [job("yT") for _ in range(Y_LAG)]
            s["next"] = prod
            s["g"] = (i + 1) * 4 * KD
            stages.append(s)
            prod += 1
            pairs += KP

        ple_stage(0)
        ffn_stage(1, 0, pairs)
        pairs += NF
        w_odd = ins["w_in_odd"][0]
        s = dict(kind="odd_in", n0=len(blocks), prod=prod - 1, hbase=pairs)
        for q in range(KD):
            blk((w_odd, q * P), KD, "gate")
            if q == 0:
                s["norm"] = job("norm")
            blk((w_odd, 2 * D + q * P), KD, "up")
        for q in range(KD):
            blk((w_odd, D + q * P), KD, "bg")
            if q == 0:
                s["coll"] = [job("coll")]
        stages.append(s)
        stages.append(dict(kind="down", n0=len(blocks), kt=KD, last=True, scale=1.0, hbase=pairs, prod=prod, g=6 * KD))
        for o in range(KD):
            blk((ins["w_out_odd"][0], o * P, 0), KD, "down")
        prod += 1
        pairs += KD
        ffn_stage(1, 1, pairs)
        pairs += NF
        ple_stage(1)
        s = dict(kind="final", prod=prod - 1)
        s["norm"] = job("norm")
        stages.append(s)
        NB = len(blocks)

        hn0 = 0
        for s in stages:
            if s["kind"] == "even_in":
                s["hn0"] = hn0
                hn0 += 2 * HA
            if s["kind"] == "even_z":
                s["hn0"] = hn0
                hn0 += HA
        act0 = 0
        for s in stages:
            s["act0"] = act0
            if s["kind"] == "gu":
                act0 += s["count"]
            elif s["kind"] == "even_z":
                act0 += HA
            elif s["kind"] == "ple":
                act0 += KD

        class Tally:

            def __init__(self, engine):
                self.engine, self.counts, self.turn, self.per = engine, {}, None, {}

            def __call__(self, _, s):
                self.counts[s.name] = self.counts.get(s.name, 0) + 1
                v = self.counts[s.name]
                self.engine.wait_ge(s, v if self.turn is None else self.turn * self.per[s.name] + v)

            def enter(self, turn, per):
                self.turn, self.per = turn, {k.name: v for k, v in per.items()}
                self.before = dict(self.counts)

            def leave(self, trips):
                for k, v in self.counts.items():
                    body = v - self.before.get(k, 0)
                    assert body == self.per.get(k, 0), (k, body)
                    self.counts[k] = self.before.get(k, 0) + body * trips
                self.turn = None

        def turns(value, turn, per):
            return value if turn is None else turn * per + value

        block = ctx.enter_context(nc.Block())

        @block.sync
        def _(sp):
            def load(n, source, off=0):
                slot = n % 4
                if n >= 4:
                    sp.wait_ge(lo_ready, n - 3 + off)
                sp.dma_start(raw[:, slot, 0:source.shape[1], :], source).then_inc(raw_loaded[slot], 16)

            def source(n):
                src, kt = blocks[n]
                if len(src) == 2:
                    return src[0].rearrange("(k p) c -> p k c", p=P)[:, :, src[1]:src[1] + P]
                return src[0][src[2]:src[2] + kt * P, src[1]:src[1] + P].rearrange("(k p) c -> p k c", p=P)

            xp = ins["x_prompt"][0].rearrange("(t p) d -> p t d", p=P)
            xd = ins["x_sample"].rearrange("b t d -> (b t) d")

            def load_x(half):
                z = slice(half * D // 2, (half + 1) * D // 2)
                sp.dma_start(xstage[:, 0:NTILE - 1, z], xp[:, :, z]).then_inc(in_loaded[5 * half], 16)
                sp.dma_start(xstage[:, NTILE - 1, z], xd[:, z]).then_inc(in_loaded[5 * half], 16)

            load_x(0)
            sp.dma_start(vstage[0:DEPTH * 4 * KD, 0, :], ins["norm_g"].rearrange("i f (k p) -> (i f k) p", p=P)).then_inc(in_loaded[1], 16)
            sp.dma_start(vstage[DEPTH * 4 * KD:NV1, 0, :], ins["final_norm"].rearrange("(k p) -> k p", p=P)).then_inc(in_loaded[1], 16)
            a, b = KA * NA, KA * NA + KC * KD
            sp.dma_start(vstage[0:a, 1, :], ins["gdn_conv_w"][0].rearrange("j (k p) -> (j k) p", p=P)).then_inc(in_loaded[1], 16)
            sp.dma_start(vstage[a:b, 1, :], ins["conv_c_w"][0].rearrange("j (k p) -> (j k) p", p=P)).then_inc(in_loaded[1], 16)
            sp.dma_start(vstage[b:b + HB, 1, :], ins["mlstm_norm_w"][0].rearrange("(k p) -> k p", p=P)).then_inc(in_loaded[1], 16)
            sp.dma_start(vstage[b + HB:b + HB + 1, 1, :], ins["gdn_norm_w"]).then_inc(in_loaded[1], 16)
            load_x(1)
            load(0, source(0))
            load(1, source(1))
            sp.dma_start(castage[0:DECB * CA, :], ins["state_gdn_conv"][0].rearrange("b t c -> (b t) c")).then_inc(in_loaded[2], 16)
            sp.dma_start(ccstage[0:DECB * CC, :], ins["state_conv"][0].rearrange("b t c -> (b t) c")).then_inc(in_loaded[2], 16)
            with nc.allow_non_contiguous_dma(reason="a few words of gate parameters"):
                for q, name in enumerate(["gdn_a_log", "gdn_dt_bias", "mlstm_b_i", "mlstm_b_f"]):
                    sp.dma_start(small[0:4, q:q + 1], ins[name].rearrange("a h -> h a")).then_inc(in_loaded[3], 16)
                sp.dma_start(m0[0:4, :], ins["state_mlstm_m"][0].rearrange("b h -> h b")).then_inc(in_loaded[3], 16)
                wv = w_in.rearrange("(k p) c -> p k c", p=P)
                sp.dma_start(wg[:, :, 0:8], wv[:, :, gcol0:gcol0 + 8]).then_inc(in_loaded[4], 16)
                sp.dma_start(wg[:, :, 8:16], wv[:, :, icol:icol + 8]).then_inc(in_loaded[4], 16)

            ahead = 2
            for s in stages:
                if s["kind"] == "gu":
                    gv = s["src"].rearrange("(k p) c -> p k c", p=P)
                    lead = 4
                    for n in range(max(ahead, s["n0"]), s["n0"] + lead):
                        load(n, source(n))
                    if "p_layer" in s:
                        sp.wait_ge(job_done, block_job[s["n0"] - 1] + 1)
                        i = s["p_layer"]
                        sp.dma_start(pstage[:, 0:NTILE - 1, :], ins["p_prompt"][i, 0].rearrange("(t p) d -> p t d", p=P)).then_inc(p_loaded, 16)
                        sp.dma_start(pstage[:, NTILE - 1, :], ins["p_sample"][i].rearrange("b t d -> (b t) d")).then_inc(p_loaded, 16)
                    trips = (2 * s["count"] - lead) // 4
                    with sp.Fori(0, trips) as i:
                        for u in range(4):
                            n = s["n0"] + lead + u
                            c = (s["col0"] + (lead + u) // 2) * P + (u % 2) * DFF
                            load(n, gv[:, :, bass.ds(i * (2 * P) + c, P)], i * 4)
                elif s["kind"] in ("down", "ple", "even_z", "odd_in", "even_in"):
                    count = {"down": KD, "ple": 2 * KD, "even_z": HA, "odd_in": 3 * KD, "even_in": 2 * NA + 1}[s["kind"]]
                    for n in range(max(ahead, s["n0"]), s["n0"] + count):
                        if blocks[n][0][0] is None:
                            sp.wait_ge(lo_ready, n - 3)
                            sp.sem_inc(raw_loaded[n % 4], 16)
                        else:
                            load(n, source(n))
                    if s["kind"] == "even_in":
                        sp.wait_ge(coll_out, 1)
                        sp.dma_start(outs["gdn_conv_p"][0, 0], castout[0:CA, :]).then_inc(out_stored, 16)
                        sp.dma_start(outs["gdn_conv_s"][0].rearrange("b t c -> (b t) c"), castout[CA:CA + DECB * CA, :]).then_inc(out_stored, 16)
                    if s["kind"] == "odd_in":
                        sp.wait_ge(coll_out, 2)
                        sp.dma_start(outs["conv_p"][0, 0], ccout[0:CC, :]).then_inc(out_stored, 16)
                        sp.dma_start(outs["conv_s"][0].rearrange("b t c -> (b t) c"), ccout[CC:CC + DECB * CC, :]).then_inc(out_stored, 16)
                elif s["kind"] == "core":
                    z0 = next(z["n0"] for z in stages if z["kind"] == "even_z")
                    for n in range(z0, z0 + 4):
                        load(n, source(n))
                    sp.wait_ge(m_final, 1)
                    with nc.allow_non_contiguous_dma(reason="a few words"):
                        sp.dma_start(outs["mlstm_m_p"][0].rearrange("b h -> h b"), mfin[:, 0:1]).then_inc(out_stored, 16)
                        sp.dma_start(outs["mlstm_m_s"][0].rearrange("b h -> h b"), mfin[:, 1:]).then_inc(out_stored, 16)
                    sp.wait_ge(ml_dve, len(ML_DVE) * (NTILE - 1))
                    for h in range(HA):
                        sp.dma_start(sg[:, h], ins["state_gdn_S"][0, :, h].rearrange("b k v -> k b v")).then_inc(states_loaded, 16)
                    sp.wait_ge(core["up"], NTILE)
                    sp.dma_start(outs["gdn_S_p"][0, 0].rearrange("h k v -> k h v"), pS[:]).then_inc(states_stored, 16)
                    for h in range(HA):
                        sp.dma_start(outs["gdn_S_s"][0, :, h].rearrange("b k v -> k b v"), sg[:, h]).then_inc(states_stored, 16)
                    sp.wait_ge(states_stored, 16 * (1 + HA))
                    for h in range(HB):
                        sp.dma_start(st[:, h, :, 0:P], ins["state_mlstm_C"][0, :, h].rearrange("b k v -> k b v")).then_inc(states_loaded, 16)
                        with nc.allow_non_contiguous_dma(reason="normalisers as a column"):
                            sp.dma_start(st[:, h, :, P:MW], ins["state_mlstm_n"][0, :, h].rearrange("b (k o) -> k b o", o=1)).then_inc(states_loaded, 16)
                    ahead = z0 + 2 * HA + 2
                    for n in range(z0 + 4, ahead):
                        load(n, source(n))
                elif s["kind"] == "mlstm_sample":
                    sp.wait_ge(core["up"], NTILE + 1)
                    sp.dma_start(outs["mlstm_C_p"][0, 0].rearrange("h k v -> k h v"), pC[:, :, 0:P]).then_inc(out_stored, 16)
                    for h in range(HB):
                        sp.dma_start(outs["mlstm_C_s"][0, :, h].rearrange("b k v -> k b v"), st[:, h, :, 0:P]).then_inc(out_stored, 16)
                    sp.wait_ge(states_done, 1)
                    sp.dma_start(outs["mlstm_n_p"][0, 0], nout[0:HB, 0:P]).then_inc(out_stored, 16)
                    sp.dma_start(outs["mlstm_n_s"][0].rearrange("b h k -> b (h k)"), nout[0:DECB, P:]).then_inc(out_stored, 16)
            for t in range(NTILE):
                sp.wait_ge([y_dve, y_act][t % 2], t // 2 + 1)
                dst = outs["y_p"][0][t * P:(t + 1) * P, :] if t < NTILE - 1 else outs["y_s"].rearrange("b t d -> (b t) d")
                sp.dma_start(dst, ystage[:, t, :]).then_inc(out_stored, 16)
            sp.wait_ge(out_stored, (2 + 2 + 2 + 1 + HB + 2 + NTILE) * 16)

        @block.gpsimd
        def _(pool):
            own = [0]

            def step(ins_):
                own[0] += 1
                ins_.then_inc(pool_own, 1)
                pool.wait_ge(pool_own, own[0])

            def select(out, pattern, base_, mult, op):
                step(pool.affine_select(out=out, in_=out, compare_op=op, fill=0.0, base=base_, pattern=pattern,
                                        channel_multiplier=mult))

            step(pool.memset(ident[:], 0.0))
            step(pool.affine_select(out=ident[:], in_=ident[:], compare_op=ALU.not_equal, fill=1.0, base=0,
                                    pattern=[[-1, P]], channel_multiplier=1))
            step(pool.memset(one[:], 1.0))
            pool.sem_inc(ident_ready, 1)
            step(pool.memset(R1[:], 0.0))
            step(pool.memset(incl[:], 1.0))
            for g in range(2):
                select(incl[:, g, :], [[1, P]], 0, -1, ALU.is_ge)
            select(incl[:, 1, :], [[-DECT, DECB], [0, DECT]], 0, 1, ALU.is_ge)
            step(pool.memset(bmask[:], 1.0))
            select(bmask[:], [[-DECT, DECB]], 0, 1, ALU.is_ge)
            select(bmask[:], [[DECT, DECB]], DECT - 1, -1, ALU.is_ge)
            step(pool.memset(level[:], 1.0))
            for l in range(LVL):
                w = 1 << l
                v = level[:, l, :]
                if P // (2 * w) > 1:
                    select(v, [[-2 * w, P // (2 * w)], [0, 2 * w]], 0, 1, ALU.is_ge)
                select(v, [[2 * w, P // (2 * w)], [0, 2 * w]], w - 1, -1, ALU.is_ge)
                step(pool.memset(v.rearrange("p (b w) -> p b w", w=2 * w)[:, :, 0:w], 0.0))
            pool.sem_inc(pool_consts, 1)

            def low(n, kt, off=0):
                slot, ws = n % 4, n % 2
                pool.wait_ge(hi_ready, n + 1 + off)
                pool.tensor_tensor(wlo[:, ws, 0:kt, :], raw[:, slot, 0:kt, :], whi[:, ws, 0:kt, :].bitcast(fp32),
                                   ALU.subtract).then_inc(lo_ready, 1)

            def decay(read, width, states_, exps):
                pool.wait_ge(*read)
                for h in range(HA):
                    ends = exps[:, h].rearrange("p (b t) -> p b t", t=DECT)[:, :, DECT - 1:DECT].to_broadcast([P, DECB, width])
                    pool.tensor_tensor(states_[:, h], states_[:, h], ends, ALU.mult).then_inc(core["decay"], 1)

            z1, z2 = (z["n0"] + 2 for z in stages if z["kind"] == "even_z")
            n = 0
            while n < NB:
                if n == z1:
                    decay((core["ks"], NTILE), P, sg, W(2))
                if n == z2:
                    decay((core["np"], NTILE + 1), MW, st, W(1))
                kt = blocks[n][1]
                if blocks[n][0][0] is None:
                    pool.wait_ge(hi_ready, n + 1)
                    quad = wlo[:, n % 2].rearrange("p k (q c) -> p k q c", q=4)[:, :, :, 0:4]
                    quadh = whi[:, n % 2].rearrange("p k (q c) -> p k q c", q=4)[:, :, :, 0:4].bitcast(fp32)
                    pool.tensor_tensor(quad, wg[:].rearrange("p k (q c) -> p k q c", q=4), quadh,
                                       ALU.subtract).then_inc(lo_ready, 1)
                    n += 1
                    continue
                run = 0
                while n + run < NB and blocks[n + run][1] == kt and blocks[n + run][0][0] is not None and not (run and n + run in (z1, z2)):
                    run += 1
                if run >= 8:
                    with pool.Fori(0, run // 4) as i:
                        for u in range(4):
                            low(n + u, kt, i * 4)
                    n += run // 4 * 4
                    run %= 4
                for u in range(run):
                    low(n, kt)
                    n += 1

        @block.tensor
        def _(pe):
            def wait_slot(j, turn=None):
                if j >= 4:
                    pe.wait_ge(slot_free[j % 4], turns(j // 4, turn, 1))

            def drain(s):
                for c in range(4):
                    pe.wait_ge(slot_free[c], (s["jobs"] + 3 - c) // 4)

            def mm(n, hi, lo, turn=None, first=None):
                j, kt, ws = block_job[n], blocks[n][1], n % 2
                wait_slot(j, turn)
                pe.wait_ge(lo_ready, turns(n + 1, turn, 4))
                for k in range(kt):
                    if first is not None:
                        pe.wait_ge(first[0], first[1] + k + 1)
                    for c in range(2):
                        cs = slice(c * HT, (c + 1) * HT)
                        pe.matmul(ps[j % 4][:, c, 0:HT], whi[:, ws, k], hi[:, k, cs], start=(k == 0), stop=False)
                        pe.matmul(ps[j % 4][:, c, 0:HT], whi[:, ws, k], lo[:, k, cs], start=False, stop=False)
                    for c in range(2):
                        cs = slice(c * HT, (c + 1) * HT)
                        last = pe.matmul(ps[j % 4][:, c, 0:HT], wlo[:, ws, k], hi[:, k, cs], start=False, stop=(k == kt - 1))
                last.then_inc(job_done, 1)

            def sum_job(j, src):
                wait_slot(j)
                for c in range(2):
                    last = pe.matmul(ps[j % 4][:, c, 0:HT], one[:].to_broadcast([P, P]), src[:, c * HT:(c + 1) * HT],
                                     start=True, stop=True)
                last.then_inc(job_done, 1)

            def norm_job(s):
                pe.wait_ge(xg_ready, 8 * s["prod"] + 8)
                sum_job(s["norm"], sumsq)

            def tposes(j, pieces):
                wait_slot(j)
                for c, col, src in pieces:
                    rows, cols = src.shape
                    last = pe.transpose(ps[j % 4][0:cols, c, col:col + rows], src, ident[0:rows, 0:rows])
                last.then_inc(job_done, 1)

            def y_job(s, q):
                pe.wait_ge(y_in, q + 1)
                tposes(s["y"][q], [(t // 4, t % 4 * P, yg[:, q, t * P:(t + 1) * P]) for t in range(NTILE)])

            def tile(t):
                return slice(t * P, (t + 1) * P)

            def spread(b, rows, first_row, t):
                for h in range(HA):
                    c = first_row + h
                    last = pe.matmul(bank(b)[:, h * P:(h + 1) * P], ident[:, c:c + 1].to_broadcast([P, P]), rows[:, tile(t)],
                                     start=True, stop=True)
                return last

            def per_head(b, lhsT, rhs, N=P):
                for h in range(HA):
                    last = pe.matmul(bank(b)[:, h * P:(h + 1) * P], lhsT(h), rhs(h), start=True, stop=True)
                return last

            def token_rows(t):
                spread(0, R1, 0, t)
                spread(1, R1, 32, t)
                pe.transpose(bank(4)[:, 0:P], R1[:, tile(t)], ident[:]).then_inc(core["bcast"], 1)

            def delta_tile(t):
                sample = t == NTILE - 1
                L = LVLS if sample else LVL
                q, k = qkv[:, 0:HA, tile(t)], qkv[:, HA:2 * HA, tile(t)]
                li, l2 = (LVL - 1) * t, (LVL - 2) * t
                if t == 0:
                    token_rows(0)
                pe.wait_ge(core["prod"], t + 1)
                per_head(4, lambda h: k[:, h], lambda h: W(0)[:, h]).then_inc(core["kk"], 1)
                if t:
                    pe.wait_ge(core["up"], t)
                per_head(3, lambda h: k[:, h], lambda h: q[:, h]).then_inc(core["np"], 1)
                if not sample:
                    mlstm_part(t, "gates")
                pe.wait_ge(core["c0"], t + 1)
                for h in range(HA):
                    last = pe.transpose(bank(4)[:, h * P:(h + 1) * P], W(7)[:, h], ident[:])
                last.then_inc(core["tr"], 1)
                for l in range(1, L):
                    pe.wait_ge(core["ctl"], li + l)
                    if l == 1:
                        pe.wait_ge(core["x0"], t + 1)
                    else:
                        pe.wait_ge(core["x6"], l2 + l - 1)
                    per_head(0, lambda h: W(1)[:, h], lambda h: W(6)[:, h]).then_inc(core["m1"], 1)
                    if l == 1:
                        pe.wait_ge(core["xt0"], t + 1)
                        pe.wait_ge(core["eg"], t + 1)
                        for h in range(HA):
                            last = pe.transpose(bank(5)[:, h * P:(h + 1) * P], k[:, h], ident[:])
                        last.then_inc(core["ktr"], 1)
                    if not sample:
                        for part in {1: ["qin"], 2: ["floor"], 3: ["kin"], 4: ["kt"], 5: ["den"], 6: ["up0"]}[l]:
                            mlstm_part(t, part)
                    pe.wait_ge(core["m1c"], li + l)
                    if l > 1:
                        pe.wait_ge(core["xr"], li + l - 1)
                    if l < L - 1:
                        per_head(2, lambda h: W(7)[:, h], lambda h: W(8)[:, h]).then_inc(core["d2"], 1)
                    per_head(1, lambda h: W(8)[:, h], lambda h: W(7)[:, h]).then_inc(core["d"], 1)
                    if not sample:
                        for part in {1: ["qk"], 2: ["vt"], 4: ["num"]}.get(l, []):
                            mlstm_part(t, part)
                pe.wait_ge(core["xr"], li + L - 1)
                if sample:
                    pe.wait_ge(states_loaded, 16 * HA)
                w = DECT

                def state(h, b):
                    return sg[:, h, b, :]

                if sample:
                    for h in range(HA):
                        for b in range(DECB):
                            both = qkv[:, h:h + HA + 1:HA, SEQ + b * w:SEQ + (b + 1) * w]
                            last = pe.matmul(state_products(h)[:, :, b * w:(b + 1) * w], state(h, b), both, start=True, stop=True)
                else:
                    last = per_head(3, lambda h: pS[:, h], lambda h: W(0)[:, h])
                last.then_inc(core["ks"], 1)
                pe.wait_ge(core["rT"], t + 1)
                for h in range(HA):
                    last = pe.transpose(bank(4)[:, h * P:(h + 1) * P], W(6)[:, h], ident[:])
                last.then_inc(core["rt"], 1)
                pe.wait_ge(core["rtok"], t + 1)
                per_head(5, lambda h: W(7)[:, h], lambda h: W(8)[:, h]).then_inc(core["u"], 1)
                if not sample:
                    token_rows(t + 1)
                pe.wait_ge(core["utok"], t + 1)
                if not sample:
                    for h in range(HA):
                        pe.matmul(bank(2)[:, h * P:(h + 1) * P], W(1)[:, h], W(5)[:, h], start=True, stop=False)
                        pe.matmul(bank(2)[:, h * P:(h + 1) * P], pS[:, h], q[:, h], start=False, stop=True)
                    per_head(3, lambda h: W(3)[:, h], lambda h: W(1)[:, h]).then_inc(core["o"], 1)
                    mlstm_part(t, "up1")
                else:
                    per_head(0, lambda h: W(1)[:, h], lambda h: W(5)[:, h]).then_inc(core["o"], 1)
                    for h in range(HA):
                        pe.wait_ge(core["uexp"], h + 1)
                        for c in range(2):
                            last = pe.matmul(ps[h % 2][:, c, :], W(3)[:, h], uexp(P, h)[:, c * 4:(c + 1) * 4, :], start=True, stop=True)
                        last.then_inc(core["sup"], 1)

            def mlstm_part(t, part):
                q, k, v = (qkv[:, a:a + HB, tile(t)] for a in (8, 12, 20))

                def state_update(b, h0):
                    for h in (h0, h0 + 1):
                        last = pe.matmul(bank(b)[:, (h - h0) * MW:(h - h0 + 1) * MW], V(6)[:, h], V8[:, 5, h * MW:(h + 1) * MW],
                                         start=True, stop=True)
                    return last

                if part == "gates":
                    if t:
                        pe.wait_ge(ml_dve, ml(ML_DVE, t - 1, "up1"))
                    spread(6, R2, 0, t)
                    last = pe.transpose(bank(7)[:, 0:P], R1[:, tile(t)], ident[:])
                elif part in ("qin", "floor", "kin"):
                    if part == "qin":
                        pe.wait_ge(ml_dve, ml(ML_DVE, t, "gates"))
                    else:
                        pe.wait_ge(ml_act, ml(ML_ACT, t, "qin" if part == "floor" else "floor"))
                    if part == "kin":
                        last = pe.transpose(bank(7)[:, 0:P], R2[:, tile(t)], ident[:])
                    else:
                        last = spread(7, R2, {"qin": 32, "floor": 64}[part], t)
                elif part == "qk":
                    last = per_head(6, lambda h: k[:, h], lambda h: q[:, h])
                elif part == "vt":
                    pe.wait_ge(ml_dve, ml(ML_DVE, t, "qk"))
                    for h in range(HB):
                        last = pe.transpose(bank(6)[:, h * P:(h + 1) * P], v[:, h], ident[:])
                elif part == "kt":
                    pe.wait_ge(ml_act, ml(ML_ACT, t, "vt"))
                    for h in range(HB):
                        last = pe.transpose(bank(6)[:, h * P:(h + 1) * P], k[:, h], ident[:])
                elif part == "num":
                    pe.wait_ge(ml_act, ml(ML_ACT, t, "kin"))
                    pe.wait_ge(ml_dve, ml(ML_DVE, t, "q"))
                    for h in range(HB):
                        pe.matmul(bank(7)[:, h * P:(h + 1) * P], V8[:, 5, h * MW:h * MW + P], V(3)[:, h], start=True, stop=False)
                        last = pe.matmul(bank(7)[:, h * P:(h + 1) * P], pC[:, h, 0:P], q[:, h], start=False, stop=True)
                elif part == "den":
                    pe.wait_ge(ml_act, ml(ML_ACT, t, "kt"))
                    for h in range(HB):
                        pe.matmul(bank(6)[:, h * P:(h + 1) * P], one[:].to_broadcast([P, P]), V(3)[:, h], start=True, stop=False)
                        last = pe.matmul(bank(6)[:, h * P:(h + 1) * P], pC[:, h, P:MW].to_broadcast([P, P]), q[:, h],
                                         start=False, stop=True)
                elif part == "up0":
                    pe.wait_ge(ml_act, ml(ML_ACT, t, "den"))
                    last = state_update(6, 0)
                else:
                    pe.wait_ge(ml_dve, ml(ML_DVE, t, "out"))
                    last = state_update(7, 2)
                last.then_inc(ml_pe, 1)

            def mlstm_sample():
                t = NTILE - 1
                q, k, v = (qkv[:, a:a + HB, tile(t)] for a in (8, 12, 20))
                spread(0, R2, 0, t)
                spread(1, R2, 32, t)
                spread(2, R2, 64, t)
                spread(3, R2, 96, t)
                pe.transpose(bank(4)[:, 0:P], R1[:, tile(t)], ident[:])
                per_head(5, lambda h: k[:, h], lambda h: q[:, h])
                for h in range(HB):
                    last = pe.transpose(bank(6)[:, h * P:(h + 1) * P], v[:, h], ident[:])
                last.then_inc(core["bcast"], 1)
                pe.wait_ge(core["kend"], 1)
                for h in range(HB):
                    last = pe.transpose(bank(0)[:, h * P:(h + 1) * P], W(4)[:, h], ident[:])
                last.then_inc(core["tr"], 1)
                pe.wait_ge(states_loaded, 16 * (HA + 2 * HB))
                w = DECT
                pe.wait_ge(core["vt"], 1)
                for h in range(HB):
                    hs = h * P
                    pe.matmul(bank(1)[:, hs:hs + P], W9[:, 5, h * MW:h * MW + P], W(3)[:, h], start=True, stop=False)
                    for b in range(DECB):
                        pe.matmul(bank(1)[:, hs + b * w:hs + (b + 1) * w], st[:, h, b, 0:P], q[:, h, b * w:(b + 1) * w],
                                  start=False, stop=(b == DECB - 1))
                pe.wait_ge(core["nq"], 1)
                for h in range(HB):
                    hs = h * P
                    pe.matmul(bank(2)[:, hs:hs + P], one[:].to_broadcast([P, P]), W(3)[:, h], start=True, stop=False)
                    last = pe.matmul(bank(2)[:, hs:hs + P], one[:].to_broadcast([P, P]), W(8)[:, h], start=False, stop=True)
                last.then_inc(core["np"], 1)
                pe.wait_ge(core["ktok"], 1)
                for h in range(HB):
                    pe.wait_ge(core["uexp"], HA + h + 1)
                    for c, (a, b) in zip(UPBANKS[h % 2], UPCUTS):
                        last = pe.matmul(bank(c)[:, 0:(b - a) * MW], W(6)[:, h], uexp(MW, h)[:, a:b, :], start=True, stop=True)
                    last.then_inc(core["sup"], 1)

            pe.wait_ge(ident_ready, 1)
            for s in stages:
                kind = s["kind"]
                if kind == "load":
                    pe.wait_ge(in_loaded[1], 6 * 16)
                    tposes(s["vec"], [(0, 0, vstage[0:NV1, 0, :]), (1, 0, vstage[0:NV2, 1, :])])
                    for q, j in enumerate(s["x"]):
                        pe.wait_ge(in_loaded[5 * (q // (KD // 2))], 2 * 16)
                        tposes(j, [(t // 4, t % 4 * P, xstage[:, t, q * P:(q + 1) * P]) for t in range(NTILE)])
                    pe.wait_ge(in_loaded[2], 2 * 16)
                    tposes(s["cs"], [(0, b * DECB * CA, castage[0:DECB * CA, b * P:(b + 1) * P]) for b in range(NA)] +
                           [(1, b * DECB * CC, ccstage[0:DECB * CC, b * P:(b + 1) * P]) for b in range(KD)])
                elif kind == "gu":
                    n0, count, lead = s["n0"], 2 * s["count"], 4
                    for u in range(lead):
                        mm(n0 + u, xh, xl, first=(xg_ready, 8 * s["prod"]) if u == 0 and s["first"] else None)
                        if u == 0 and s["norm"] is not None:
                            norm_job(s)
                    with pe.Fori(0, (count - lead) // 4) as i:
                        for u in range(4):
                            mm(n0 + lead + u, xh, xl, turn=i)
                elif kind == "down":
                    for o in range(KD):
                        mm(s["n0"] + o, hh, hl, first=(h_ready, s["hbase"]) if o == 0 else None)
                        if o == 0 and "pT" in s:
                            pe.wait_ge(p_loaded, 32 * (s["layer"] + 1))
                            for q, j in enumerate(s["pT"]):
                                tposes(j, [(t // 4, t % 4 * P, pstage[:, t, q * P:(q + 1) * P]) for t in range(NTILE)])
                elif kind == "even_in":
                    n = s["n0"]
                    for b in range(NA):
                        mm(n + b, xh, xl, first=(xg_ready, 8 * s["prod"]) if b == 0 else None)
                        if b == 0:
                            norm_job(s)
                    mm(n + NA, xh, xl)
                    pe.wait_ge(coll_ready, 1)
                    for j, first, last in ((s["coll"][0], 0, 8), (s["coll"][1], 8, NA)):
                        tposes(j, [((b - first) // 4, b % 4 * P, cacoll[:, b, :]) for b in range(first, last)])
                    for b in range(NA):
                        mm(n + NA + 1 + b, xh, xl)
                        if b >= HN_LAG:
                            q = b - HN_LAG
                            pe.wait_ge(hn_sq, s["hn0"] + q + 1)
                            sum_job(s["l2"][q], [sq, ut][q % 2])
                elif kind == "core":
                    drain(s)
                    pe.wait_ge(rows_ready, 1)
                    for t in range(NTILE):
                        delta_tile(t)
                elif kind == "mlstm_sample":
                    drain(s)
                    mlstm_sample()
                    pe.wait_ge(core["up"], NTILE + 1)
                    pe.transpose(bank(0)[0:HB, 0:P], pC[:, :, P], ident[:])
                    for h in range(HB):
                        last = pe.transpose(bank(1)[0:DECB, h * P:(h + 1) * P], st[:, h, :, P], ident[:])
                    last.then_inc(core["tr"], 1)
                elif kind == "even_z":
                    if s["first"] == 0:
                        pe.wait_ge(core["up"], NTILE)
                    else:
                        pe.wait_ge(states_done, 1)
                    for q, j in enumerate(s["onorm"]):
                        pe.wait_ge([o_sq_act, o_sq_dve][q // 2], 2 * (s["first"] // HA) + q % 2 + 1)
                        sum_job(j, osq[q])
                    for q in range(HA):
                        mm(s["n0"] + q, xh, xl)
                elif kind == "ple":
                    pe.wait_ge(h_ready, s["hbase"] + KP)
                    for o in range(KD):
                        mm(s["n0"] + o, hh[:, PH:PH + KP, :], hl[:, PH:PH + KP, :])
                    for o in range(KD):
                        mm(s["n0"] + KD + o, xh, xl, first=(xg_ready, 8 * s["prod"]) if o == 0 else None)
                        if o == 0:
                            norm_job(s)
                        if s["y"] and o >= Y_LAG:
                            y_job(s, o - Y_LAG)
                    if s["y"]:
                        for q in range(KD - Y_LAG, KD):
                            y_job(s, q)
                elif kind == "odd_in":
                    n = s["n0"]
                    for b in range(2 * KD):
                        mm(n + b, xh, xl, first=(xg_ready, 8 * s["prod"]) if b == 0 else None)
                        if b == 0:
                            norm_job(s)
                    for b in range(KD):
                        mm(n + 2 * KD + b, xh, xl)
                        if b == 0:
                            pe.wait_ge(coll_ready, 2)
                            tposes(s["coll"][0], [(b // 4, b % 4 * P, cccoll[:, b, :]) for b in range(KD)])
                elif kind == "final":
                    pe.wait_ge(xg_ready, 8 * s["prod"] + 8)
                    wait_slot(s["norm"])
                    for t in range(NTILE):
                        last = pe.matmul(ps[s["norm"] % 4][:, 0, t:t + 1], sumsq[:, tile(t)], one[:], start=True, stop=True)
                    last.then_inc(job_done, 1)

        @block.scalar
        def _(act):
            own = Tally(act)

            def prep(n, turn=None):
                if n >= NB:
                    return
                kt = blocks[n][1]
                act.wait_ge(raw_loaded[n % 4], turns(16 * (n // 4 + 1), turn, 16))
                if n >= 2:
                    act.wait_ge(job_done, turns(block_job[n - 2] + 1, turn, 4))
                if blocks[n][0][0] is None:
                    act.wait_ge(in_loaded[4], 2 * 16)
                    act.copy(whi[:, n % 2].rearrange("p k (q c) -> p k q c", q=4)[:, :, :, 0:4],
                             wg[:].rearrange("p k (q c) -> p k q c", q=4)).then_inc(hi_ready, 1)
                else:
                    act.copy(whi[:, n % 2, 0:kt, :], raw[:, n % 4, 0:kt, :]).then_inc(hi_ready, 1)

            def x_high(j, g):
                act.activation(xh[:, j, :], x[:, j, :], ACT.Copy, scale=vec1[:, g + j:g + j + 1]).then_inc(xg_hi, 1)

            def produce(p, j, g, ready=x_new, later=False):
                act.wait_ge(ready, 8 * (p - 1) + j + 1 if ready is x_new else j + 1)
                act.activation([sq, stt][j % 2][:], x[:, j, :], ACT.Square).then_inc(sq_ready, 1)
                if g is not None and not later:
                    x_high(j, g)
                elif g is None:
                    act.activation(yg[:, j, :], x[:, j, :], ACT.Copy, scale=vec1[:, DEPTH * 4 * KD + j:DEPTH * 4 * KD + j + 1]).then_inc(y_in, 1)

            def y_copy(s, q):
                j = s["y"][q]
                act.wait_ge(job_done, j + 1)
                own(act.copy(ystage[:, 0:4, q * P:(q + 1) * P], ps[j % 4][:, 0, :].rearrange("p (t c) -> p t c", c=P)).then_inc(act_own, 1), act_own)
                own(act.copy(ystage[:, 4, q * P:(q + 1) * P], ps[j % 4][:, 1, 0:P]).then_inc(y_copied, 1), y_copied)
                act.sem_inc(slot_free[j % 4], 1)

            def norm_root(s):
                j = s["norm"]
                act.wait_ge(job_done, j + 1)
                own(act.activation(halves(r[:]), ps[j % 4][:, :, 0:HT], ACT.Sqrt, scale=1.0 / D, bias=eps[:]).then_inc(root_ready, 1), root_ready)
                act.sem_inc(slot_free[j % 4], 1)

            def head_squares(s, q, jobs_, piece):
                if q >= 2:
                    act.wait_ge(job_done, jobs_[q - 2] + 1)
                act.activation([sq, ut][q % 2][:], piece, ACT.Square).then_inc(hn_sq, 1)

            def head_root(s, q, j, scale):
                act.wait_ge(job_done, j + 1)
                if q >= 1:
                    act.wait_ge(hn_used, s["hn0"] + q)
                own(act.activation(halves(root[:]), ps[j % 4][:, :, 0:HT], ACT.Sqrt, scale=scale, bias=eps[:]).then_inc(hn_root, 1), hn_root)
                act.sem_inc(slot_free[j % 4], 1)

            def mlstm_part(t, part):
                if part == "gates":
                    act.wait_ge(ml_dve, ml(ML_DVE, t, "gates"))
                else:
                    act.wait_ge(ml_pe, ml(ML_PE, t, part))
                if part == "gates":
                    last = act.activation(V(0), V(0), ACT.Exp)
                elif part in ("qin", "floor"):
                    last = act.activation(V({"qin": 1, "floor": 2}[part]), heads(7), ACT.Exp)
                elif part == "kin":
                    last = act.activation(kcol[:, 0:4], bank(7)[:, 96:96 + HB], ACT.Exp)
                elif part == "vt":
                    last = act.copy(V8[:, 5, :].rearrange("p (h c) -> p h c", h=HB)[:, :, 0:P], heads(6))
                elif part == "kt":
                    act.wait_ge(ml_act, ml(ML_ACT, t, "kin"))
                    for h in range(HB):
                        last = act.activation(V(6)[:, h], heads(6)[:, h], ACT.Copy, scale=kcol[:, h:h + 1])
                else:
                    last = act.activation(V(7), heads(6), ACT.Abs)
                last.then_inc(ml_act, 1)

            for s in stages:
                kind = s["kind"]
                if kind == "load":
                    for q, j in enumerate(s["x"]):
                        act.wait_ge(job_done, j + 1)
                        own(act.copy(x[:, q, 0:SEQ], ps[j % 4][:, 0, :]).then_inc(act_own, 1), act_own)
                        own(act.copy(x[:, q, SEQ:T], ps[j % 4][:, 1, 0:P]).then_inc(x_copied, 1), x_copied)
                        act.sem_inc(slot_free[j % 4], 1)
                        if q == 0:
                            act.wait_ge(vec_ready, 1)
                        if q >= 2:
                            act.wait_ge(xg_ready, q - 1)
                        produce(0, q, 0, x_copied)
                        if q in (4, 6):
                            prep(q // 2 - 2)
                elif kind == "gu":
                    n0, count, lead = s["n0"], 2 * s["count"], 4

                    def step(u, turn=None):
                        prep(n0 + u + 2, turn)
                        if u == 0 and s["norm"] is not None:
                            norm_root(s)
                        if u % 2 == 0:
                            act.wait_ge(gate_in, turns(s["act0"] + u // 2 + 1, turn, 2))
                            act.activation(stt[:], gt[:], ACT.Silu).then_inc(act_out, 1)

                    for u in range(lead):
                        step(u)
                    trips = (count - lead - 2) // 4
                    with act.Fori(0, trips) as i:
                        for u in range(4):
                            step(lead + u, i)
                    for u in range(lead + 4 * trips, count):
                        step(u)
                elif kind == "down":
                    for o in range(KD):
                        prep(s["n0"] + o + 2)
                        if s["last"]:
                            produce(s["prod"], o, s["g"])
                elif kind == "even_in":
                    n = s["n0"]
                    for b in range(NA):
                        prep(n + b + 2)
                        if b == 0:
                            norm_root(s)
                        act.wait_ge(conv_in, b + 1)
                        pos = s["pos"][b]
                        act.activation(qkv[:, pos, 0:SEQ], ct[:, 0:SEQ], ACT.Silu)
                        act.activation(qkv[:, pos, SEQ:T].rearrange("p (b t) -> p b t", t=DECT),
                                       ct[:, SEQ + CA:HISTA].rearrange("p (b t) -> p b t", t=DECT + CA)[:, :, 0:DECT],
                                       ACT.Silu).then_inc(conv_out, 1)
                    prep(n + NA + 2)
                    act.wait_ge(row_in, 1)
                    own(act.activation(R1[0:4, :], R1[0:4, :], ACT.Sigmoid).then_inc(act_own, 1), act_own)
                    own(act.activation(small[0:4, 4:5], small[0:4, 0:1], ACT.Exp).then_inc(act_own, 1), act_own)
                    for src, t1, t2, bias, sgn in ((dt_, hf_, sq_, small[0:4, 1:2], 1.0), (fg_, hi_, ct_, small[0:4, 5:6], -1.0)):
                        a, b_, c = src[0:4, 0:T], t1[0:4, 0:T], t2[0:4, 0:T]
                        own(act.activation(b_, a, ACT.Abs, bias=bias, scale=sgn).then_inc(act_own, 1), act_own)
                        own(act.activation(b_, b_, ACT.Exp, scale=-1.0).then_inc(act_own, 1), act_own)
                        own(act.activation(b_, b_, ACT.Ln, bias=1.0).then_inc(act_own, 1), act_own)
                        own(act.activation(c, a, ACT.Relu, bias=bias, scale=sgn).then_inc(row_act, 1), row_act)
                    for b in range(NA):
                        q = b - HN_LAG
                        if q >= 0:
                            if q == 0:
                                act.wait_ge(conv_out, NA)
                            head_squares(s, q, s["l2"], qkv[:, q, :])
                        prep(n + NA + 1 + b + 2)
                        if q >= 0:
                            head_root(s, q, s["l2"][q], 1.0)
                elif kind == "core":
                    for t in range(NTILE):
                        L = LVLS if t == NTILE - 1 else LVL
                        li, l2 = (LVL - 1) * t, (LVL - 2) * t
                        act.wait_ge(core["expin"], t + 1)
                        act.activation(W(1), W(1), ACT.Exp).then_inc(core["gam"], 1)
                        act.activation(W(2), heads(1), ACT.Exp)
                        act.activation(kcol[:, 4:8], gcols[:, GC - HA:GC], ACT.Exp).then_inc(core["eg"], 1)
                        for l in range(1, L):
                            act.wait_ge(core["m1"], li + l)
                            act.copy(W(8), heads(0)).then_inc(core["m1c"], 1)
                            if t < NTILE - 1:
                                for part in {1: ["gates", "qin"], 2: ["floor"], 3: ["vt", "kin"], 4: ["kt"], 5: ["den"]}.get(l, []):
                                    mlstm_part(t, part)
                        act.wait_ge(core["rt"], t + 1)
                        act.copy(W(8), heads(4)).then_inc(core["rtok"], 1)
                        act.wait_ge(core["u"], t + 1)
                        act.copy(W(1), heads(5)).then_inc(core["utok"], 1)
                elif kind == "mlstm_sample":
                    g = NTILE
                    act.wait_ge(core["bcast"], g + 1)
                    act.copy(W9[:, 5, :].rearrange("p (h c) -> p h c", h=HB)[:, :, 0:P], heads(6)).then_inc(core["vt"], 1)
                    act.wait_ge(core["expin"], g + 1)
                    act.activation(W(0), W(0), ACT.Exp).then_inc(core["gam"], 1)
                    act.activation(W(1), heads(1), ACT.Exp)
                    act.activation(W(2), heads(2), ACT.Exp)
                    act.activation(W(4), heads(3), ACT.Exp).then_inc(core["eg"], 1)
                    act.wait_ge(core["tr"], g + 1)
                    act.copy(W(6), heads(0)).then_inc(core["ktok"], 1)
                elif kind == "even_z":
                    if s["first"] == 0:
                        act.wait_ge(core["up"], NTILE)
                    else:
                        act.wait_ge(states_done, 1)
                    o0 = 16 + s["first"]
                    for q in range(2):
                        act.activation(osq[q][:], qkv[:, o0 + q, :], ACT.Square).then_inc(o_sq_act, 1)
                    for q, j in enumerate(s["onorm"]):
                        act.wait_ge(job_done, j + 1)
                        own(act.activation(halves(oroot[q][:]), ps[j % 4][:, :, 0:HT], ACT.Sqrt, scale=1.0 / P, bias=eps[:]).then_inc(hn_root, 1), hn_root)
                        act.sem_inc(slot_free[j % 4], 1)
                    if s["first"]:
                        for q in range(HA):
                            act.copy(hh[:, q, :], qkv[:, 16 + q, :]).then_inc(o_high, 1)
                    for q in range(HA):
                        prep(s["n0"] + q + 2)
                        act.wait_ge(gate_in, s["act0"] + q + 1)
                        act.activation(stt[:], gt[:], ACT.Sigmoid if s["first"] else ACT.Silu).then_inc(act_out, 1)
                elif kind == "ple":
                    for o in range(KD):
                        j = block_job[s["n0"] + o]
                        prep(s["n0"] + o + 2)
                        act.wait_ge(job_done, j + 1)
                        own(act.copy(halves(sig[:, o, :]), ps[j % 4][:, :, 0:HT]).then_inc(emb_copied, 1), emb_copied)
                        act.sem_inc(slot_free[j % 4], 1)
                    for o in range(KD):
                        prep(s["n0"] + KD + o + 2)
                        if o == 0:
                            norm_root(s)
                        act.wait_ge(gate_in, s["act0"] + o + 1)
                        act.activation(hf[:], gt[:], ACT.Sigmoid).then_inc(act_out, 1)
                        produce(s["next"], o, s["g"] if s["i"] + 1 < DEPTH else None, later=True)
                        if s["y"] and o > Y_LAG:
                            y_copy(s, o - Y_LAG - 1)
                    if s["y"]:
                        for q in range(KD - Y_LAG - 1, KD):
                            y_copy(s, q)
                    else:
                        act.wait_ge(job_done, block_job[s["n0"] + 2 * KD - 1] + 1)
                        for o in range(KD):
                            x_high(o, s["g"])
                elif kind == "odd_in":
                    for b in range(3 * KD):
                        prep(s["n0"] + b + 2)
                        if b == 0:
                            norm_root(s)
                elif kind == "final":
                    j = s["norm"]
                    act.wait_ge(job_done, j + 1)
                    act.activation(gcol[:, 0:NTILE], ps[j % 4][:, 0, 0:NTILE], ACT.Sqrt, scale=1.0 / D, bias=eps[:]).then_inc(col_root, 1)
                    act.wait_ge(y_dve, 1)
                    for t in range(1, NTILE, 2):
                        act.activation(ystage[:, t, :], ystage[:, t, :], ACT.Copy, scale=gcol[:, t:t + 1]).then_inc(y_act, 1)

        @block.vector
        def _(dve):
            own = Tally(dve)

            def o1(i):
                own(i.then_inc(dve_own, 1), dve_own)

            def mul(out, a, b):
                o1(dve.tensor_tensor(out, a, b, ALU.mult))

            def free(j):
                dve.sem_inc(slot_free[j % 4], 1)

            def P2(j):
                return ps[j % 4][:, :, 0:HT]

            def done(j, turn=None):
                dve.wait_ge(job_done, turns(j + 1, turn, 4))

            def x_low(p, j, g):
                dve.wait_ge(xg_hi, 8 * p + j + 1)
                own(dve.scalar_tensor_tensor(xl[:, j, :], x[:, j, :], vec1[:, g + j:g + j + 1], xh[:, j, :].bitcast(fp32),
                                             ALU.mult, ALU.subtract).then_inc(xg_ready, 1), xg_ready)

            def produce(p, j, g, later=False):
                dve.wait_ge(sq_ready, 8 * p + j + 1)
                src = [sq, stt][j % 2][:]
                if j == 0:
                    o1(dve.tensor_copy(sumsq[:], src))
                elif g is None:
                    own(dve.tensor_tensor(sumsq[:], sumsq[:], src, ALU.add).then_inc(xg_ready, 1), xg_ready)
                else:
                    o1(dve.tensor_tensor(sumsq[:], sumsq[:], src, ALU.add))
                if g is None:
                    if j == 0:
                        dve.sem_inc(xg_ready, 1)
                        own.counts[xg_ready.name] += 1
                    return
                if not later:
                    x_low(p, j, g)

            def norm_recip(s):
                dve.wait_ge(root_ready, own_norms[0] + 1)
                own_norms[0] += 1
                o1(dve.reciprocal(r[:], r[:]))

            own_norms = [0]

            def split_hidden(slot, turn=None, step=None):
                mul(hf[:], stt[:], ut[:])
                at_ = slice(slot, slot + 1) if turn is None else bass.ds(turn * step + slot, 1)
                o1(dve.tensor_tensor(hh[:, at_, :], stt[:].unsqueeze(1), ut[:].unsqueeze(1), ALU.mult))
                own(dve.tensor_tensor(hl[:, at_, :], hf[:].unsqueeze(1), hh[:, at_, :].bitcast(fp32), ALU.subtract).then_inc(h_ready, 1), h_ready)

            def head_norm(s, q, piece, scalar):
                dve.wait_ge(hn_root, s["hn0"] + q + 1)
                o1(dve.reciprocal(inv[:], root[:]))
                own(dve.scalar_tensor_tensor(piece, piece, scalar, inv[:], ALU.mult, ALU.mult).then_inc(hn_used, 1), hn_used)

            def delta_tile(t):
                sample = t == NTILE - 1
                L = LVLS if sample else LVL
                li, l2 = (LVL - 1) * t, (LVL - 2) * t
                z = slice(t * P, (t + 1) * P)
                q, k, v = (qkv[:, a:a + HA, z] for a in (0, 4, 16))
                over_heads = lambda m: m.unsqueeze(1).to_broadcast([P, HA, P])
                dve.wait_ge(core["bcast"], t + 1)
                o1(dve.tensor_copy(gcols[:], bank(4)[:, 32:32 + GC]))
                for h in range(HA):
                    sm = core["expin"] if h == HA - 1 else dve_own
                    own(dve.tensor_scalar(W(1)[:, h], heads(1)[:, h], gcols[:, h:h + 1], 0.0, ALU.subtract, ALU.min).then_inc(sm, 1), sm)
                own(dve.tensor_tensor(W(0), k, heads(0), ALU.mult).then_inc(core["prod"], 1), core["prod"])
                mul(v, v, heads(0))
                if t:
                    o1(dve.tensor_copy(qkv[:, 16:16 + HA, (t - 1) * P:t * P], heads(2)))
                    mlstm_part(t - 1, "up1")
                dve.wait_ge(core["gam"], t + 1)
                mul(W(1), W(1), over_heads(incl[:, 1 if sample else 0, :]))
                dve.wait_ge(core["kk"], t + 1)
                mul(W(4), heads(4), W(1))
                own(dve.tensor_tensor(W(7), W(4), over_heads(level[:, 0, :]), ALU.mult).then_inc(core["c0"], 1), core["c0"])
                dve.wait_ge(core["np"], t + 1)
                mul(W(5), heads(3), W(1))
                dve.wait_ge(core["tr"], t + 1)
                own(dve.tensor_tensor(W(6), over_heads(ident[:]), heads(4), ALU.subtract).then_inc(core["x0"], 1), core["x0"])

                def masked(l):
                    own(dve.tensor_tensor(W(1), W(4), over_heads(level[:, l, :]), ALU.mult).then_inc(core["ctl"], 1), core["ctl"])

                masked(1)
                own(dve.tensor_tensor(W(7), over_heads(ident[:]), W(7), ALU.subtract).then_inc(core["xt0"], 1), core["xt0"])
                dve.wait_ge(core["eg"], t + 1)
                if not sample:
                    mul(W(0), W(0), W(2))
                if not sample:
                    mlstm_part(t, "gates")
                for l in range(1, L):
                    if l < L - 1:
                        dve.wait_ge(core["m1c"], li + l)
                        masked(l + 1)
                        dve.wait_ge(core["d2"], l2 + l)
                        own(dve.tensor_tensor(W(6), W(6), heads(2), ALU.subtract).then_inc(core["x6"], 1), core["x6"])
                    dve.wait_ge(core["d"], li + l)
                    own(dve.tensor_tensor(W(7), W(7), heads(1), ALU.subtract).then_inc(core["xr"], 1), core["xr"])
                    if l == 1:
                        dve.wait_ge(core["ktr"], t + 1)
                        o1(dve.tensor_tensor(W(3), heads(5), kcol[:, 4:8].unsqueeze(2).to_broadcast([P, HA, P]), ALU.mult))
                        if sample:
                            mul(k, W(0), W(2))
                    if l == 2:
                        mul(q, q, W(2))
                    if not sample:
                        for part in {1: ["qk"], 2: ["q"]}.get(l, []):
                            mlstm_part(t, part)
                dve.wait_ge(core["ks"], t + 1)
                if sample:
                    for h in range(HA):
                        sm = core["rT"] if h == HA - 1 else dve_own
                        own(dve.tensor_tensor(W(6)[:, h], v[:, h], state_products(h)[:, 1], ALU.subtract).then_inc(sm, 1), sm)
                    for h in range(HA):
                        o1(dve.tensor_copy(W(4)[:, h], state_products(h)[:, 0]))
                else:
                    own(dve.tensor_tensor(W(6), v, heads(3), ALU.subtract).then_inc(core["rT"], 1), core["rT"])
                if not sample:
                    mlstm_part(t, "out")
                    mlstm_part(t, "up0")
                dve.wait_ge(core["o"], t + 1)
                if sample:
                    o1(dve.tensor_tensor(v, W(4), heads(0), ALU.add))
                if not sample:
                    for h in range(HA):
                        sm = core["up"] if h == HA - 1 else dve_own
                        own(dve.scalar_tensor_tensor(pS[:, h], pS[:, h], W(2)[:, h, P - 1:P], heads(3)[:, h], ALU.mult, ALU.add).then_inc(sm, 1), sm)
                    return

                def apart(h):
                    own(dve.tensor_tensor(uexp(P, h), W(1)[:, h].unsqueeze(1).to_broadcast([P, DECB, P]),
                                          bmask[:].unsqueeze(2).to_broadcast([P, DECB, P]), ALU.mult).then_inc(core["uexp"], 1), core["uexp"])

                apart(0)
                for h in range(HA):
                    if h + 1 < HA:
                        apart(h + 1)
                    dve.wait_ge(core["decay"], h + 1)
                    dve.wait_ge(core["sup"], h + 1)
                    for c in range(2):
                        sm = core["up"] if h == HA - 1 and c else dve_own
                        own(dve.tensor_tensor(sg[:, h, 4 * c:4 * c + 4], sg[:, h, 4 * c:4 * c + 4],
                                              ps[h % 2][:, c, :].rearrange("p (b v) -> p b v", v=P), ALU.add).then_inc(sm, 1), sm)

            def mlstm_part(t, part):
                z = slice(t * P, (t + 1) * P)
                q, k, v = (qkv[:, a:a + HB, z] for a in (8, 12, 20))
                scale = float(DK) ** -0.5
                if part == "gates":
                    dve.wait_ge(ml_pe, ml(ML_PE, t, "gates"))
                    o1(dve.tensor_copy(gcol[:, 4:8], bank(7)[:, 96:100]))
                    for h in range(HB):
                        sm = ml_dve if h == HB - 1 else dve_own
                        own(dve.tensor_scalar(V(0)[:, h], heads(6)[:, h], gcol[:, 4 + h:5 + h], 0.0, ALU.add, ALU.min).then_inc(sm, 1), sm)
                elif part == "qk":
                    dve.wait_ge(ml_act, ml(ML_ACT, t, "gates"))
                    mul(V(0), V(0), incl[:, 0, :].unsqueeze(1).to_broadcast([P, HB, P]))
                    dve.wait_ge(ml_pe, ml(ML_PE, t, "qk"))
                    own(dve.scalar_tensor_tensor(V(3), heads(6), scale, V(0), ALU.mult, ALU.mult).then_inc(ml_dve, 1), ml_dve)
                elif part == "q":
                    dve.wait_ge(ml_act, ml(ML_ACT, t, "qin"))
                    o1(dve.memset(V8[:, 5, :].rearrange("p (h c) -> p h c", h=HB)[:, :, P:MW], 1.0))
                    own(dve.scalar_tensor_tensor(q, q, scale, V(1), ALU.mult, ALU.mult).then_inc(ml_dve, 1), ml_dve)
                elif part == "out":
                    dve.wait_ge(ml_act, ml(ML_ACT, t, "den"))
                    o1(dve.tensor_tensor(V(7), V(7), V(2), ALU.max))
                    o1(dve.reciprocal(V(7), V(7)))
                    own(dve.tensor_tensor(v, heads(7), V(7), ALU.mult).then_inc(ml_dve, 1), ml_dve)
                else:
                    dve.wait_ge(ml_pe, ml(ML_PE, t, part))
                    b, h0 = (6, 0) if part == "up0" else (7, 2)
                    for h in (h0, h0 + 1):
                        sm = dve_own if h == h0 else ml_dve
                        own(dve.scalar_tensor_tensor(pC[:, h], pC[:, h], V(1)[:, h, P - 1:P], bank(b)[:, (h - h0) * MW:(h - h0 + 1) * MW],
                                                     ALU.mult, ALU.add).then_inc(sm, 1), sm)

            def mlstm_sample():
                z = slice(SEQ, T)
                q, k, v = (qkv[:, a:a + HB, z] for a in (8, 12, 20))
                scale = float(DK) ** -0.5
                dve.wait_ge(core["bcast"], NTILE + 1)
                o1(dve.tensor_copy(gcol[:, 4:8], bank(4)[:, 96:100]))
                for h in range(HB):
                    sm = core["expin"] if h == HB - 1 else dve_own
                    own(dve.tensor_scalar(W(0)[:, h], heads(0)[:, h], gcol[:, 4 + h:5 + h], 0.0, ALU.add, ALU.min).then_inc(sm, 1), sm)
                dve.wait_ge(core["gam"], NTILE + 1)
                mul(W(0), W(0), incl[:, 1, :].unsqueeze(1).to_broadcast([P, HB, P]))
                o1(dve.scalar_tensor_tensor(W(3), heads(5), scale, W(0), ALU.mult, ALU.mult))
                dve.wait_ge(core["eg"], NTILE + 1)
                o1(dve.scalar_tensor_tensor(q, q, scale, W(1), ALU.mult, ALU.mult))
                o1(dve.memset(W9[:, 5, :].rearrange("p (h c) -> p h c", h=HB)[:, :, P:MW], 1.0))
                own(dve.tensor_tensor(W(4), W(4), k, ALU.mult).then_inc(core["kend"], 1), core["kend"])
                for h in range(HB):
                    sm = core["nq"] if h == HB - 1 else dve_own
                    own(dve.tensor_tensor(W(8)[:, h].rearrange("p (b t) -> p b t", t=DECT), q[:, h].rearrange("p (b t) -> p b t", t=DECT),
                                          st[:, h, :, P:MW].to_broadcast([P, DECB, DECT]), ALU.mult).then_inc(sm, 1), sm)
                def apart(h):
                    own(dve.tensor_tensor(uexp(MW, h), W9[:, 5, h * MW:(h + 1) * MW].unsqueeze(1).to_broadcast([P, DECB, MW]),
                                          bmask[:].unsqueeze(2).to_broadcast([P, DECB, MW]), ALU.mult).then_inc(core["uexp"], 1), core["uexp"])

                dve.wait_ge(core["np"], NTILE + 1)
                apart(0)
                o1(dve.tensor_scalar(W(0), heads(2), -1.0, None, ALU.mult))
                o1(dve.tensor_tensor(W(0), W(0), heads(2), ALU.max))
                o1(dve.tensor_tensor(W(0), W(0), W(2), ALU.max))
                apart(1)
                o1(dve.reciprocal(W(0), W(0)))
                mul(v, heads(1), W(0))
                for h in range(HB):
                    dve.wait_ge(core["decay"], HA + h + 1)
                    dve.wait_ge(core["sup"], HA + h + 1)
                    for c, (a, b) in zip(UPBANKS[h % 2], UPCUTS):
                        sm = core["up"] if h == HB - 1 and b == DECB else dve_own
                        own(dve.tensor_tensor(st[:, h, a:b], st[:, h, a:b],
                                              bank(c)[:, 0:(b - a) * MW].rearrange("p (b v) -> p b v", v=MW), ALU.add).then_inc(sm, 1), sm)
                    if h + 2 < HB:
                        apart(h + 2)

            o1(dve.memset(eps[:], EPS))
            o1(dve.memset(pS[:], 0.0))
            o1(dve.memset(pC[:], 0.0))
            dve.wait_ge(pool_consts, 1)
            for s in stages:
                kind = s["kind"]
                if kind == "load":
                    j = s["vec"]
                    done(j)
                    o1(dve.tensor_copy(vec1[:], ps[j % 4][:, 0, 0:NV1]))
                    o1(dve.tensor_copy(vec2[:], ps[j % 4][:, 1, 0:NV2]))
                    free(j)
                    dve.sem_inc(vec_ready, 1)
                    for q in range(KD):
                        produce(0, q, 0)
                    j = s["cs"]
                    done(j)
                    o1(dve.tensor_copy(castate[:].rearrange("p a b -> p (a b)"), ps[j % 4][:, 0, 0:NA * DECB * CA]))
                    o1(dve.tensor_copy(ccstate[:].rearrange("p a b -> p (a b)"), ps[j % 4][:, 1, 0:KD * DECB * CC]))
                    free(j)
                elif kind == "gu":
                    n0, lead = s["n0"], 4

                    def pair(q, turn=None):
                        ja, jb = block_job[n0 + 2 * q], block_job[n0 + 2 * q + 1]
                        if q == 0 and s["norm"] is not None:
                            norm_recip(s)
                        done(ja, turn)
                        own(dve.tensor_tensor(halves(gt[:]), P2(ja), halves(r[:]), ALU.mult).then_inc(gate_in, 1), gate_in)
                        free(ja)
                        done(jb, turn)
                        mul(halves(ut[:]), P2(jb), halves(r[:]))
                        free(jb)
                        dve.wait_ge(act_out, turns(s["act0"] + q + 1, turn, 2))
                        split_hidden(q, turn, 2)

                    pair(0)
                    pair(1)
                    trips = (s["count"] - 2) // 2
                    with dve.Fori(0, trips) as i:
                        own.enter(i, {gate_in: 2, dve_own: 6, h_ready: 2})
                        pair(2, i)
                        pair(3, i)
                    own.leave(trips)
                elif kind == "down":
                    for o in range(KD):
                        j = block_job[s["n0"] + o]
                        done(j)
                        sm = x_new if s["last"] else dve_own
                        own(dve.scalar_tensor_tensor(halves(x[:, o, :]), P2(j), s["scale"], halves(x[:, o, :]),
                                                     ALU.mult, ALU.add).then_inc(sm, 1), sm)
                        free(j)
                        if s["last"]:
                            produce(s["prod"], o, s["g"])
                        if o == 0 and "pT" in s:
                            for q, j in enumerate(s["pT"]):
                                done(j)
                                for c, z in ((0, slice(0, SEQ)), (1, slice(SEQ, T))):
                                    w = z.stop - z.start
                                    o1(dve.tensor_copy(hh[:, PH + q, z], ps[j % 4][:, c, 0:w]))
                                    sm = h_ready if c else dve_own
                                    own(dve.tensor_tensor(hl[:, PH + q, z], ps[j % 4][:, c, 0:w], hh[:, PH + q, z].bitcast(fp32),
                                                          ALU.subtract).then_inc(sm, 1), sm)
                                free(j)
                elif kind == "even_in":
                    n = s["n0"]
                    NR = CA + DECB * CA
                    hs = hist[:, SEQ + CA:HISTA].rearrange("p (b t) -> p b t", t=DECT + CA)
                    o1(dve.memset(hist[:, 0:CA], 0.0))
                    for b in range(NA):
                        j = block_job[n + b]
                        if b == 0:
                            norm_recip(s)
                        done(j)
                        p_ = ps[j % 4]
                        mul(hist[:, CA:CA + HT], p_[:, 0, 0:HT], r[:, 0:HT])
                        mul(hist[:, CA + HT:CA + SEQ], p_[:, 1, 0:SEQ - HT], r[:, HT:SEQ])
                        mul(hs[:, :, CA:], p_[:, 1, SEQ - HT:HT].rearrange("p (b t) -> p b t", t=DECT),
                            r[:, SEQ:T].rearrange("p (b t) -> p b t", t=DECT))
                        free(j)
                        o1(dve.tensor_copy(hs[:, :, 0:CA], castate[:, b, :].rearrange("p (b t) -> p b t", t=CA)))
                        o1(dve.tensor_copy(cacoll[:, b, 0:CA], hist[:, SEQ:SEQ + CA]))
                        sm = coll_ready if b == NA - 1 else dve_own
                        own(dve.tensor_copy(cacoll[:, b, CA:].rearrange("p (b t) -> p b t", t=CA), hs[:, :, DECT:]).then_inc(sm, 1), sm)
                        C = HISTA - CA
                        if b:
                            dve.wait_ge(conv_out, b)
                        o1(dve.tensor_scalar(ct[:, 0:C], hist[:, 0:C], vec2[:, b:b + 1], None, ALU.mult))
                        for w in range(1, KA):
                            sm = conv_in if w == KA - 1 else dve_own
                            own(dve.scalar_tensor_tensor(ct[:, 0:C], hist[:, w:w + C], vec2[:, w * NA + b:w * NA + b + 1],
                                                         ct[:, 0:C], ALU.mult, ALU.add).then_inc(sm, 1), sm)
                    dve.wait_ge(conv_out, NA)
                    j = block_job[n + NA]
                    done(j)
                    for q, dst in enumerate((R1, dt_, ig_, fg_)):
                        mul(halves(dst[0:4, :]), ps[j % 4][32 * q:32 * q + 4, :, 0:HT], halves(r[32 * q:32 * q + 4, :]))
                    free(j)
                    dve.wait_ge(in_loaded[3], 5 * 16)
                    own(dve.tensor_scalar(small[0:4, 5:6], small[0:4, 3:4], -1.0, None, ALU.mult).then_inc(row_in, 1), row_in)
                    for j, a, b in ((s["coll"][0], 0, 8), (s["coll"][1], 8, NA)):
                        done(j)
                        for c in range((b - a) // 4):
                            sm = dve_own
                            last = dve.tensor_copy(castout[0:NR, (a + 4 * c) * P:(a + 4 * c + 4) * P], ps[j % 4][0:NR, c, :])
                            if b == NA:
                                own(last.then_inc(coll_out, 1), coll_out)
                            else:
                                o1(last)
                        free(j)
                    reset = sumsq[0:4, :]
                    R = lambda t_: t_[0:4, 0:T]
                    NP = SEQ // P

                    def seg(row, last=False):
                        a = row[:, 0:SEQ].rearrange("p (c t) -> p c t", t=P)
                        b = row[:, SEQ:T].rearrange("p (c t) -> p c t", t=DECT)
                        return (a[:, :, P - 1:P], b[:, :, DECT - 1:DECT]) if last else (a, b)

                    def resets():
                        o1(dve.memset(R2[:], 0.0))
                        o1(dve.memset(reset, 1.0))
                        o1(dve.memset(reset[:, 0:SEQ].rearrange("p (c t) -> p c t", t=P)[:, :, 0:1], 0.0))
                        o1(dve.memset(reset[:, SEQ:T].rearrange("p (c t) -> p c t", t=DECT)[:, :, 0:1], 0.0))

                    def decay_rows():
                        dve.wait_ge(row_act, 1)
                        o1(dve.tensor_scalar(small[0:4, 6:7], small[0:4, 4:5], -1.0, None, ALU.mult))
                        o1(dve.tensor_tensor(R(hf_), R(hf_), R(sq_), ALU.add))
                        o1(dve.tensor_scalar(R(dt_), R(hf_), small[0:4, 6:7], None, ALU.mult))
                        o1(dve.tensor_tensor_scan(R(hf_), reset, R(dt_), 0.0, ALU.mult, ALU.add))
                        o1(dve.tensor_copy(R1[32:36, :], R(hf_)))
                        for dst, row, end in zip(seg(R1[64:68, :]), seg(R(hf_)), seg(R(hf_), True)):
                            o1(dve.tensor_tensor(dst, end.to_broadcast(row.shape), row, ALU.subtract))

                    def forget_rows():
                        dve.wait_ge(row_act, 2)
                        o1(dve.scalar_tensor_tensor(R(fg_), R(hi_), -1.0, R(ct_), ALU.mult, ALU.subtract))
                        o1(dve.tensor_scalar(R(ig_), R(ig_), small[0:4, 2:3], None, ALU.add))
                        o1(dve.tensor_tensor_scan(R(sq_), reset, R(fg_), 0.0, ALU.mult, ALU.add))
                        o1(dve.tensor_tensor_scan(ct_[0:4, 0:SEQ], fg_[0:4, 0:SEQ], ig_[0:4, 0:SEQ], 0.0, ALU.add, ALU.max))
                        for b in range(DECB):
                            z = slice(SEQ + b * DECT, SEQ + (b + 1) * DECT)
                            o1(dve.tensor_tensor_scan(ct_[0:4, z], fg_[0:4, z], ig_[0:4, z], m0[0:4, b:b + 1], ALU.add, ALU.max))

                    def maximum_rows():
                        o1(dve.memset(minr[:, 0:1], 0.0))
                        o1(dve.tensor_copy(minr[:, 1:NP].unsqueeze(2), seg(R(ct_), True)[0][:, 0:NP - 1]))
                        o1(dve.tensor_copy(minr[:, NP:NSEG], m0[:, :]))
                        o1(dve.tensor_copy(mfin[:, 0:1], ct_[0:4, SEQ - 1:SEQ]))
                        own(dve.tensor_copy(mfin[:, 1:].unsqueeze(2), seg(R(ct_), True)[1]).then_inc(m_final, 1), m_final)
                        o1(dve.tensor_tensor(R2[0:4, :], R(sq_), R(ct_), ALU.subtract))
                        for dst, row, m_ in zip(seg(R2[32:36, :]), seg(R2[0:4, :]), (minr[:, 0:NP], minr[:, NP:NSEG])):
                            o1(dve.tensor_tensor(dst, row, m_.unsqueeze(2).to_broadcast(row.shape), ALU.add))

                    def key_rows():
                        o1(dve.tensor_scalar(R2[64:68, :], R(ct_), -1.0, None, ALU.mult))
                        o1(dve.tensor_tensor(R(hf_), R(ig_), R(sq_), ALU.subtract))
                        o1(dve.tensor_copy(R1[96:100, :], R(hf_)))
                        for dst, row, end in zip(seg(R2[96:100, :]), seg(R(hf_)), seg(R2[0:4, :], True)):
                            o1(dve.tensor_tensor(dst, row, end.to_broadcast(row.shape), ALU.add))
                        dve.sem_inc(rows_ready, 1)

                    row_steps = [resets, decay_rows, forget_rows, maximum_rows, key_rows]
                    assert len(row_steps) <= NA - 4
                    for b in range(NA):
                        j = block_job[n + NA + 1 + b]
                        done(j)
                        mul(halves(qkv[:, s["pos"][NA + b], :]), P2(j), halves(r[:]))
                        free(j)
                        if b < len(row_steps):
                            row_steps[b]()
                        q = b - HN_LAG
                        if q >= 0:
                            head_norm(s, q, qkv[:, q, :], float(DK) ** -0.5 if q < HA else 1.0)
                elif kind == "core":
                    dve.wait_ge(out_stored, 4 * 16)
                    for t in range(NTILE):
                        delta_tile(t)
                elif kind == "mlstm_sample":
                    dve.wait_ge(states_loaded, 16 * (HA + 2 * HB))
                    mlstm_sample()
                    dve.wait_ge(core["tr"], NTILE + 2)
                    o1(dve.tensor_copy(nout[0:HB, 0:P], bank(0)[0:HB, 0:P]))
                    own(dve.tensor_copy(nout[0:DECB, P:], bank(1)[0:DECB, :]).then_inc(states_done, 1), states_done)
                elif kind == "even_z":
                    c1 = NV2 - 1 - HB
                    for q in range(2, HA):
                        own(dve.tensor_tensor(osq[q][:], qkv[:, 16 + s["first"] + q, :], qkv[:, 16 + s["first"] + q, :],
                                              ALU.mult).then_inc(o_sq_dve, 1), o_sq_dve)

                    def normalise(q):
                        dve.wait_ge(hn_root, s["hn0"] + q + 1)
                        o1(dve.reciprocal(oroot[q][:], oroot[q][:]))
                        o = qkv[:, 16 + s["first"] + q, :]
                        w_ = vec2[:, c1 + q:c1 + q + 1] if s["first"] else vec2[:, NV2 - 1:NV2]
                        o1(dve.scalar_tensor_tensor(o, o, w_, oroot[q][:], ALU.mult, ALU.mult))

                    normalise(0)
                    if s["first"]:
                        for q in range(HA):
                            dve.wait_ge(o_high, q + 1)
                            own(dve.tensor_tensor(hl[:, q, :], qkv[:, 16 + q, :], hh[:, q, :].bitcast(fp32), ALU.subtract).then_inc(h_ready, 1), h_ready)
                    for q in range(HA):
                        if q + 1 < HA:
                            normalise(q + 1)
                        o = qkv[:, 16 + s["first"] + q, :]
                        j = block_job[s["n0"] + q]
                        done(j)
                        own(dve.tensor_tensor(halves(gt[:]), P2(j), halves(r[:]), ALU.mult).then_inc(gate_in, 1), gate_in)
                        free(j)
                        dve.wait_ge(act_out, s["act0"] + q + 1)
                        if s["first"] == 0:
                            mul(o, stt[:], o)
                            continue
                        q += HA
                        mul(ut[:], stt[:], o)
                        o1(dve.tensor_tensor(hh[:, q, :], stt[:], o, ALU.mult))
                        own(dve.tensor_tensor(hl[:, q, :], ut[:], hh[:, q, :].bitcast(fp32), ALU.subtract).then_inc(h_ready, 1), h_ready)
                elif kind == "ple":
                    for o in range(KD):
                        j = block_job[s["n0"] + KD + o]
                        if o == 0:
                            norm_recip(s)
                        done(j)
                        own(dve.tensor_tensor(halves(gt[:]), P2(j), halves(r[:]), ALU.mult).then_inc(gate_in, 1), gate_in)
                        free(j)
                        dve.wait_ge(act_out, s["act0"] + o + 1)
                        dve.wait_ge(emb_copied, KD * s["i"] + o + 1)
                        mul(ut[:], hf[:], sig[:, o, :])
                        own(dve.tensor_tensor(x[:, o, :], x[:, o, :], ut[:], ALU.add).then_inc(x_new, 1), x_new)
                        produce(s["next"], o, s["g"] if s["i"] + 1 < DEPTH else None, later=True)
                    if s["i"] + 1 < DEPTH:
                        for o in range(KD):
                            x_low(s["next"], o, s["g"])
                elif kind == "odd_in":
                    n = s["n0"]
                    hs = hist[:, SEQ + CC:HISTC].rearrange("p (b t) -> p b t", t=DECT + CC)
                    o1(dve.memset(hist[:, 0:CC], 0.0))
                    for b in range(KD):
                        ja, jb = block_job[n + 2 * b], block_job[n + 2 * b + 1]
                        if b == 0:
                            norm_recip(s)
                        done(ja)
                        mul(halves(gt[:]), P2(ja), halves(r[:]))
                        free(ja)
                        done(jb)
                        mul(halves(ut[:]), P2(jb), halves(r[:]))
                        free(jb)
                        mul(hist[:, CC:CC + SEQ], gt[:, 0:SEQ], ut[:, 0:SEQ])
                        mul(hs[:, :, CC:], gt[:, SEQ:T].rearrange("p (b t) -> p b t", t=DECT),
                            ut[:, SEQ:T].rearrange("p (b t) -> p b t", t=DECT))
                        o1(dve.tensor_copy(hs[:, :, 0:CC], ccstate[:, b, :].rearrange("p (b t) -> p b t", t=CC)))
                        o1(dve.tensor_copy(cccoll[:, b, 0:CC], hist[:, SEQ:SEQ + CC]))
                        sm = coll_ready if b == KD - 1 else dve_own
                        own(dve.tensor_copy(cccoll[:, b, CC:].rearrange("p (b t) -> p b t", t=CC), hs[:, :, DECT:]).then_inc(sm, 1), sm)
                        C = HISTC - CC
                        wc = lambda w: vec2[:, KA * NA + w * KD + b:KA * NA + w * KD + b + 1]
                        o1(dve.tensor_scalar(ct[:, 0:C], hist[:, 0:C], wc(0), None, ALU.mult))
                        for w in range(1, KC):
                            o1(dve.scalar_tensor_tensor(ct[:, 0:C], hist[:, w:w + C], wc(w), ct[:, 0:C], ALU.mult, ALU.add))
                        o1(dve.tensor_copy(sig[:, b, 0:SEQ], ct[:, 0:SEQ]))
                        o1(dve.tensor_copy(sig[:, b, SEQ:T].rearrange("p (b t) -> p b t", t=DECT),
                                           ct[:, SEQ + CC:HISTC].rearrange("p (b t) -> p b t", t=DECT + CC)[:, :, 0:DECT]))
                    for b in range(KD):
                        j = block_job[n + 2 * KD + b]
                        done(j)
                        mul(halves(ut[:]), P2(j), halves(r[:]))
                        free(j)
                        if b == 0:
                            NR = CC + DECB * CC
                            j = s["coll"][0]
                            done(j)
                            for c in range(2):
                                sm = coll_out if c else dve_own
                                own(dve.tensor_copy(ccout[0:NR, c * 4 * P:(c + 1) * 4 * P], ps[j % 4][0:NR, c, :]).then_inc(sm, 1), sm)
                            free(j)
                        mul(hf[:], sig[:, b, :], ut[:])
                        o1(dve.tensor_tensor(hh[:, b, :], sig[:, b, :], ut[:], ALU.mult))
                        own(dve.tensor_tensor(hl[:, b, :], hf[:], hh[:, b, :].bitcast(fp32), ALU.subtract).then_inc(h_ready, 1), h_ready)
                elif kind == "final":
                    dve.wait_ge(col_root, 1)
                    o1(dve.reciprocal(gcol[:, 0:NTILE], gcol[:, 0:NTILE]))
                    dve.wait_ge(y_copied, KD)
                    for t in range(0, NTILE, 2):
                        dve.tensor_scalar(ystage[:, t, :], ystage[:, t, :], gcol[:, t:t + 1], None, ALU.mult).then_inc(y_dve, 1)


def kernel(**inputs):
    import numpy as np
    import concourse.bacc as bacc
    from concourse.bass_utils import run_bass_kernel_spmd
    nc = bacc.Bacc("TRN2", target_bir_lowering=False, num_devices=1)
    arrays, ins = {}, {}
    for name, value in inputs.items():
        a = np.ascontiguousarray(value)
        arrays["in_" + name] = a
        ins[name] = nc.dram_tensor("in_" + name, a.shape, mybir.dt.from_np(a.dtype), kind="ExternalInput").ap()
    xp, xs = arrays["in_x_prompt"].shape, arrays["in_x_sample"].shape
    conv, S, C = (arrays["in_state_" + k].shape for k in ("gdn_conv", "gdn_S", "mlstm_C"))
    n, m, cc = (arrays["in_state_" + k].shape for k in ("mlstm_n", "mlstm_m", "conv"))
    one = lambda s: (s[0], xp[0]) + tuple(s[2:])
    shapes = dict(y_p=xp, y_s=xs, gdn_conv_p=one(conv), gdn_S_p=one(S), mlstm_C_p=one(C), mlstm_n_p=one(n),
                  mlstm_m_p=one(m), conv_p=one(cc), gdn_conv_s=conv, gdn_S_s=S, mlstm_C_s=C, mlstm_n_s=n,
                  mlstm_m_s=m, conv_s=cc)
    outs = {k: nc.dram_tensor("out_" + k, tuple(v), mybir.dt.float32, kind="ExternalOutput").ap() for k, v in shapes.items()}
    stream_step(nc, ins, outs)
    res = run_bass_kernel_spmd(nc, [arrays], core_ids=[0]).results[0]
    return tuple(res["out_" + k] for k in shapes)
```
